# Optimizing a Trainium2 kernel written in Bass

```python
import jax, jax.numpy as jnp
from jax import lax
import numpy as np
import jax
import jax.numpy as jnp

D_MODEL = 1024
BATCH = 1
SEQ = 256
DEPTH = 2

GRID_W = 64
NA_HEADS = 8
NA_HEAD_DIM = 64
NA_WIDTH = NA_HEADS * NA_HEAD_DIM
NA_ROWS = 8
NA_COLS = 16
Q_BLOCK_COLS = 16
KEY_BAND_COLS = Q_BLOCK_COLS + NA_COLS
N_COL_BLOCKS = GRID_W // Q_BLOCK_COLS
F_GROUPS = 4
F_GROUP_DIM = 128
F_WIDTH = F_GROUPS * F_GROUP_DIM
IN_COLS = 3 * NA_WIDTH + F_WIDTH + 2 * D_MODEL
D_FF = 2816
RMS_EPS = 1e-6


def rms_norm(x, g):
    xf = x.astype(jnp.float32)
    y = xf * lax.rsqrt(jnp.mean(xf * xf, axis=-1, keepdims=True) + RMS_EPS)
    return (y * g.astype(jnp.float32)).astype(x.dtype)

def swiglu(x, w_in, w_out):
    gu = x @ w_in
    g, u = jnp.split(gu, 2, axis=-1)
    return (jax.nn.silu(g) * u) @ w_out

def neighbourhood_attention(q, k, v, rpb):
    B, T, H, Dh = q.shape
    rows = T // GRID_W
    kh = min(NA_ROWS, rows)
    r = jnp.arange(rows)
    row_start = jnp.clip(r - kh // 2, 0, rows - kh)
    row_idx = row_start[:, None] + jnp.arange(kh)
    j = jnp.arange(N_COL_BLOCKS)
    band_start = jnp.clip(j * Q_BLOCK_COLS - NA_COLS // 2, 0, GRID_W - KEY_BAND_COLS)
    key_col = band_start[:, None] + jnp.arange(KEY_BAND_COLS)
    q_col = j[:, None] * Q_BLOCK_COLS + jnp.arange(Q_BLOCK_COLS)
    win_start = jnp.clip(q_col - NA_COLS // 2, 0, GRID_W - NA_COLS)
    col_ok = (key_col[:, None, :] >= win_start[..., None]) & (
        key_col[:, None, :] < win_start[..., None] + NA_COLS)

    qg = q.reshape(B, rows, N_COL_BLOCKS, Q_BLOCK_COLS, H, Dh)
    kg = k.reshape(B, rows, GRID_W, H, Dh)
    vg = v.reshape(B, rows, GRID_W, H, Dh)
    gi_r = row_idx[:, None, :, None]
    gi_c = key_col[None, :, None, :]
    k_win = kg[:, gi_r, gi_c]
    v_win = vg[:, gi_r, gi_c]

    dr = row_idx - r[:, None] + (NA_ROWS - 1)
    dc = jnp.clip(key_col[:, None, :] - q_col[..., None], -(NA_COLS - 1), NA_COLS - 1) + (NA_COLS - 1)
    bias = rpb[:, dr[:, None, None, :, None], dc[None, :, :, None, :]]
    bias = jnp.transpose(bias, (1, 2, 0, 3, 4, 5)).astype(jnp.float32)

    scale = Dh ** -0.5
    s = jnp.einsum('brjqhd,brjuvhd->brjhquv', qg, k_win).astype(jnp.float32) * scale + bias[None]
    s = jnp.where(col_ok[None, None, :, None, :, None, :], s, -jnp.inf)
    sh = s.shape
    p = jax.nn.softmax(s.reshape(sh[:-2] + (kh * KEY_BAND_COLS,)), axis=-1).reshape(sh)
    o = jnp.einsum('brjhquv,brjuvhd->brjqhd', p.astype(v.dtype), v_win)
    return o.reshape(B, T, H * Dh)

def fourier_mix(u):
    B, T, _ = u.shape
    ug = u.astype(jnp.float32).reshape(B, T, F_GROUPS, F_GROUP_DIM)
    f = jnp.fft.fft2(ug, axes=(1, 3), norm="ortho").real
    return f.reshape(B, T, F_WIDTH).astype(u.dtype)

def mixer(h, w_in, gate_bias, rpb, w_na_out, w_f_out, w_o):
    B, T, _ = h.shape
    z = h @ w_in
    s1 = NA_WIDTH
    q = z[..., :s1]
    k = z[..., s1:2 * s1]
    v = z[..., 2 * s1:3 * s1]
    uf = z[..., 3 * s1:3 * s1 + F_WIDTH]
    ga = z[..., 3 * s1 + F_WIDTH:3 * s1 + F_WIDTH + D_MODEL]
    gf = z[..., 3 * s1 + F_WIDTH + D_MODEL:]
    shp = (B, T, NA_HEADS, NA_HEAD_DIM)
    y_na = neighbourhood_attention(q.reshape(shp), k.reshape(shp), v.reshape(shp), rpb) @ w_na_out
    y_f = fourier_mix(uf) @ w_f_out
    g_na = jax.nn.sigmoid(ga + gate_bias[0])
    g_f = jax.nn.sigmoid(gf + gate_bias[1])
    return (g_na * y_na + g_f * y_f) @ w_o

def first_inputs(seed: int = 0) -> dict:
    key = jax.random.key(seed)
    ks = jax.random.split(key, 20)
    L, D, F = DEPTH, D_MODEL, D_FF

    def w(k, shape, fan_in, mult=1.0):
        return jax.random.normal(k, shape, jnp.float32) * (mult * fan_in ** -0.5)

    def gain(k, shape):
        return 1.0 + 0.05 * jax.random.normal(k, shape, jnp.float32)

    return {
        "x": jax.random.normal(ks[0], (BATCH, SEQ, D), jnp.float32),
        "ffn1_norm": gain(ks[1], (L, D)),
        "ffn1_w_in": w(ks[2], (L, D, 2 * F), D),
        "ffn1_w_out": w(ks[3], (L, F, D), F),
        "mix_norm": gain(ks[4], (L, D)),
        "mix_w_in": w(ks[5], (L, D, IN_COLS), D),
        "mix_gate_bias": 0.1 * jax.random.normal(ks[6], (L, 2, D), jnp.float32),
        "na_rpb": 0.5 * jax.random.normal(ks[7], (L, NA_HEADS, 2 * NA_ROWS - 1, 2 * NA_COLS - 1), jnp.float32),
        "na_w_out": w(ks[8], (L, NA_WIDTH, D), NA_WIDTH),
        "f_w_out": w(ks[9], (L, F_WIDTH, D), F_WIDTH),
        "mix_w_o": w(ks[10], (L, D, D), D),
        "ffn2_norm": gain(ks[11], (L, D)),
        "ffn2_w_in": w(ks[12], (L, D, 2 * F), D),
        "ffn2_w_out": w(ks[13], (L, F, D), F),
        "final_norm": gain(ks[14], (D,)),
    }

def first_block(x, ffn1_norm, ffn1_w_in, ffn1_w_out, mix_norm, mix_w_in, mix_gate_bias,
              na_rpb, na_w_out, f_w_out, mix_w_o, ffn2_norm, ffn2_w_in, ffn2_w_out,
              final_norm):
    for l in range(DEPTH):
        x = x + 0.5 * swiglu(rms_norm(x, ffn1_norm[l]), ffn1_w_in[l], ffn1_w_out[l])
        x = x + mixer(rms_norm(x, mix_norm[l]), mix_w_in[l], mix_gate_bias[l], na_rpb[l],
                      na_w_out[l], f_w_out[l], mix_w_o[l])
        x = x + 0.5 * swiglu(rms_norm(x, ffn2_norm[l]), ffn2_w_in[l], ffn2_w_out[l])
    return rms_norm(x, final_norm)


HEAD_DIM = 64
ROT_DIM = HEAD_DIM // 4
ROPE_THETA = 500000.0
NORM_EPS = 1e-6
Q_BLOCK = 128

SB_HEADS = 4
NSA_HEADS = 8
NSA_GROUPS = 2
NSA_HPG = NSA_HEADS // NSA_GROUPS
NSA_CMP_LEN = 32
NSA_CMP_STRIDE = 16
NSA_CMP_HIDDEN = 2 * HEAD_DIM
NSA_SEL_LEN = 64
NSA_SEL_N = 16
NSA_WINDOW = 512
NSA_FORCED_SCORE = 1.0e4
DSA_HEADS = 4
DSA_IDX_HEADS = 8
DSA_IDX_DIM = 32
DSA_IDX_ROT = DSA_IDX_DIM // 4
DSA_TOPK = 256

SB_W = SB_HEADS * HEAD_DIM
NSA_QW = NSA_HEADS * HEAD_DIM
NSA_KVW = NSA_GROUPS * HEAD_DIM
DSA_QW = DSA_HEADS * HEAD_DIM
IN_WIDTHS = (SB_W, SB_W, SB_W,
             NSA_QW, NSA_KVW, NSA_KVW, NSA_KVW, NSA_KVW, NSA_KVW, NSA_KVW, 3 * NSA_HEADS,
             DSA_QW, HEAD_DIM, HEAD_DIM, DSA_IDX_HEADS * DSA_IDX_DIM, DSA_IDX_DIM, DSA_IDX_HEADS)
D_IN = sum(IN_WIDTHS)


def rms_norm_2(x, g):
    xf = x.astype(jnp.float32)
    y = xf * lax.rsqrt(jnp.mean(xf * xf, axis=-1, keepdims=True) + NORM_EPS)
    return (y * g.astype(jnp.float32)).astype(x.dtype)

def rope_tables(pos, rot_dim):
    inv = ROPE_THETA ** (-jnp.arange(0, rot_dim, 2, dtype=jnp.float32) / rot_dim)
    ang = pos.astype(jnp.float32)[:, None] * inv[None, :]
    return jnp.cos(ang), jnp.sin(ang)

def apply_rope(x, cos, sin):
    half = cos.shape[-1]
    xf = x[..., :2 * half].astype(jnp.float32)
    x1, x2 = xf[..., :half], xf[..., half:]
    c, s = cos[:, None, :], sin[:, None, :]
    rot = jnp.concatenate([x1 * c - x2 * s, x2 * c + x1 * s], axis=-1).astype(x.dtype)
    return jnp.concatenate([rot, x[..., 2 * half:]], axis=-1)

def masked_softmax(s, mask):
    s = jnp.where(mask, s.astype(jnp.float32), -jnp.inf)
    m = jnp.max(s, axis=-1, keepdims=True)
    m = jnp.where(jnp.isfinite(m), m, 0.0)
    p = jnp.exp(s - m)
    den = jnp.sum(p, axis=-1, keepdims=True)
    return p / jnp.where(den > 0, den, 1.0)

def unblock(y):
    n, b, t = y.shape[:3]
    return jnp.moveaxis(y, 0, 1).reshape((b, n * t) + y.shape[3:])

def swiglu_ffn(x, g, w_gu, w_down):
    h = rms_norm_2(x, g)
    gate, up = jnp.split(h @ w_gu, 2, axis=-1)
    return (jax.nn.silu(gate) * up) @ w_down

def stick_breaking_attention(q, k, v):
    B, S, H, d = q.shape
    scale = d ** -0.5
    kh = k.transpose(0, 2, 1, 3)
    vh = v.transpose(0, 2, 1, 3)
    s_pos = jnp.arange(S)

    def block(i):
        q0 = i * Q_BLOCK
        qb = lax.dynamic_slice_in_dim(q, q0, Q_BLOCK, axis=1)
        z = jnp.einsum('bthd,bhsd->bhts', qb, kh).astype(jnp.float32) * scale
        t_pos = q0 + jnp.arange(Q_BLOCK)
        past = s_pos[None, :] < t_pos[:, None]
        log_1m = jnp.where(past, jax.nn.log_sigmoid(-z), 0.0)
        tail = lax.cumsum(log_1m, axis=3, reverse=True) - log_1m
        w = jnp.where(past, jnp.exp(jax.nn.log_sigmoid(z) + tail), 0.0)
        return jnp.einsum('bhts,bhsd->bthd', w.astype(v.dtype), vh)

    return unblock(lax.map(block, jnp.arange(S // Q_BLOCK)))

def nsa_compress(x, pe, w1, w2):
    B, S, G, d = x.shape
    nchunk = S // NSA_CMP_STRIDE
    r = NSA_CMP_LEN // NSA_CMP_STRIDE
    nc = nchunk - r + 1
    chunks = x.reshape(B, nchunk, NSA_CMP_STRIDE, G, d)
    blocks = jnp.concatenate([chunks[:, m:m + nc] for m in range(r)], axis=2)
    blocks = blocks + pe[None, None, :, None, :]
    flat = blocks.transpose(0, 1, 3, 2, 4).reshape(B, nc, G, NSA_CMP_LEN * d)
    return jax.nn.silu(flat @ w1) @ w2

def nsa_attention(q, k_cmp, v_cmp, k_sel, v_sel, k_win, v_win, gate_logits,
                  q_norm, k_norm, pe, w1, w2, cos, sin):
    B, S, _, d = q.shape
    G, hpg, T = NSA_GROUPS, NSA_HPG, Q_BLOCK
    scale = d ** -0.5
    dt = v_sel.dtype
    qg = apply_rope(rms_norm_2(q, q_norm), cos, sin).reshape(B, S, G, hpg, d)
    k_sel = apply_rope(rms_norm_2(k_sel, k_norm[1]), cos, sin)
    k_win = apply_rope(rms_norm_2(k_win, k_norm[2]), cos, sin)
    gates = jax.nn.sigmoid(gate_logits).reshape(B, S, G, hpg, 3)

    kc = rms_norm_2(nsa_compress(k_cmp, pe[0], w1[0], w2[0]), k_norm[0])
    nc = kc.shape[1]
    cmp_start = jnp.arange(nc) * NSA_CMP_STRIDE
    cmp_end = cmp_start + NSA_CMP_LEN - 1
    cos_c, sin_c = rope_tables(cmp_end, ROT_DIM)
    kc = apply_rope(kc, cos_c, sin_c).transpose(0, 2, 1, 3)
    vc = nsa_compress(v_cmp, pe[1], w1[1], w2[1]).transpose(0, 2, 1, 3)

    ns = S // NSA_SEL_LEN
    n_sel = min(NSA_SEL_N, ns)
    ks_blocks = k_sel.reshape(B, ns, NSA_SEL_LEN, G, d).transpose(0, 3, 1, 2, 4)
    vs_blocks = v_sel.reshape(B, ns, NSA_SEL_LEN, G, d).transpose(0, 3, 1, 2, 4)
    sel_start = jnp.arange(ns) * NSA_SEL_LEN
    overlap = ((cmp_start[:, None] < sel_start[None, :] + NSA_SEL_LEN)
               & (cmp_end[:, None] >= sel_start[None, :])).astype(jnp.float32)
    gather_blocks = jax.vmap(jax.vmap(lambda src, ix: src[ix]))

    pad = ((0, 0), (NSA_WINDOW, 0), (0, 0), (0, 0))
    kw_pad = jnp.pad(k_win, pad)
    vw_pad = jnp.pad(v_win, pad)

    def block(i):
        q0 = i * T
        t_pos = q0 + jnp.arange(T)
        qb = lax.dynamic_slice_in_dim(qg, q0, T, axis=1)

        sc = jnp.einsum('btghd,bgcd->bghtc', qb, kc) * scale
        pc = masked_softmax(sc, cmp_end[None, :] <= t_pos[:, None])
        o_cmp = jnp.einsum('bghtc,bgcd->btghd', pc.astype(dt), vc)

        imp = jnp.einsum('bghtc,cn->bgtn', pc, overlap)
        j = jnp.arange(ns)[None, :]
        cur = (t_pos // NSA_SEL_LEN)[:, None]
        visible = j * NSA_SEL_LEN <= t_pos[:, None]
        forced = (j == 0) | (j == cur) | (j == cur - 1)
        score = jnp.where(visible, jnp.where(forced, NSA_FORCED_SCORE, imp), -jnp.inf)
        _, sel = lax.top_k(score, n_sel)
        k_g = gather_blocks(ks_blocks, sel)
        v_g = gather_blocks(vs_blocks, sel).reshape(B, G, T, n_sel * NSA_SEL_LEN, d)
        tok = sel[..., None] * NSA_SEL_LEN + jnp.arange(NSA_SEL_LEN)
        smask = (tok <= t_pos[:, None, None]).reshape(B, G, 1, T, n_sel * NSA_SEL_LEN)
        ss = jnp.einsum('btghd,bgtnld->bghtnl', qb, k_g) * scale
        ps = masked_softmax(ss.reshape(B, G, hpg, T, n_sel * NSA_SEL_LEN), smask)
        o_sel = jnp.einsum('bghtm,bgtmd->btghd', ps.astype(dt), v_g)

        kwb = lax.dynamic_slice_in_dim(kw_pad, q0, T + NSA_WINDOW, axis=1)
        vwb = lax.dynamic_slice_in_dim(vw_pad, q0, T + NSA_WINDOW, axis=1)
        s_abs = q0 - NSA_WINDOW + jnp.arange(T + NSA_WINDOW)
        wmask = ((s_abs[None, :] <= t_pos[:, None]) & (s_abs[None, :] > t_pos[:, None] - NSA_WINDOW)
                 & (s_abs[None, :] >= 0))
        sw = jnp.einsum('btghd,bsgd->bghts', qb, kwb) * scale
        pw = masked_softmax(sw, wmask)
        o_win = jnp.einsum('bghts,bsgd->btghd', pw.astype(dt), vwb)

        g = lax.dynamic_slice_in_dim(gates, q0, T, axis=1)
        return g[..., 0:1] * o_cmp + g[..., 1:2] * o_sel + g[..., 2:3] * o_win

    out = unblock(lax.map(block, jnp.arange(S // T)))
    return out.reshape(B, S, NSA_HEADS * d)

def dsa_attention(q, k, v, iq, ik, iw, q_norm, k_norm, cos, sin, cos_i, sin_i):
    B, S, _, d = q.shape
    T = Q_BLOCK
    scale = d ** -0.5
    dt = v.dtype
    top_k = min(DSA_TOPK, S // 4)
    q = apply_rope(rms_norm_2(q, q_norm), cos, sin)
    k = apply_rope(rms_norm_2(k[:, :, None, :], k_norm), cos, sin)[:, :, 0, :]
    iq = apply_rope(iq, cos_i, sin_i)
    ik = apply_rope(ik[:, :, None, :], cos_i, sin_i)[:, :, 0, :]
    iw = iw.astype(jnp.float32) * (DSA_IDX_HEADS ** -0.5) * (DSA_IDX_DIM ** -0.5)
    s_pos = jnp.arange(S)
    gather_rows = jax.vmap(lambda src, ix: src[ix])

    def block(i):
        q0 = i * T
        t_pos = q0 + jnp.arange(T)
        qi = lax.dynamic_slice_in_dim(iq, q0, T, axis=1)
        wi = lax.dynamic_slice_in_dim(iw, q0, T, axis=1)
        logits = jax.nn.relu(jnp.einsum('bthd,bsd->bths', qi, ik).astype(jnp.float32))
        score = jnp.einsum('bths,bth->bts', logits, wi)
        score = jnp.where(s_pos[None, None, :] <= t_pos[None, :, None], score, -jnp.inf)
        _, idx = lax.top_k(score, top_k)
        kg = gather_rows(k, idx)
        vg = gather_rows(v, idx)
        qb = lax.dynamic_slice_in_dim(q, q0, T, axis=1)
        sc = jnp.einsum('bthd,btkd->bhtk', qb, kg) * scale
        p = masked_softmax(sc, (idx <= t_pos[None, :, None])[:, None])
        return jnp.einsum('bhtk,btkd->bthd', p.astype(dt), vg)

    out = unblock(lax.map(block, jnp.arange(S // T)))
    return out.reshape(B, S, DSA_HEADS * d)

def hybrid_mixer(h, w_in, w_gate, nsa_q_norm, nsa_k_norm, nsa_cmp_pe, nsa_cmp_w1, nsa_cmp_w2,
                 dsa_q_norm, dsa_k_norm, w_br_a, w_br_b, w_br_c, w_out, cos, sin, cos_i, sin_i):
    B, S, _ = h.shape
    offs = np.cumsum(IN_WIDTHS)[:-1].tolist()
    (sb_q, sb_k, sb_v, nq, nkc, nvc, nks, nvs, nkw, nvw, ngate,
     dq, dk, dv, iq, ik, iw) = jnp.split(h @ w_in, offs, axis=-1)

    def heads(t, n, d):
        return t.reshape(B, S, n, d)

    o_a = stick_breaking_attention(heads(sb_q, SB_HEADS, HEAD_DIM), heads(sb_k, SB_HEADS, HEAD_DIM),
                                   heads(sb_v, SB_HEADS, HEAD_DIM)).reshape(B, S, SB_W)
    kv = lambda t: heads(t, NSA_GROUPS, HEAD_DIM)
    o_b = nsa_attention(heads(nq, NSA_HEADS, HEAD_DIM), kv(nkc), kv(nvc), kv(nks), kv(nvs), kv(nkw), kv(nvw),
                        heads(ngate, NSA_HEADS, 3), nsa_q_norm, nsa_k_norm, nsa_cmp_pe, nsa_cmp_w1, nsa_cmp_w2,
                        cos, sin)
    o_c = dsa_attention(heads(dq, DSA_HEADS, HEAD_DIM), dk, dv, heads(iq, DSA_IDX_HEADS, DSA_IDX_DIM), ik, iw,
                        dsa_q_norm, dsa_k_norm, cos, sin, cos_i, sin_i)

    g_a, g_b, g_c = jnp.split(jax.nn.sigmoid(h @ w_gate), 3, axis=-1)
    merged = g_a * (o_a @ w_br_a) + g_b * (o_b @ w_br_b) + g_c * (o_c @ w_br_c)
    return merged @ w_out

def second_inputs(seed: int = 0) -> dict:
    key = jax.random.key(seed)
    ks = jax.random.split(key, 21)
    f32 = jnp.float32

    def normal(k, shape, scale):
        return jax.random.normal(k, shape, f32) * scale

    def gain(k, shape):
        return 1.0 + 0.02 * jax.random.normal(k, shape, f32)

    D, L = D_MODEL, DEPTH
    cmp_in = NSA_CMP_LEN * HEAD_DIM
    return {
        "x": jax.random.normal(ks[0], (BATCH, SEQ, D), f32),
        "ffn1_norm": gain(ks[1], (L, D)),
        "ffn1_w_gu": normal(ks[2], (L, D, 2 * D_FF), D ** -0.5),
        "ffn1_w_down": normal(ks[3], (L, D_FF, D), D_FF ** -0.5),
        "mix_norm": gain(ks[4], (L, D)),
        "w_in": normal(ks[5], (L, D, D_IN), D ** -0.5),
        "w_gate": normal(ks[6], (L, D, 3 * D), D ** -0.5),
        "nsa_q_norm": gain(ks[7], (L, HEAD_DIM)),
        "nsa_k_norm": gain(ks[8], (L, 3, HEAD_DIM)),
        "nsa_cmp_pe": normal(ks[9], (L, 2, NSA_CMP_LEN, HEAD_DIM), 0.1),
        "nsa_cmp_w1": normal(ks[10], (L, 2, cmp_in, NSA_CMP_HIDDEN), cmp_in ** -0.5),
        "nsa_cmp_w2": normal(ks[11], (L, 2, NSA_CMP_HIDDEN, HEAD_DIM), NSA_CMP_HIDDEN ** -0.5),
        "dsa_q_norm": gain(ks[12], (L, HEAD_DIM)),
        "dsa_k_norm": gain(ks[13], (L, HEAD_DIM)),
        "w_br_a": normal(ks[14], (L, SB_W, D), SB_W ** -0.5),
        "w_br_b": normal(ks[15], (L, NSA_QW, D), NSA_QW ** -0.5),
        "w_br_c": normal(ks[16], (L, DSA_QW, D), DSA_QW ** -0.5),
        "w_out": normal(ks[17], (L, D, D), D ** -0.5),
        "ffn2_norm": gain(ks[18], (L, D)),
        "ffn2_w_gu": normal(ks[19], (L, D, 2 * D_FF), D ** -0.5),
        "ffn2_w_down": normal(ks[20], (L, D_FF, D), D_FF ** -0.5),
    }

def second_block(x, ffn1_norm, ffn1_w_gu, ffn1_w_down, mix_norm, w_in, w_gate, nsa_q_norm, nsa_k_norm,
              nsa_cmp_pe, nsa_cmp_w1, nsa_cmp_w2, dsa_q_norm, dsa_k_norm, w_br_a, w_br_b, w_br_c, w_out,
              ffn2_norm, ffn2_w_gu, ffn2_w_down):
    S = x.shape[1]
    pos = jnp.arange(S)
    cos, sin = rope_tables(pos, ROT_DIM)
    cos_i, sin_i = rope_tables(pos, DSA_IDX_ROT)
    for l in range(DEPTH):
        x = x + 0.5 * swiglu_ffn(x, ffn1_norm[l], ffn1_w_gu[l], ffn1_w_down[l])
        h = rms_norm_2(x, mix_norm[l])
        x = x + hybrid_mixer(h, w_in[l], w_gate[l], nsa_q_norm[l], nsa_k_norm[l], nsa_cmp_pe[l],
                             nsa_cmp_w1[l], nsa_cmp_w2[l], dsa_q_norm[l], dsa_k_norm[l],
                             w_br_a[l], w_br_b[l], w_br_c[l], w_out[l], cos, sin, cos_i, sin_i)
        x = x + 0.5 * swiglu_ffn(x, ffn2_norm[l], ffn2_w_gu[l], ffn2_w_down[l])
    return x


def setup_inputs(seed=0):
    out = dict(first_inputs(seed))
    for name, value in second_inputs(seed + 1).items():
        if name != "x":
            out[name + "_2"] = value
    return out


def reference(
    x, ffn1_norm, ffn1_w_in, ffn1_w_out, mix_norm, mix_w_in, mix_gate_bias, na_rpb, na_w_out,
    f_w_out, mix_w_o, ffn2_norm, ffn2_w_in, ffn2_w_out, final_norm, ffn1_norm_2, ffn1_w_gu_2,
    ffn1_w_down_2, mix_norm_2, w_in_2, w_gate_2, nsa_q_norm_2, nsa_k_norm_2, nsa_cmp_pe_2,
    nsa_cmp_w1_2, nsa_cmp_w2_2, dsa_q_norm_2, dsa_k_norm_2, w_br_a_2, w_br_b_2, w_br_c_2,
    w_out_2, ffn2_norm_2, ffn2_w_gu_2, ffn2_w_down_2,
):
    x = first_block(
        x, ffn1_norm, ffn1_w_in, ffn1_w_out, mix_norm, mix_w_in, mix_gate_bias, na_rpb,
        na_w_out, f_w_out, mix_w_o, ffn2_norm, ffn2_w_in, ffn2_w_out, final_norm,
    )
    return second_block(
        x, ffn1_norm_2, ffn1_w_gu_2, ffn1_w_down_2, mix_norm_2, w_in_2, w_gate_2, nsa_q_norm_2,
        nsa_k_norm_2, nsa_cmp_pe_2, nsa_cmp_w1_2, nsa_cmp_w2_2, dsa_q_norm_2, dsa_k_norm_2,
        w_br_a_2, w_br_b_2, w_br_c_2, w_out_2, ffn2_norm_2, ffn2_w_gu_2, ffn2_w_down_2,
    )


_drawn_inputs = setup_inputs


def setup_inputs(seed=0):
    import zlib

    import numpy as np

    out = dict(_drawn_inputs(seed))
    spreads = {}
    factors = {'ffn1_norm_2': 3.031,
     'nsa_q_norm_2': 8.0,
     'nsa_k_norm_2': 8.0,
     'dsa_q_norm_2': 8.0,
     'dsa_k_norm_2': 8.0,
     'ffn2_norm_2': 4.496}
    for name, (base, spread) in spreads.items():
        noise = np.random.default_rng([zlib.crc32(name.encode()), seed]).standard_normal(out[name].shape)
        drawn = base * np.exp(spread * noise) if base else spread * noise
        out[name] = jnp.asarray(drawn.astype(out[name].dtype))
    for name, factor in factors.items():
        out[name] = (out[name] * factor).astype(out[name].dtype)
    return out
```

```python
from contextlib import ExitStack

import numpy as np
from concourse import mybir

F32 = mybir.dt.float32
F32R = mybir.dt.float32r
ACT = mybir.ActivationFunctionType
ALU = mybir.AluOpType
AX = mybir.AxisListType

P = 128
D = 1024
KD = D // P
T = 256
TT = T // P
DFF = 2816
FC = DFF // P
LAYERS = 2
HALF = 512
CH = 1024
SLOT = 3 * CH
EPS = 1e-6
MASKED = -1.0e30

NA_HEADS, DH = 8, 64
NA_W = NA_HEADS * DH
F_GROUPS, F_DIM = 4, 128
GRID_W, NA_ROWS, NA_COLS = 64, 8, 16
SCALE = DH ** -0.5
PAIRS = NA_HEADS // 2
MIX1_SLOTS = 16
SB_HEADS, NSA_HEADS, NSA_GROUPS, DSA_HEADS = 4, 8, 2, 4
IDX_HEADS, IDX_DIM, TOPK = 8, 32, 64
CMP_LEN, CMP_STRIDE = 32, 16
NCMP = T // CMP_STRIDE - CMP_LEN // CMP_STRIDE + 1
CB = 16
MIX2_SLOTS = 22


class Stream:

    def __init__(self, nc, sb, sem, dram):
        self.nc, self.dram = nc, dram
        self.raw = [sb("w_raw_front", [P, 2, 2 * CH], F32), sb("w_raw_back", [P, 2, CH], F32)]
        self.hi = [sb("w_hi_front", [P, 2, 2 * CH], F32R), sb("w_hi_back", [P, 2, CH], F32R)]
        self.lo = [sb("w_lo_front", [P, 2, 2 * CH], F32R), sb("w_lo_back", [P, 2, CH], F32R)]
        self.loaded = [[sem(f"w_{part}_loaded{i}") for i in range(2)] for part in ("front", "back")]
        self.hi_done = [sem("w_front_hi"), sem("w_back_hi")]
        self.split = [sem("w_front_split"), sem("w_back_split")]
        self.used = [sem("w_front_used"), sem("w_back_used")]

    def load(self, sp, part, slot, parity):
        sp.wait_ge(self.split[part], slot + 1)
        at = slice(0, 2 * CH) if part == 0 else slice(2 * CH, SLOT)
        sp.dma_start(self.raw[part][:, parity], self.dram[slot][:, at]).then_inc(
            self.loaded[part][parity], 16)

    def load_slots(self, sp, first, count):
        with sp.Fori(0, count // 2) as i:
            for k in range(2):
                self.load(sp, 0, first + 2 * i + k + 1, 1 - k)
                self.load(sp, 1, first + 2 * i + k, k)

    def round_hi(self, act, part, base, slot):
        parity = slot % 2
        act.wait_ge(self.loaded[part][parity], 8 * (base + slot - parity) + 16)
        act.wait_ge(self.used[part], (base + slot) * (2 - part) + 2 - part)
        self.nc.scalar.copy(self.hi[part][:, parity], self.raw[part][:, parity]).then_inc(
            self.hi_done[part], 1)

    def feed(self, act, base, slot):
        self.round_hi(act, 0, base, slot + 1)
        self.round_hi(act, 1, base, slot)

    def rest(self, pool, part, slot, parity):
        pool.wait_ge(self.hi_done[part], slot + 1)
        self.nc.gpsimd.tensor_tensor(
            self.lo[part][:, parity], self.raw[part][:, parity],
            self.hi[part][:, parity].bitcast(F32), ALU.subtract).then_inc(self.split[part], 1)

    def chunk(self, pe, base, slot, c):
        part = c // 2
        if c != 1:
            pe.wait_ge(self.split[part], base + slot + 3)
        at = slice((c % 2) * CH, (c % 2) * CH + CH)
        return self.hi[part][:, slot % 2, at], self.lo[part][:, slot % 2, at]

    def taken(self, last, c):
        last.then_inc(self.used[c // 2], 1)

    def wait_taken(self, eng, base, slot, c):
        if c == 2:
            eng.wait_ge(self.used[1], base + slot + 3)
        else:
            eng.wait_ge(self.used[0], (base + slot) * 2 + 4 + c + 1)


class State:
    pass


class Marks:

    def __init__(self, sem, prefix, totals):
        self.sem = {name: sem(prefix + name) for name in totals}
        self.totals = totals
        self.made = {name: 0 for name in totals}

    def inc(self, instruction, name):
        self.made[name] += 1
        instruction.then_inc(self.sem[name], 1)

    def need(self, eng, layer, name, k):
        eng.wait_ge(self.sem[name], layer * self.totals[name] + k)

    def check(self):
        assert self.made == self.totals, {
            n: (self.made[n], self.totals[n]) for n in self.totals if self.made[n] != self.totals[n]}


def product(nc, out, a, b, start, stop):
    (ah, al), (bh, bl) = a, b
    nc.tensor.matmul(out, ah, bl, start=start, stop=False)
    nc.tensor.matmul(out, al, bh, start=False, stop=False)
    return nc.tensor.matmul(out, ah, bh, start=False, stop=stop)


def shared_state(nc, sb, ps, sem):
    s = State()
    s.nc = nc
    s.x = sb("x", [P, TT, D], F32)
    s.xn = sb("squares", [P, TT, D], F32)
    s.ss = sb("sum_sq", [P, TT, 2], F32)
    s.ms = sb("mean_sq", [P, TT], F32)
    s.rms = sb("rms", [P, TT], F32)
    s.inv = sb("inv_rms", [P, TT], F32)
    s.scrap = sb("scrap", [P, 1], F32)
    s.xh = sb("xt_hi", [P, KD, T], F32R)
    s.xl = sb("xt_lo", [P, KD, T], F32R)
    s.act = sb("silu_gate", [P, 2, T], F32)
    s.hid = sb("hidden", [P, 2, T], F32)
    s.diag = s.hid[:, :, 0:P]
    s.hh = sb("hidden_hi", [P, 2, T], F32R)
    s.hl = sb("hidden_lo", [P, 2, T], F32R)
    s.ident = sb("identity", [P, P], F32)
    s.pj = [ps(f"ps_proj{i}", [P, HALF], F32) for i in range(2)]
    s.py = [ps(f"ps_y{i}", [P, HALF], F32) for i in range(4)]
    s.pa = [ps(f"ps_aux{i}", [P, HALF], F32) for i in range(2)]
    s.x_ready = sem("x_ready")
    s.sum_sq_ready = sem("sum_sq_ready")
    s.mean_sq_ready = sem("mean_sq_ready")
    s.rms_ready = sem("rms_ready")
    s.inv_ready = sem("inv_ready")
    s.diag_ready = sem("diag_ready")
    s.table_in = sem("table_in")
    s.y_tile = sem("y_tile")
    s.xt_banks = sem("xt_banks")
    s.xh_ready = sem("xh_ready")
    s.xl_ready = sem("xl_ready")
    s.silu_done = sem("silu_done")
    s.hid_done = sem("hid_done")
    s.hh_done = sem("hh_done")
    s.h_ready = sem("h_ready")
    return s



def norm_banks(s):
    return s.pj[0], s.pa[0], s.pa[1], s.pj[1]


def norm_scalar(s, n, g, nx, then):
    nc, act = s.nc, s.nc.scalar

    def fetch_table(func, k):
        act.wait_ge(s.table_in, 2 * n + k)
        nc.scalar.activation(s.scrap[:], s.ident[:, 0:1], func).then_inc(s.table_in, 1)

    fetch_table(ACT.Sqrt, 1)
    for i in range(TT):
        for half in range(2):
            act.wait_ge(s.x_ready, 4 * nx + 2 * i + half + 1)
            cols = slice(half * HALF, (half + 1) * HALF)
            nc.scalar.activation(s.xn[:, i, cols], s.x[:, i, cols], ACT.Square,
                                 accum_out=s.ss[:, i, half:half + 1]).then_inc(s.sum_sq_ready, 1)
        act.wait_ge(s.mean_sq_ready, 2 * n + i + 1)
        act.wait_ge(s.sum_sq_ready, 4 * n + 2 * i + 2)
        nc.scalar.activation(s.rms[:, i:i + 1], s.ss[:, i, 1:2], ACT.Sqrt, bias=s.ms[:, i:i + 1],
                             scale=1.0 / D).then_inc(s.rms_ready, 1)
    fetch_table(then, 2)
    for k in range(KD):
        if k % 2 == 0:
            act.wait_ge(s.xt_banks, 4 * n + k // 2 + 1)
        bank = norm_banks(s)[k // 2][:, (k % 2) * T:(k % 2 + 1) * T]
        nc.scalar.activation(s.xh[:, k], bank, ACT.Copy,
                             scale=s.par[:, g * KD + k:g * KD + k + 1]).then_inc(s.xh_ready, 1)


def first_mean(s, n, i):
    s.nc.vector.wait_ge(s.sum_sq_ready, 4 * n + 2 * i + 1)
    s.nc.vector.tensor_scalar(s.ms[:, i:i + 1], s.ss[:, i, 0:1], 1.0 / D, EPS, ALU.mult,
                              ALU.add).then_inc(s.mean_sq_ready, 1)


def diagonal(s, n, i):
    nc, dve = s.nc, s.nc.vector
    dve.wait_ge(s.rms_ready, 2 * n + i + 1)
    nc.vector.reciprocal(s.inv[:, i:i + 1], s.rms[:, i:i + 1]).then_inc(s.inv_ready, 1)
    dve.wait_ge(s.inv_ready, 2 * n + i + 1)
    nc.vector.tensor_scalar(s.diag[:, i], s.ident[:], s.inv[:, i:i + 1], None,
                            ALU.mult).then_inc(s.diag_ready, 1)


def norm_rest(s, n, g):
    nc, dve = s.nc, s.nc.vector
    for k in range(KD):
        if k % 2 == 0:
            dve.wait_ge(s.xh_ready, 8 * n + k + 2)
        bank = norm_banks(s)[k // 2][:, (k % 2) * T:(k % 2 + 1) * T]
        nc.vector.scalar_tensor_tensor(s.xl[:, k], bank, s.par[:, g * KD + k:g * KD + k + 1],
                                       s.xh[:, k].bitcast(F32), ALU.mult, ALU.subtract).then_inc(
            s.xl_ready, 1)


def norm_start(s, n):
    for i in range(TT):
        first_mean(s, n, i)
        diagonal(s, n, i)


def norm_tensor(s, n):
    nc, pe = s.nc, s.nc.tensor
    for i in range(TT):
        pe.wait_ge(s.diag_ready, 2 * n + i + 1)
        for k in range(KD):
            at = (k % 2) * T + i * P
            last = nc.tensor.matmul(norm_banks(s)[k // 2][:, at:at + P],
                                    s.x[:, i, k * P:(k + 1) * P], s.diag[:, i])
            if i == TT - 1 and k % 2 == 1:
                last.then_inc(s.xt_banks, 1)


def wait_normed(s, n, k):
    s.nc.tensor.wait_ge(s.xl_ready, 8 * n + max(k + 1, 2))



def ffn_up(s, w, base, slot, n, first=False):
    nc, pe = s.nc, s.nc.tensor
    for c in range(2):
        hi, lo = w.chunk(pe, base, slot, c)
        for k in range(KD):
            if first and c == 0:
                wait_normed(s, n, k)
            cols = slice(k * P, (k + 1) * P)
            last = product(nc, s.pj[slot % 2][:, c * T:(c + 1) * T],
                           (hi[:, cols], lo[:, cols]), (s.xh[:, k], s.xl[:, k]), k == 0, k == KD - 1)
        w.taken(last, c)


def ffn_down(s, w, base, slot, h_count, start=False, stop=False):
    nc, pe = s.nc, s.nc.tensor
    hi, lo = w.chunk(pe, base, slot, 2)
    pe.wait_ge(s.h_ready, h_count)
    par = slot % 2
    for i in range(TT):
        toks = slice(i * P, (i + 1) * P)
        for half in range(2):
            cols = slice(half * HALF, (half + 1) * HALF)
            last = product(nc, s.py[2 * i + half][:], (s.hh[:, par, toks], s.hl[:, par, toks]),
                           (hi[:, cols], lo[:, cols]), start, stop)
        if stop and i == 0:
            last.then_inc(s.y_tile, 1)
    w.taken(last, 2)


def ffn_tensor(s, w, base, slot0, n, c0):
    norm_tensor(s, n)
    ffn_up(s, w, base, slot0, n, first=True)
    ffn_up(s, w, base, slot0 + 1, n)
    ffn_down(s, w, base, slot0, c0 + 1, start=True)
    with s.nc.tensor.Fori(1, FC // 2) as g:
        for k in range(2):
            ffn_up(s, w, base + 2 * g, slot0 + k, n)
            ffn_down(s, w, base + 2 * g, slot0 + k - 1, c0 + 2 * g + k)
    ffn_down(s, w, base, slot0 + FC - 1, c0 + FC, stop=True)


def ffn_scalar(s, w, base, slot0, n, g, nx):
    nc, act = s.nc, s.nc.scalar

    def silu(before, slot):
        w.wait_taken(act, base + before, slot, 1)
        nc.scalar.activation(s.act[:, slot % 2], s.pj[slot % 2][:, 0:T], ACT.Silu).then_inc(
            s.silu_done, 1)

    w.feed(act, base, slot0)
    norm_scalar(s, n, g, nx, ACT.Silu)
    silu(0, slot0)
    w.feed(act, base, slot0 + 1)
    with act.Fori(0, FC // 2 - 1) as i:
        for k in (1, 2):
            silu(2 * i, slot0 + k)
            w.feed(act, base + 2 * i, slot0 + k + 1)
    silu(0, slot0 + FC - 1)


def ffn_vector(s, w, base, slot0, n, c0, g, last):
    nc, dve = s.nc, s.nc.vector
    norm_rest(s, n, g)
    with dve.Fori(0, FC // 2) as i:
        for k in range(2):
            done = c0 + 2 * i + k + 1
            dve.wait_ge(s.silu_done, done)
            nc.vector.tensor_tensor(s.hid[:, k], s.act[:, k], s.pj[k][:, T:2 * T],
                                    ALU.mult).then_inc(s.hid_done, 1)
            dve.wait_ge(s.hid_done, done)
            nc.vector.tensor_copy(s.hh[:, k], s.hid[:, k]).then_inc(s.hh_done, 1)
            dve.wait_ge(s.hh_done, done)
            nc.vector.tensor_tensor(s.hl[:, k], s.hid[:, k], s.hh[:, k].bitcast(F32),
                                    ALU.subtract).then_inc(s.h_ready, 1)
    finish(s, w, base, slot0 + FC - 1, 2, n, 0.5, None if last else n + 1)


def finish(s, w, base, slot, c, n, factor, n_next):
    nc, dve = s.nc, s.nc.vector

    def add(i, half):
        xs = s.x[:, i, half * HALF:(half + 1) * HALF]
        nc.vector.scalar_tensor_tensor(xs, s.py[2 * i + half][:], factor, xs, ALU.mult,
                                       ALU.add).then_inc(s.x_ready, 1)

    dve.wait_ge(s.y_tile, n + 1)
    add(0, 0)
    add(0, 1)
    w.wait_taken(dve, base, slot, c)
    add(1, 0)
    if n_next is not None:
        first_mean(s, n_next, 0)
        diagonal(s, n_next, 0)
    add(1, 1)
    if n_next is not None:
        first_mean(s, n_next, 1)
        diagonal(s, n_next, 1)


Q_V, Q_U, Q_Q, Q_K, Q_GATE, Q_Y, Q_O = 0, 4, 8, 12, 16, 32, 40
JOBS1 = PAIRS * TT

MIX1_TOTALS = dict(
    v_ready=2, u_ready=2, q_ready=4, k_ready=4, dft1_done=4, dft1_ready=4, dft2_done=4,
    dft_hi=4, dft_ready=4, gate_ready=16, scores_done=JOBS1, biased=JOBS1, max_ready=JOBS1,
    exp_ready=2 * JOBS1, inv_sum=JOBS1, probs_ready=JOBS1, probsT_done=JOBS1,
    probsT_ready=JOBS1, pv_done=JOBS1, o_hi=JOBS1, o_ready=JOBS1, sigmoid_ready=16, gated=8,
    summed=8, m_hi=8, m_ready=8)


def mix1_state(sb):
    u = sb("m1_u", [P, TT, NA_W], F32)
    v = sb("m1_v", [P, TT, NA_W], F32)
    m = State()
    m.qT = sb("m1_qT", [P, PAIRS, T], F32)
    m.kbd = sb("m1_k_block", [P, PAIRS, 2, T], F32)
    m.v = v
    m.u = u
    m.dft_t = sb("m1_dft_time", [P, TT, 2 * T], F32)
    m.dft_c = sb("m1_dft_chan", [P, 2, P], F32)
    m.a = sb("m1_dft_a", [P, F_GROUPS, 2 * T], F32)
    m.fh = sb("m1_fourier_hi", [P, F_GROUPS, T], F32R)
    m.fl = sb("m1_fourier_lo", [P, F_GROUPS, T], F32R)
    m.oh = sb("m1_attn_hi", [P, PAIRS, T], F32R)
    m.ol = sb("m1_attn_lo", [P, PAIRS, T], F32R)
    m.gate = sb("m1_gates", [P, KD, 2, T], F32)
    m.bias = sb("m1_rel_bias", [P, TT, NA_HEADS, T], F32)
    m.sc = sb("m1_scores", [P, 2, 2, T], F32)
    m.pT = sb("m1_probsT", [P, 2, 4, P], F32)
    m.nmax = sb("m1_neg_max", [P, 2, 2], F32)
    m.sum = sb("m1_exp_sum", [P, 2, 2], F32)
    m.inv = sb("m1_inv_exp_sum", [P, 2, 2], F32)
    m.gy = u[:, :].rearrange("p b (j t) -> p b j t", j=2)
    m.m = v[:, 0].rearrange("p (b t) -> p b t", b=2)
    return m


def project(s, w, base, slot0, q, out, n=None):
    hi, lo = w.chunk(s.nc.tensor, base, slot0 + q // 3, q % 3)
    for k in range(KD):
        if n is not None:
            wait_normed(s, n, k)
        cols = slice(k * P, (k + 1) * P)
        last = product(s.nc, out, (hi[:, cols], lo[:, cols]), (s.xh[:, k], s.xl[:, k]),
                       k == 0, k == KD - 1)
    w.taken(last, q % 3)


def project_wide(s, w, base, slot0, q0, banks, n=None):
    for j in range(KD // 2):
        q = q0 + j
        hi, lo = w.chunk(s.nc.tensor, base, slot0 + q // 3, q % 3)
        for kk in range(2):
            k, cols = 2 * j + kk, slice(kk * HALF, (kk + 1) * HALF)
            if n is not None:
                wait_normed(s, n, k)
            for i in range(TT):
                toks = slice(i * P, (i + 1) * P)
                last = product(s.nc, banks[i][:], (s.xh[:, k, toks], s.xl[:, k, toks]),
                               (hi[:, cols], lo[:, cols]), k == 0, k == KD - 1)
        w.taken(last, q % 3)


def project_out(s, merged_hi, merged_lo, w, base, slot0, q0, mark, layer):
    pe = s.nc.tensor
    for k in range(KD):
        q = q0 + k
        hi, lo = w.chunk(pe, base, slot0 + q // 3, q % 3)
        mark.need(pe, layer, "m_ready", k + 1)
        for i in range(TT):
            toks = slice(i * P, (i + 1) * P)
            for half in range(2):
                cols = slice(half * HALF, (half + 1) * HALF)
                last = product(s.nc, s.py[2 * i + half][:], (merged_hi[:, k, toks], merged_lo[:, k, toks]),
                               (hi[:, cols], lo[:, cols]), k == 0, k == KD - 1)
            if k == KD - 1 and i == 0:
                last.then_inc(s.y_tile, 1)
        w.taken(last, q % 3)


def mix1_tensor(s, m, mark, w, base, slot0, n, layer):
    nc, pe = s.nc, s.nc.tensor

    def need(name, k):
        mark.need(pe, layer, name, k)

    norm_tensor(s, n)
    project_wide(s, w, base, slot0, Q_V, s.py[0:2], n)
    project_wide(s, w, base, slot0, Q_U, s.py[2:4])
    for j in range(8):
        if j >= 6:
            need("k_ready", j - 5)
        elif j >= 2:
            need("q_ready", j - 1)
        project(s, w, base, slot0, Q_Q + j, s.pj[j % 2][:, 0:T])
    need("u_ready", 2)
    pe.wait_ge(s.consts_loaded, 16 * CONSTS1)
    for g in range(F_GROUPS):
        if g >= 2:
            need("dft1_ready", g - 1)
        for i in range(TT):
            last = nc.tensor.matmul(s.pa[g % 2][:], m.u[:, i, g * F_DIM:(g + 1) * F_DIM],
                                    m.dft_t[:, i], start=i == 0, stop=i == TT - 1)
        mark.inc(last, "dft1_done")
    for g in range(F_GROUPS):
        need("dft1_ready", min(g + 3, F_GROUPS))
        if g >= 2:
            need("dft_ready", g - 1)
        out = s.pa[g % 2][:, 0:T]
        nc.tensor.matmul(out, m.dft_c[:, 0], m.a[:, g, 0:T], start=True, stop=False)
        mark.inc(nc.tensor.matmul(out, m.dft_c[:, 1], m.a[:, g, T:2 * T], start=False, stop=True),
                 "dft2_done")
    need("q_ready", 4)
    for job in range(JOBS1 + 1):
        if job < JOBS1:
            pair, i = divmod(job, TT)
            if job == 0:
                need("v_ready", 2)
                need("k_ready", 4)
            if job >= 2:
                need("biased", job - 1)
            mark.inc(nc.tensor.matmul(s.py[job % 2][:], m.qT[:, pair, i * P:(i + 1) * P],
                                      m.kbd[:, pair].rearrange("p e t -> p (e t)")), "scores_done")
            if job >= 1:
                need("gate_ready", 2 * job - 1)
            project(s, w, base, slot0, Q_GATE + 2 * job, s.pj[0][:, 0:T])
        if job >= 1:
            b = (job - 1) % 2
            need("probs_ready", job)
            if job >= 3:
                need("probsT_ready", job - 2)
            for e in range(2):
                for kc in range(TT):
                    last = nc.tensor.transpose(s.py[2 + b][:, (e * 2 + kc) * P:(e * 2 + kc + 1) * P],
                                               m.sc[:, b, e, kc * P:(kc + 1) * P], s.ident[:])
            mark.inc(last, "probsT_done")
        if job < JOBS1:
            if job >= 1:
                need("gate_ready", 2 * job)
            project(s, w, base, slot0, Q_GATE + 2 * job + 1, s.pj[1][:, 0:T])
        if job >= 1:
            pair = (job - 1) // TT
            need("probsT_ready", job)
            if job >= 3:
                need("o_ready", job - 2)
            elif job == 1:
                need("dft_ready", 4)
            for e in range(2):
                head = 2 * pair + e
                for kc in range(TT):
                    last = nc.tensor.matmul(s.pa[b][e * DH:(e + 1) * DH, 0:P],
                                            m.v[:, kc, head * DH:(head + 1) * DH],
                                            m.pT[:, b, e * 2 + kc], start=kc == 0, stop=kc == TT - 1)
            mark.inc(last, "pv_done")
    need("o_ready", JOBS1)
    for c in range(KD):
        q = Q_Y + c
        if c < 2:
            need("gate_ready", 15 + c)
        else:
            need("gated", c - 1)
        hi, lo = w.chunk(pe, base, slot0 + q // 3, q % 3)
        for j, (h_, l_) in enumerate(((m.oh, m.ol), (m.fh, m.fl))):
            for k in range(PAIRS):
                cols = slice((j * PAIRS + k) * P, (j * PAIRS + k + 1) * P)
                last = product(nc, s.pj[c % 2][:, j * T:(j + 1) * T], (hi[:, cols], lo[:, cols]),
                               (h_[:, k], l_[:, k]), k == 0, k == PAIRS - 1)
        w.taken(last, q % 3)
    project_out(s, s.xh, s.xl, w, base, slot0, Q_O, mark, layer)


def mix1_scalar(s, m, mark, w, base, slot0, n, nx, layer):
    nc, act = s.nc, s.nc.scalar

    def need(name, k):
        mark.need(act, layer, name, k)

    def feed(q):
        if q % 3 == 2 and q // 3 + 1 < MIX1_SLOTS:
            w.feed(act, base, slot0 + q // 3 + 1)

    w.feed(act, base, slot0)
    norm_scalar(s, n, 1, nx, ACT.Exp)
    for q0, dest, banks, name in ((Q_V, m.v, s.py[0:2], "v_ready"), (Q_U, m.u, s.py[2:4], "u_ready")):
        for q in range(q0, q0 + 4):
            feed(q)
        w.wait_taken(act, base, slot0 + (q0 + 3) // 3, (q0 + 3) % 3)
        for i in range(TT):
            mark.inc(nc.scalar.copy(dest[:, i], banks[i][:]), name)
    for q in range(Q_Q, Q_K):
        feed(q)
    for j in range(PAIRS):
        q = Q_K + j
        feed(q)
        w.wait_taken(act, base, slot0 + q // 3, q % 3)
        for e in range(2):
            rows = slice(e * DH, (e + 1) * DH)
            last = nc.scalar.copy(m.kbd[rows, j, e], s.pj[j % 2][rows, 0:T])
        mark.inc(last, "k_ready")
    for g in range(F_GROUPS):
        need("dft1_done", g + 1)
        mark.inc(nc.scalar.copy(m.a[:, g], s.pa[g % 2][:]), "dft1_ready")

    def gate(idx):
        q = Q_GATE + idx
        feed(q)
        w.wait_taken(act, base, slot0 + q // 3, q % 3)
        mark.inc(nc.scalar.copy(m.gate[:, idx // 2, idx % 2], s.pj[idx % 2][:, 0:T]), "gate_ready")

    for job in range(JOBS1 + 1):
        if job < JOBS1:
            gate(2 * job)
        if job >= 1:
            need("probsT_done", job)
            b = (job - 1) % 2
            mark.inc(nc.scalar.copy(m.pT[:, b].rearrange("p j q -> p (j q)"), s.py[2 + b][:]),
                     "probsT_ready")
        if job < JOBS1:
            gate(2 * job + 1)
            need("max_ready", job + 1)
            b = job % 2
            for e in range(2):
                mark.inc(nc.scalar.activation(m.sc[:, b, e], m.sc[:, b, e], ACT.Exp,
                                              bias=m.nmax[:, b, e:e + 1],
                                              accum_out=m.sum[:, b, e:e + 1]), "exp_ready")

    def sigmoid(c):
        for j in range(2):
            col = 3 * KD + j * KD + c
            mark.inc(nc.scalar.activation(m.gate[:, c, j], m.gate[:, c, j], ACT.Sigmoid,
                                          bias=s.par[:, col:col + 1]), "sigmoid_ready")

    need("gate_ready", 16)
    sigmoid(0)
    for c in range(KD):
        if c + 1 < KD:
            sigmoid(c + 1)
        feed(Q_Y + c)
        need("summed", c + 1)
        mark.inc(nc.scalar.copy(s.xh[:, c], m.m[:, c % 2]), "m_hi")
    for q in range(Q_O, Q_O + 8):
        feed(q)


def mix1_vector(s, m, mark, w, base, slot0, n, layer):
    nc, dve = s.nc, s.nc.vector

    def need(name, k):
        mark.need(dve, layer, name, k)

    norm_rest(s, n, 1)
    for j in range(PAIRS):
        q = Q_Q + j
        w.wait_taken(dve, base, slot0 + q // 3, q % 3)
        mark.inc(nc.vector.tensor_copy(m.qT[:, j], s.pj[j % 2][:, 0:T]), "q_ready")
    for g in range(F_GROUPS):
        need("dft2_done", g + 1)
        mark.inc(nc.vector.tensor_copy(m.fh[:, g], s.pa[g % 2][:, 0:T]), "dft_hi")
        need("dft_hi", g + 1)
        mark.inc(nc.vector.tensor_tensor(m.fl[:, g], s.pa[g % 2][:, 0:T],
                                         m.fh[:, g].bitcast(F32), ALU.subtract), "dft_ready")
    dve.wait_ge(s.bias_loaded, 16 * layer + 16)
    for job in range(JOBS1 + 2):
        b = job % 2
        if job < JOBS1:
            pair, i = divmod(job, TT)
            need("scores_done", job + 1)
            if job >= 2:
                need("probsT_done", job - 1)
            scores = m.sc[:, b].rearrange("p e t -> p (e t)")
            mark.inc(nc.vector.scalar_tensor_tensor(
                scores, s.py[b][:], SCALE,
                m.bias[:, i, 2 * pair:2 * pair + 2].rearrange("p e t -> p (e t)"),
                ALU.mult, ALU.add), "biased")
            need("biased", job + 1)
            mark.inc(nc.vector.tensor_reduce(m.nmax[:, b], m.sc[:, b], AX.X, ALU.max, negate=True),
                     "max_ready")
        if job >= 2:
            done, i = job - 1, (job - 2) % TT
            need("pv_done", done)
            toks = slice(i * P, (i + 1) * P)
            oh, ol = m.oh[:, (job - 2) // TT, toks], m.ol[:, (job - 2) // TT, toks]
            mark.inc(nc.vector.tensor_copy(oh, s.pa[b][:, 0:P]), "o_hi")
            need("o_hi", done)
            mark.inc(nc.vector.tensor_tensor(ol, s.pa[b][:, 0:P], oh.bitcast(F32), ALU.subtract),
                     "o_ready")
        if job < JOBS1:
            need("exp_ready", 2 * job + 2)
            mark.inc(nc.vector.reciprocal(m.inv[:, b], m.sum[:, b]), "inv_sum")
            need("inv_sum", job + 1)
            for e in range(2):
                last = nc.vector.tensor_scalar(m.sc[:, b, e], m.sc[:, b, e], m.inv[:, b, e:e + 1],
                                               None, ALU.mult)
            mark.inc(last, "probs_ready")
    merge_vector(s, m, mark, w, base, slot0, Q_Y, layer)
    finish(s, w, base, slot0 + (Q_O + 7) // 3, (Q_O + 7) % 3, n, 1.0, n + 1)


def merge_vector(s, m, mark, w, base, slot0, q0, layer):
    nc, dve = s.nc, s.nc.vector
    for c in range(KD):
        q, b = q0 + c, c % 2
        mark.need(dve, layer, "sigmoid_ready", 2 * c + 2)
        w.wait_taken(dve, base, slot0 + q // 3, q % 3)
        mark.inc(nc.vector.tensor_tensor(m.gy[:, b].rearrange("p j t -> p (j t)"),
                                         m.gate[:, c].rearrange("p j t -> p (j t)"),
                                         s.pj[b][:], ALU.mult), "gated")
        mark.need(dve, layer, "gated", c + 1)
        mark.inc(nc.vector.tensor_tensor(m.m[:, b], m.gy[:, b, 0], m.gy[:, b, 1], ALU.add), "summed")
        mark.need(dve, layer, "m_hi", c + 1)
        mark.inc(nc.vector.tensor_tensor(s.xl[:, c], m.m[:, b], s.xh[:, c].bitcast(F32),
                                         ALU.subtract), "m_ready")


def final_norm(s, eng_name, nx):
    nc = s.nc
    if eng_name == "scalar":
        act = nc.scalar
        for i in range(TT):
            act.wait_ge(s.x_ready, 4 * nx + 2 * i + 2)
            nc.scalar.activation(s.xn[:, i], s.x[:, i], ACT.Square,
                                 accum_out=s.ss[:, i, 0:1]).then_inc(s.final_step, 1)
        act.wait_ge(s.final_step, 3)
        nc.scalar.activation(s.rms[:], s.ms[:], ACT.Sqrt).then_inc(s.final_step, 1)
    else:
        dve = nc.vector
        dve.wait_ge(s.final_step, 2)
        nc.vector.tensor_scalar(s.ms[:], s.ss[:, :, 0], 1.0 / D, EPS, ALU.mult, ALU.add).then_inc(
            s.final_step, 1)
        dve.wait_ge(s.final_step, 4)
        nc.vector.reciprocal(s.inv[:], s.rms[:]).then_inc(s.final_step, 1)
        dve.wait_ge(s.final_step, 5)
        for i in range(TT):
            nc.vector.scalar_tensor_tensor(s.x[:, i], s.x[:, i], s.inv[:, i:i + 1], s.gfin[:],
                                           ALU.mult, ALU.mult).then_inc(s.x_ready, 2)


GATES_EARLY = 15
P2_SBQ, P2_WIDE, P2_G0, P2_CMP, P2_G1, P2_Y = 0, 4, 22, 26, 30, 41
GATES_LATE_C = GATES_EARLY // 3
P2_O = P2_Y + KD + 3 * (KD - GATES_LATE_C)
KV_W = 3 * NSA_GROUPS * DH
NG = NSA_HEADS + DSA_HEADS + 2 * NSA_GROUPS + 1
NORM_W = NG * DH
ZN_W = NORM_W + NSA_GROUPS * DH
ZI_IK, ZI_IW, ZI_GATE, ZI_NVS, ZI_DV = 256, 288, 296, 320, 448
KD_AT = (NSA_HEADS + DSA_HEADS) * DH
NKV = 2 * NSA_GROUPS + 1
SBW = T + P
REPLACED = -3.0e38
NSA_JOBS = [(p, i, br) for p in range(NSA_HEADS // 2) for i in range(TT) for br in (1, 2)]
DSA_JOBS = [(p, i, 3) for p in range(DSA_HEADS // 2) for i in range(TT)]
JOBS = NSA_JOBS + DSA_JOBS
GROUPS = [(p, i) for p in range((NSA_HEADS + DSA_HEADS) // 2) for i in range(TT)]


def job_group(job):
    p, i, br = JOBS[job]
    return (p + (NSA_HEADS // 2 if br == 3 else 0)) * TT + i


LAST_JOB = {g: max(j for j in range(len(JOBS)) if job_group(j) == g) for g in range(len(GROUPS))}
GATE_AT = {1: 8, 4: 9, 7: 10, 10: 11, 13: 12, 16: 13, 19: 14}

MIX2_TOTALS = dict(
    sq_ready=2, sk_ready=2, wide_ready=10, z_done=4, zm_ready=4, abs_ready=4, e_ready=4,
    l_ready=4, sp_ready=4, d_done=4, dm_ready=4, w_ready=4, osb_done=2, osb_hi=2, osb_ready=2,
    xg_done=1, xb_ready=1, xbh_ready=1, xbl_ready=1, gate_ready=15, hid_ready=2, cmp2_done=1,
    kc_raw=1, square_ready=2, ms_ready=2, root_ready=2, vec_step=57,
    iq_turned=1, iqd_ready=1, qk_turned=1, kdup_ready=1, kc_dup=1, iqT_done=1, ikT_done=1,
    iqT_ready=1, ikT_ready=1, qT_done=3, qT_ready=3, kT_done=3, kT_ready=3, kcT_done=1,
    kcT_ready=1, vbd_ready=1, gate_exp=1, gate_sig=1, idx_done=8, relu_ready=8, acc_ready=16,
    dbias_ready=2, cs_done=1, cs_ready=1, cexp_ready=1, cp_ready=1, pcT_done=1, pcT_ready=1,
    scores_done=20, biased=20, max_ready=20, exp_ready=40, inv_sum=20, inv_gated=16,
    probs_ready=20, probsT_done=20, probsT_ready=20, pv_done=20, o_hi=12, o_ready=12,
    sigmoid_ready=24, gated=16, summed=16, m_hi=8, m_ready=8)

PAR2 = NORM_W + DH + 2 * DH + 2 * (CMP_LEN // 2)


def mix2_state(nc, sb, s):
    with ExitStack() as early:
        zn = early.enter_context(nc.sbuf_tensor("m2_z_heads", [P, TT, ZN_W], F32))
        tmp = early.enter_context(nc.sbuf_tensor("m2_tmp", [P, TT * NORM_W], F32))
    mh = sb("m2_merged_hi", [P, KD, T], F32R)
    ml = sb("m2_merged_lo", [P, KD, T], F32R)
    merged = sb("m2_merged", [P, 2, T], F32)
    assert TT * (ZN_W + NORM_W) == 2 * KD * T + 2 * T
    zv = sb("m2_z_sbv_cmp", [P, TT, HALF], F32)
    sq = sb("m2_sb_qT", [P, 2, T], F32)
    sk = sb("m2_sb_kT", [P, 2, T], F32)
    sw = sb("m2_weights", [P, 2, HALF], F32)
    sc = sb("m2_scores", [P, 2, HALF], F32)
    oh = sb("m2_attn_hi", [P, 8, T], F32R)
    ol = sb("m2_attn_lo", [P, 8, T], F32R)
    gates = sb("m2_gates", [P, 7, T], F32)
    m = State()
    m.par = sb("m2_params", [P, PAR2], F32)
    m.sq = sq
    m.sk = sk
    m.zv = zv
    m.sc = sc
    m.sw = sw
    m.oh = oh
    m.ol = ol
    m.zi = sb("m2_z_index_v", [P, TT, HALF], F32)
    m.zn = zn
    m.mh = mh
    m.ml = ml
    m.xb = tmp[:, 0:CH].rearrange("p (a o g c) -> p a o g c", a=2, o=16, g=2)
    m.squares = tmp[:, :].rearrange("p (i n) -> p i n", i=TT)
    m.kdup = tmp[:, 0:TT * NKV * P].rearrange("p (i j e d) -> p i j e d", i=TT, j=NKV, e=2)
    m.ikdup = tmp[:, 1280:1536].rearrange("p (i e d) -> p i e d", i=TT, e=4)
    m.vbd = tmp[:, 1536:2048].rearrange("p (h d) -> p h d", h=NSA_HEADS)
    m.pT = tmp[:, 0:CH].rearrange("p (b j q) -> p b j q", b=2, j=4)
    m.xbh = oh[:, 4:8].rearrange("p a (o g c) -> p (a o) g c", g=2, c=CB)
    m.xbl = ol[:, 4:8].rearrange("p a (o g c) -> p (a o) g c", g=2, c=CB)
    m.qT = sb("m2_qT", [P, 6, T], F32)
    m.kbd = sb("m2_k_block", [P, NKV, 2, T], F32)
    m.iqT = sq
    m.pcT = sk[:, 0]
    m.ikbd = sb("m2_ik_block", [P, 4, T], F32)
    m.kcbd = sb("m2_kc_block", [P, NSA_GROUPS, 2, CB], F32)
    m.gate = ([s.xn[:].rearrange("p i d -> p (i d)")[:, g * T:] for g in range(8)]
             + [gates[:, g:].rearrange("p g t -> p (g t)") for g in range(7)])
    m.hidk = sb("m2_hidden_k", [P, NSA_GROUPS * CB], F32)
    m.hidv = sb("m2_hidden_v", [P, NSA_GROUPS, 4, CB], F32)
    m.kc = sb("m2_kc", [2 * CB, DH], F32)
    m.kcs = sb("m2_kc_square", [2 * CB, DH], F32)
    m.kc2 = sb("m2_kc_twice", [2 * CB, 2, DH], F32)
    m.stat = sb("m2_stats", [P, 4, TT * NG], F32)
    m.kstat = sb("m2_kc_stats", [2 * CB, 4], F32)
    m.turn = [t[:, j, 0:TT * NG * 8] for t in (sc, sw) for j in range(2)]
    m.acc = sw[:, 0].rearrange("p (i t) -> p i t", i=TT)
    m.work = sw[:, 1].rearrange("p (i t) -> p i t", i=TT)
    m.dbias = s.act
    m.m8 = sb("m2_top8", [P, 8], F32)
    m.iws = sb("m2_index_w", [P, TT, IDX_HEADS], F32)
    m.gsig = sb("m2_branch_gates", [P, TT, 3 * NSA_HEADS], F32)
    m.cs = sk[:, 1].rearrange("p (i h c) -> p i h c", i=TT, c=CB)
    m.cmx = sb("m2_cmp_max", [P, 2, TT * NSA_HEADS], F32)
    m.nmax = sb("m2_neg_max", [P, 2, 2], F32)
    m.sum = sb("m2_exp_sum", [P, 2, 2], F32)
    m.inv = sb("m2_inv_exp_sum", [P, 2, 2], F32)
    m.gy = zv[:, 0:1].rearrange("p a (b t) -> p (a b) t", b=2)
    m.gz = zv[:, 1:2].rearrange("p a (b t) -> p (a b) t", b=2)
    m.m = merged
    m.causal = sb("m2_causal", [P, TT, T], F32)
    m.sbmask = sb("m2_sb_mask", [P, SBW], F32)
    m.tri = sb("m2_tri_ones", [P, 2, P], F32)
    m.cmask = sb("m2_cmp_mask", [P, TT, CB], F32)
    m.hmask = sb("m2_head_mask", [P, NSA_HEADS], F32)
    m.rope = sb("m2_rope", [P, TT, 2, 8], F32)
    m.ropei = sb("m2_rope_index", [P, TT, 2, 4], F32)
    m.ropec = sb("m2_rope_cmp", [2 * CB, 2, 8], F32)
    return m


def mix2_tensor(s, m, mark, w, base, slot0, n, layer):
    nc, pe = s.nc, s.nc.tensor

    def need(name, k):
        mark.need(pe, layer, name, k)

    def gate(g):
        if g < 2:
            need("dm_ready", 3 + g)
        else:
            need("gate_ready", g - 1)
        project(s, w, base, slot0, P2_G0 + g if g < 4 else P2_G1 + g - 4, s.pj[g % 2][:, 0:T])

    def sb_z(h, last):
        rows, bank = slice((h % 2) * DH, (h % 2 + 1) * DH), s.pj[h % 2]
        nc.tensor.matmul(bank[:, 0:T], m.sk[rows, h // 2, 0:P], m.sq[rows, h // 2], start=True,
                         stop=False)
        return nc.tensor.matmul(bank[:, T:SBW], m.sk[rows, h // 2, P:T], m.sq[rows, h // 2, P:T],
                                start=False, stop=last)

    def sb_scores(h):
        if h < 2:
            need("sk_ready", h + 1)
        else:
            need("dm_ready", h - 1)
        mark.inc(sb_z(h, True), "z_done")

    def sb_tails(h):
        sp, bank = m.sc[:, h % 2], s.pj[h % 2]
        need("sp_ready", h + 1)
        sb_z(h, False)
        nc.tensor.matmul(bank[:, 0:T], m.tri[:, 0], sp[:, 0:T], start=False, stop=False)
        nc.tensor.matmul(bank[:, P:T], m.tri[:, 1], sp[:, T:SBW], start=False, stop=False)
        mark.inc(nc.tensor.matmul(bank[:, T:SBW], m.tri[:, 0], sp[:, T:SBW], start=False,
                                  stop=True), "d_done")

    def sb_out(pair):
        for h in (2 * pair, 2 * pair + 1):
            need("w_ready", h + 1)
            rows, cols = slice((h % 2) * DH, (h % 2 + 1) * DH), slice(h * DH, (h + 1) * DH)
            nc.tensor.matmul(s.pa[pair][rows, 0:T], m.zv[:, 0, cols], m.sw[:, h % 2, 0:T],
                             start=True, stop=False)
            last = nc.tensor.matmul(s.pa[pair][rows, P:T], m.zv[:, 1, cols], m.sw[:, h % 2, T:SBW],
                                    start=False, stop=True)
        mark.inc(last, "osb_done")

    norm_tensor(s, n)
    pe.wait_ge(s.zeroed, 1)
    for j in range(4):
        if j >= 2:
            need("sq_ready", j - 1)
        project(s, w, base, slot0, P2_SBQ + j, s.pj[j % 2][:, 0:T], n if j == 0 else None)
    project_wide(s, w, base, slot0, P2_WIDE, s.py[0:2])
    for h in (0, 1):
        sb_scores(h)
    project_wide(s, w, base, slot0, P2_WIDE + 4, s.py[2:4])
    for h in (0, 1):
        sb_tails(h)
    need("wide_ready", 2)
    project_wide(s, w, base, slot0, P2_WIDE + 8, s.py[0:2])
    sb_out(0)
    for h in (2, 3):
        sb_scores(h)
    need("wide_ready", 4)
    project_wide(s, w, base, slot0, P2_WIDE + 12, s.py[2:4])
    for h in (2, 3):
        sb_tails(h)
    need("wide_ready", 6)
    width = ZN_W - 2 * HALF
    for j in range(2):
        q = P2_WIDE + 16 + j
        hi, lo = w.chunk(pe, base, slot0 + q // 3, q % 3)
        for kk in range(4):
            k, cols = 4 * j + kk, slice(kk * width, (kk + 1) * width)
            for i in range(TT):
                toks = slice(i * P, (i + 1) * P)
                last = product(nc, s.py[i][:, 0:width], (s.xh[:, k, toks], s.xl[:, k, toks]),
                               (hi[:, cols], lo[:, cols]), k == 0, k == KD - 1)
        w.taken(last, q % 3)
    sb_out(1)
    need("wide_ready", 8)
    for a in range(2):
        for g in range(NSA_GROUPS):
            at = T + (a * NSA_GROUPS + g) * DH
            for i in range(TT):
                for e in range(2):
                    col = (a * NSA_GROUPS + g) * P + i * DH
                    last = nc.tensor.matmul(s.py[2][e * DH:(e + 1) * DH, col:col + DH],
                                            m.zv[:, i, at:at + DH], s.ident[:, e::2])
    mark.inc(last, "xg_done")
    for g in range(4):
        gate(g)
    need("osb_ready", 2)
    need("xbl_ready", 1)
    for j in range(4):
        q, a = P2_CMP + j, j // 2
        hi, lo = w.chunk(pe, base, slot0 + q // 3, q % 3)
        for k in range(8):
            o, cols = (j % 2) * 8 + k, slice(k * P, (k + 1) * P)
            xh = m.xbh[:, a * 16 + o].rearrange("p g c -> p (g c)")
            xl = m.xbl[:, a * 16 + o].rearrange("p g c -> p (g c)")
            last = product(nc, s.pa[1][:, a * 2 * CB:(a + 1) * 2 * CB], (hi[:, cols], lo[:, cols]),
                           (xh, xl), o == 0, o == 15)
        w.taken(last, q % 3)
    gate(4)
    need("hid_ready", 2)
    w2 = m.par[:, NORM_W + DH:NORM_W + 3 * DH]
    nc.tensor.matmul(s.pa[0][0:2 * CB, 0:DH], m.hidk[:], w2[:, 0:DH])
    mark.inc(nc.tensor.matmul(s.pa[0][:, DH:2 * DH], m.hidv[:].rearrange("p g r c -> p (g r c)"),
                              w2[:, DH:2 * DH]), "cmp2_done")
    gate(5)
    need("wide_ready", 10)
    need("iq_turned", 1)
    for cq in range(2):
        for i in range(TT):
            last = nc.tensor.transpose(s.py[0][:, cq * T + i * P:cq * T + (i + 1) * P],
                                       m.zi[:, i, cq * P:(cq + 1) * P], s.ident[:])
    mark.inc(last, "iqT_done")
    need("iqd_ready", 1)
    for i in range(TT):
        last = nc.tensor.transpose(s.py[1][:, i * P:(i + 1) * P],
                                   m.ikdup[:, i].rearrange("p e d -> p (e d)"), s.ident[:])
    mark.inc(last, "ikT_done")
    gate(6)
    need("qk_turned", 1)
    for c3, bank in enumerate((2, 3, 0)):
        if bank == 0:
            need("iqT_ready", 1)
        for cc in range(2):
            c = 2 * c3 + cc
            for i in range(TT):
                last = nc.tensor.transpose(s.py[bank][:, cc * T + i * P:cc * T + (i + 1) * P],
                                           m.zn[:, i, c * P:(c + 1) * P], s.ident[:])
        mark.inc(last, "qT_done")
    need("kdup_ready", 1)
    for j3, bank in enumerate((1, 2, 3)):
        if bank == 1:
            need("ikT_ready", 1)
        else:
            need("qT_ready", bank - 1)
        for j in range(2 * j3, min(2 * j3 + 2, NKV)):
            for i in range(TT):
                at = (j - 2 * j3) * T + i * P
                last = nc.tensor.transpose(s.py[bank][:, at:at + P],
                                           m.kdup[:, i, j].rearrange("p e d -> p (e d)"), s.ident[:])
        mark.inc(last, "kT_done")
    gate(7)
    need("kc_dup", 1)
    pe.sem_inc(s.order, 1)
    mark.inc(nc.tensor.transpose(s.pa[1][:, 0:2 * CB], m.kc2[:].rearrange("c e d -> c (e d)"),
                                 s.ident[0:2 * CB, 0:2 * CB]), "kcT_done")
    need("kcT_ready", 1)
    need("vbd_ready", 1)
    need("qT_ready", 2)
    for i in range(TT):
        for p in range(NSA_HEADS // 2):
            last = nc.tensor.matmul(s.pa[0][:, i * P + p * 2 * CB:i * P + (p + 1) * 2 * CB],
                                    m.qT[:, p, i * P:(i + 1) * P],
                                    m.kcbd[:, p // 2].rearrange("p e c -> p (e c)"))
    mark.inc(last, "cs_done")
    need("kT_ready", 3)
    need("qT_ready", 3)
    for u in range(8):
        i, cq, hh = u // 4, u // 2 % 2, u % 2
        kw = (i + 1) * P
        if u >= 4:
            need("relu_ready", u - 3)
        mark.inc(nc.tensor.matmul(s.py[u % 4][:, 0:2 * kw], m.iqT[:, cq, i * P:(i + 1) * P],
                                  m.ikbd[:, 2 * hh:2 * hh + 2, 0:kw]), "idx_done")
    need("cp_ready", 1)
    for i in range(TT):
        last = nc.tensor.transpose(s.pa[1][:, i * P:(i + 1) * P],
                                   m.cs[:, i].rearrange("p h c -> p (h c)"), s.ident[:])
    mark.inc(last, "pcT_done")
    need("pcT_ready", 1)
    for step in range(len(JOBS) + 2):
        if step < len(JOBS):
            p, i, br = JOBS[step]
            if step < 2:
                need("relu_ready", 8)
            else:
                need("biased", step - 1)
            kv = {1: p // 2, 2: NSA_GROUPS + p // 2, 3: NKV - 1}[br]
            qc, kw = p + (NSA_HEADS // 2 if br == 3 else 0), (i + 1) * P
            mark.inc(nc.tensor.matmul(s.py[step % 2][:, 0:2 * kw], m.qT[:, qc, i * P:(i + 1) * P],
                                      m.kbd[:, kv, :, 0:kw]), "scores_done")
        if 1 <= step <= len(JOBS):
            job = step - 1
            i, b = JOBS[job][1], job % 2
            need("probs_ready", job + 1)
            if job >= 2:
                need("probsT_ready", job - 1)
            for e in range(2):
                for kc in range(i + 1):
                    j = e * (i + 1) + kc
                    last = nc.tensor.transpose(s.py[2 + b][:, j * P:(j + 1) * P],
                                               m.sc[:, b, j * P:(j + 1) * P], s.ident[:])
            mark.inc(last, "probsT_done")
        if step in GATE_AT:
            gate(GATE_AT[step])
        if step >= 2:
            job = step - 2
            p, i, br = JOBS[job]
            g, toks = job_group(job), slice(i * P, (i + 1) * P)
            out, first = s.pa[g % 2], job == 0 or job_group(job - 1) != g
            need("probsT_ready", job + 1)
            if first and g >= 2:
                need("o_ready", g - 1)
            if first and br != 3:
                nc.tensor.matmul(out[:, 0:P], m.vbd[:, 2 * p:2 * p + 2].rearrange("p h d -> p (h d)"),
                                 m.pcT[:, toks], start=True, stop=False)
            for e in range(2):
                for kc in range(i + 1):
                    v = {1: m.zi[:, kc, ZI_NVS + p // 2 * DH:][:, 0:DH],
                         2: m.zn[:, kc, NORM_W + p // 2 * DH:][:, 0:DH],
                         3: m.zi[:, kc, ZI_DV:ZI_DV + DH]}[br]
                    last = nc.tensor.matmul(out[e * DH:(e + 1) * DH, 0:P], v,
                                            m.pT[:, job % 2, e * (i + 1) + kc],
                                            start=br == 3 and kc == 0, stop=kc == i and br >= 2)
            mark.inc(last, "pv_done")
    need("o_ready", len(GROUPS))
    q = P2_Y
    for c in range(KD):
        if c >= GATES_LATE_C:
            for r in range(3):
                late = 3 * (c - GATES_LATE_C) + r
                if late < 2:
                    need("biased", len(JOBS))
                elif late < 4:
                    need("probsT_ready", len(JOBS))
                else:
                    need("sigmoid_ready", GATES_EARLY + late - 3)
                project(s, w, base, slot0, q, s.py[late % 4][:, 0:T])
                q += 1
        need("gate_ready" if c < 2 else "gated", 15 if c < 2 else 2 * (c - 1))
        hi, lo = w.chunk(pe, base, slot0 + q // 3, q % 3)
        for k in range(8):
            out = (s.pj[c % 2][:, 0:T] if k < 2 else s.pj[c % 2][:, T:2 * T] if k < 6
                   else s.pa[c % 2][:, 0:T])
            cols = slice(k * P, (k + 1) * P)
            last = product(nc, out, (hi[:, cols], lo[:, cols]), (m.oh[:, k], m.ol[:, k]),
                           k in (0, 2, 6), k in (1, 5, 7))
        w.taken(last, q % 3)
        q += 1
    assert q == P2_O
    need("sigmoid_ready", 3 * KD)
    project_out(s, m.mh, m.ml, w, base, slot0, P2_O, mark, layer)


def mix2_scalar(s, m, mark, w, base, slot0, n, nx, layer):
    nc, act = s.nc, s.nc.scalar
    fed = [0]

    def need(name, k):
        mark.need(act, layer, name, k)

    def chunk(q, wait=True):
        while fed[0] <= q:
            if fed[0] % 3 == 2 and fed[0] // 3 + 1 < MIX2_SLOTS:
                w.feed(act, base, slot0 + fed[0] // 3 + 1)
            fed[0] += 1
        if wait:
            w.wait_taken(act, base, slot0 + q // 3, q % 3)

    def gate(g):
        chunk(P2_G0 + g if g < 4 else P2_G1 + g - 4)
        mark.inc(nc.scalar.copy(m.gate[g][:, 0:T], s.pj[g % 2][:, 0:T]), "gate_ready")

    def wide(b, dests):
        chunk(P2_WIDE + (4 * b + 3 if b < 4 else 17))
        for i in range(TT):
            bank = s.py[2 * (b % 2) + i]
            mark.inc(nc.scalar.copy(dests[i], bank[:, 0:dests[i].shape[-1]]), "wide_ready")

    def sb_softplus(h):
        for k in (h, h + 1):
            need("abs_ready", k + 1)
            a = m.sw[:, k % 2, 0:SBW]
            mark.inc(nc.scalar.activation(a, a, ACT.Exp, scale=-1.0), "e_ready")
        for k in (h, h + 1):
            need("e_ready", k + 1)
            a = m.sw[:, k % 2, 0:SBW]
            mark.inc(nc.scalar.activation(a, a, ACT.Ln, bias=1.0), "l_ready")

    def sb_weights(h):
        for k in (h, h + 1):
            need("dm_ready", k + 1)
            a = m.sw[:, k % 2, 0:SBW]
            mark.inc(nc.scalar.activation(a, a, ACT.Exp), "w_ready")

    w.feed(act, base, slot0)
    norm_scalar(s, n, 1, nx, ACT.Exp)
    chunk(P2_SBQ + 1, False)
    for j in range(2):
        chunk(P2_SBQ + 2 + j)
        mark.inc(nc.scalar.copy(m.sk[:, j], s.pj[j][:, 0:T]), "sk_ready")
    wide(0, [m.zv[:, i] for i in range(TT)])
    sb_softplus(0)
    wide(1, [m.zi[:, i] for i in range(TT)])
    sb_weights(0)
    wide(2, [m.zn[:, i, 0:HALF] for i in range(TT)])
    sb_softplus(2)
    wide(3, [m.zn[:, i, HALF:2 * HALF] for i in range(TT)])
    sb_weights(2)
    wide(4, [m.zn[:, i, 2 * HALF:ZN_W] for i in range(TT)])
    need("xb_ready", 1)
    mark.inc(nc.scalar.copy(m.xbh[:], m.xb[:].rearrange("p a o g c -> p (a o) g c")), "xbh_ready")
    gate(0)
    gate(1)
    need("xbl_ready", 1)
    for i in range(TT):
        mark.inc(nc.scalar.activation(m.squares[:, i], m.zn[:, i, 0:NORM_W], ACT.Square),
                 "square_ready")
    gate(2)
    gate(3)
    chunk(P2_CMP + 3)
    mark.inc(nc.scalar.activation(m.hidk[:], s.pa[1][:, 0:2 * CB], ACT.Silu), "hid_ready")
    hv = s.pa[1][:, 2 * CB:4 * CB].rearrange("p (g a c) -> p g a c", g=NSA_GROUPS, a=1)
    mark.inc(nc.scalar.activation(m.hidv[:], hv.to_broadcast([P, NSA_GROUPS, 4, CB]), ACT.Silu),
             "hid_ready")
    gate(4)
    need("ms_ready", 1)
    mark.inc(nc.scalar.activation(m.stat[:, 2], m.stat[:, 1], ACT.Sqrt), "root_ready")
    need("ms_ready", 2)
    mark.inc(nc.scalar.activation(m.kstat[:, 2:3], m.kstat[:, 1:2], ACT.Sqrt), "root_ready")
    gate(5)
    need("iqT_done", 1)
    mark.inc(nc.scalar.copy(m.iqT[:].rearrange("p a t -> p (a t)"), s.py[0][:]), "iqT_ready")
    need("ikT_done", 1)
    for e in range(4):
        rows = slice(e * IDX_DIM, (e + 1) * IDX_DIM)
        last = nc.scalar.copy(m.ikbd[rows, e], s.py[1][rows, 0:T])
    mark.inc(last, "ikT_ready")
    gate(6)
    for c3, bank in enumerate((2, 3, 0)):
        need("qT_done", c3 + 1)
        mark.inc(nc.scalar.copy(m.qT[:, 2 * c3:2 * c3 + 2].rearrange("p a t -> p (a t)"),
                                s.py[bank][:]), "qT_ready")
    for j3, bank in enumerate((1, 2, 3)):
        need("kT_done", j3 + 1)
        k = min(2, NKV - 2 * j3)
        for e in range(2):
            rows = slice(e * DH, (e + 1) * DH)
            last = nc.scalar.copy(m.kbd[rows, 2 * j3:2 * j3 + k, e],
                                  s.py[bank][rows, 0:k * T].rearrange("p (a t) -> p a t", a=k))
        mark.inc(last, "kT_ready")
    gate(7)
    mark.inc(nc.scalar.activation(m.gsig[:], m.zi[:, :, ZI_GATE:ZI_NVS], ACT.Exp, scale=-1.0),
             "gate_exp")
    need("cs_ready", 1)
    mark.inc(nc.scalar.activation(m.cs[:], m.cs[:], ACT.Exp), "cexp_ready")
    for u in range(8):
        kw = (u // 4 + 1) * P
        need("idx_done", u + 1)
        if u >= 2:
            need("acc_ready", 2 * (u - 1))
        mark.inc(nc.scalar.activation(m.sc[:, u % 2, 0:2 * kw], s.py[u % 4][:, 0:2 * kw], ACT.Relu),
                 "relu_ready")
    need("pcT_done", 1)
    mark.inc(nc.scalar.copy(m.pcT[:], s.pa[1][:, 0:T]), "pcT_ready")
    for step in range(len(JOBS) + 1):
        if step >= 1:
            job = step - 1
            b, width = job % 2, 2 * (JOBS[job][1] + 1)
            need("probsT_done", job + 1)
            mark.inc(nc.scalar.copy(m.pT[:, b, 0:width].rearrange("p j q -> p (j q)"),
                                    s.py[2 + b][:, 0:width * P]), "probsT_ready")
        if step in GATE_AT:
            gate(GATE_AT[step])
        if step < len(JOBS):
            b, kw = step % 2, (JOBS[step][1] + 1) * P
            need("max_ready", step + 1)
            for e in range(2):
                at = m.sc[:, b, e * kw:(e + 1) * kw]
                mark.inc(nc.scalar.activation(at, at, ACT.Exp, bias=m.nmax[:, b, e:e + 1],
                                              accum_out=m.sum[:, b, e:e + 1]), "exp_ready")
    q_at = [P2_Y]

    def sigmoids(c):
        for r in range(3):
            g = 3 * c + r
            if c < GATES_LATE_C:
                src = dest = m.gate[g][:, 0:T]
            else:
                late = g - GATES_EARLY
                chunk(q_at[0])
                q_at[0] += 1
                mark.need(act, layer, "gated", 2 * (late // 3 + 1))
                src, dest = s.py[late % 4][:, 0:T], m.gate[late][:, 0:T]
            mark.inc(nc.scalar.activation(dest, src, ACT.Sigmoid), "sigmoid_ready")

    need("gate_ready", GATES_EARLY)
    sigmoids(0)
    for c in range(KD):
        chunk(q_at[0], False)
        q_at[0] += 1
        if c + 1 < KD:
            sigmoids(c + 1)
        need("summed", 2 * c + 2)
        mark.inc(nc.scalar.copy(m.mh[:, c], m.m[:, c % 2]), "m_hi")
    chunk(P2_O + KD - 1, False)


def mix2_vector(s, m, mark, w, base, slot0, n, layer):
    nc, dve = s.nc, s.nc.vector

    def need(name, k):
        mark.need(dve, layer, name, k)

    def step(ins):
        mark.inc(ins, "vec_step")
        need("vec_step", mark.made["vec_step"])

    def after(name):
        need(name, mark.made[name])

    norm_rest(s, n, 1)
    dve.wait_ge(s.consts2_loaded, 16 * CONSTS2)
    for j in range(2):
        q = P2_SBQ + j
        w.wait_taken(dve, base, slot0 + q // 3, q % 3)
        mark.inc(nc.vector.tensor_scalar(m.sq[:, j], s.pj[j][:, 0:T], SCALE, None, ALU.mult),
                 "sq_ready")
    for pair in range(2):
        for h in (2 * pair, 2 * pair + 1):
            z, a = m.sc[:, h % 2, 0:SBW], m.sw[:, h % 2, 0:SBW]
            need("z_done", h + 1)
            if h >= 2:
                need("d_done", h - 1)
                need("osb_done", 1)
            mark.inc(nc.vector.tensor_tensor(z, s.pj[h % 2][:, 0:SBW], m.sbmask[:], ALU.add),
                     "zm_ready")
            after("zm_ready")
            mark.inc(nc.vector.scalar_tensor_tensor(a, z, -1.0, z, ALU.mult, ALU.max), "abs_ready")
        for h in (2 * pair, 2 * pair + 1):
            z, a = m.sc[:, h % 2, 0:SBW], m.sw[:, h % 2, 0:SBW]
            need("l_ready", h + 1)
            mark.inc(nc.vector.scalar_tensor_tensor(z, z, 0.0, a, ALU.max, ALU.add), "sp_ready")
        for h in (2 * pair, 2 * pair + 1):
            need("d_done", h + 1)
            mark.inc(nc.vector.tensor_tensor(m.sw[:, h % 2, 0:SBW], s.pj[h % 2][:, 0:SBW],
                                             m.sbmask[:], ALU.add), "dm_ready")
        need("osb_done", pair + 1)
        mark.inc(nc.vector.tensor_copy(m.oh[:, pair], s.pa[pair][:, 0:T]), "osb_hi")
        after("osb_hi")
        mark.inc(nc.vector.tensor_tensor(m.ol[:, pair], s.pa[pair][:, 0:T],
                                         m.oh[:, pair].bitcast(F32), ALU.subtract), "osb_ready")
    need("xg_done", 1)
    dve.wait_ge(s.par2_loaded, 16 * layer + 16)
    nc.vector.memset(m.xb[:].rearrange("p a o g c -> p (a o g) c")[:, :, NCMP:CB], 0.0)
    xg = s.py[2][:].rearrange("p (a g c o) -> p a g c o", a=2, g=NSA_GROUPS, c=CB)
    pe_col = NORM_W + 3 * DH
    for a in range(2):
        for half in range(2):
            pos = m.par[:, pe_col + a * 16 + half * 8:pe_col + a * 16 + half * 8 + 8]
            last = nc.vector.tensor_tensor(
                m.xb[:, a, half * 8:half * 8 + 8, :, 0:NCMP].rearrange("p o g c -> p g c o"),
                xg[:, a, :, half:half + NCMP, :],
                pos.rearrange("p (x y o) -> p x y o", x=1, y=1).to_broadcast([P, 2, NCMP, 8]),
                ALU.add)
    mark.inc(last, "xb_ready")
    need("xbh_ready", 1)
    mark.inc(nc.vector.tensor_tensor(m.xbl[:], m.xb[:].rearrange("p a o g c -> p (a o) g c"),
                                     m.xbh[:].bitcast(F32), ALU.subtract), "xbl_ready")

    def turn(x, half, cos, sin, name):
        shape = list(x.shape[:-1]) + [half]
        x1, x2 = x[..., 0:half], x[..., half:2 * half]
        size = 1
        for dim in shape[1:]:
            size *= dim
        t = []
        for buf in m.turn:
            flat = buf[0:shape[0], 0:size]
            t.append(flat.rearrange("p (i g f) -> p i g f", i=shape[1], f=half) if len(shape) == 4
                     else flat)
        for out, a, table in ((t[0], x1, cos), (t[1], x2, sin), (t[2], x2, cos), (t[3], x1, sin)):
            last = nc.vector.tensor_tensor(out, a, table.to_broadcast(shape), ALU.mult)
        step(last)
        nc.vector.tensor_tensor(x1, t[0], t[1], ALU.subtract)
        mark.inc(nc.vector.tensor_tensor(x2, t[2], t[3], ALU.add), name)

    def table(r, k, half):
        return r[:, :, k].rearrange("p i (g f) -> p i g f", g=1)

    need("wide_ready", 4)
    turn(m.zi[:, :, 0:ZI_IW].rearrange("p i (g f) -> p i g f", f=IDX_DIM), 4,
         table(m.ropei, 0, 4), table(m.ropei, 1, 4), "iq_turned")
    heads = m.zn[:, :, 0:NORM_W].rearrange("p i (g f) -> p i g f", f=DH)
    need("square_ready", 2)
    step(nc.vector.tensor_reduce(m.stat[:, 0], m.squares[:].rearrange("p i (g f) -> p (i g) f", f=DH),
                                 AX.X, ALU.add))
    mark.inc(nc.vector.tensor_scalar(m.stat[:, 1], m.stat[:, 0], 1.0 / DH, EPS, ALU.mult, ALU.add),
             "ms_ready")
    need("cmp2_done", 1)
    mark.inc(nc.vector.tensor_tensor(
        m.vbd[:], s.pa[0][:, DH:2 * DH].rearrange("p (h d) -> p h d", h=1).to_broadcast(
            [P, NSA_HEADS, DH]),
        m.hmask[:].rearrange("p (h d) -> p h d", d=1).to_broadcast([P, NSA_HEADS, DH]), ALU.mult),
        "vbd_ready")
    step(nc.vector.tensor_copy(m.kc[:], s.pa[0][0:2 * CB, 0:DH]))
    step(nc.vector.tensor_tensor(m.kcs[:], m.kc[:], m.kc[:], ALU.mult))
    step(nc.vector.tensor_reduce(m.kstat[:, 0:1], m.kcs[:], AX.X, ALU.add))
    mark.inc(nc.vector.tensor_scalar(m.kstat[:, 1:2], m.kstat[:, 0:1], 1.0 / DH, EPS, ALU.mult,
                                     ALU.add), "ms_ready")
    ik = m.zi[:, :, ZI_IK:ZI_IW].rearrange("p i (e d) -> p i e d", e=1)
    after("iq_turned")
    mark.inc(nc.vector.tensor_copy(m.ikdup[:], ik.to_broadcast([P, TT, 4, IDX_DIM])), "iqd_ready")
    need("root_ready", 1)
    step(nc.vector.reciprocal(m.stat[:, 3], m.stat[:, 2]))
    step(nc.vector.tensor_tensor(
        heads, heads, m.stat[:, 3].rearrange("p (i g f) -> p i g f", i=TT, f=1).to_broadcast(
            [P, TT, NG, DH]), ALU.mult))
    for i in range(TT):
        last = nc.vector.tensor_tensor(m.zn[:, i, 0:NORM_W], m.zn[:, i, 0:NORM_W],
                                       m.par[:, 0:NORM_W], ALU.mult)
    step(last)
    turn(m.zn[:, :, 0:NORM_W].rearrange("p i (g f) -> p i g f", f=DH), 8,
         table(m.rope, 0, 8), table(m.rope, 1, 8), "qk_turned")
    after("qk_turned")
    for i in range(TT):
        keys = m.zn[:, i, KD_AT:KD_AT + NKV * DH].rearrange("p (j e d) -> p j e d", j=NKV, e=1)
        last = nc.vector.tensor_copy(m.kdup[:, i], keys.to_broadcast([P, NKV, 2, DH]))
    mark.inc(last, "kdup_ready")
    need("root_ready", 2)
    step(nc.vector.reciprocal(m.kstat[:, 3:4], m.kstat[:, 2:3]))
    step(nc.vector.scalar_tensor_tensor(m.kc[:], m.kc[:], m.kstat[:, 3:4],
                                        m.par[0:2 * CB, NORM_W:NORM_W + DH], ALU.mult, ALU.mult))
    turn(m.kc[:], 8, m.ropec[:, 0], m.ropec[:, 1], "kc_raw")
    after("kc_raw")
    mark.inc(nc.vector.tensor_copy(m.kc2[:], m.kc[:].rearrange("c (e d) -> c e d", e=1)
                                   .to_broadcast([2 * CB, 2, DH])), "kc_dup")
    step(nc.vector.tensor_scalar(m.iws[:], m.zi[:, :, ZI_IW:ZI_GATE],
                                 (IDX_HEADS * IDX_DIM) ** -0.5, None, ALU.mult))
    need("gate_exp", 1)
    step(nc.vector.tensor_scalar(m.gsig[:], m.gsig[:], 1.0, None, ALU.add))
    mark.inc(nc.vector.reciprocal(m.gsig[:], m.gsig[:]), "gate_sig")
    need("kcT_done", 1)
    for e in range(2):
        rows = slice(e * DH, (e + 1) * DH)
        last = nc.vector.tensor_copy(m.kcbd[rows, :, e],
                                     s.pa[1][rows, 0:2 * CB].rearrange("p (g c) -> p g c", c=CB))
    mark.inc(last, "kcT_ready")
    need("cs_done", 1)
    for i in range(TT):
        last = nc.vector.scalar_tensor_tensor(
            m.cs[:, i], s.pa[0][:, i * P:(i + 1) * P].rearrange("p (h c) -> p h c", c=CB), SCALE,
            m.cmask[:, i].rearrange("p (h c) -> p h c", h=1).to_broadcast([P, NSA_HEADS, CB]),
            ALU.mult, ALU.add)
    step(last)
    flat = m.cs[:].rearrange("p i h c -> p (i h) c")

    def over_keys(x):
        return x.rearrange("p (n c) -> p n c", c=1).to_broadcast([P, TT * NSA_HEADS, CB])

    step(nc.vector.tensor_reduce(m.cmx[:, 0], flat, AX.X, ALU.max))
    step(nc.vector.tensor_scalar(m.cmx[:, 0], m.cmx[:, 0], 0.1 * MASKED, None, ALU.max))
    mark.inc(nc.vector.tensor_tensor(flat, flat, over_keys(m.cmx[:, 0]), ALU.subtract), "cs_ready")
    need("cexp_ready", 1)
    step(nc.vector.tensor_reduce(m.cmx[:, 1], flat, AX.X, ALU.add))
    step(nc.vector.tensor_scalar(m.cmx[:, 1], m.cmx[:, 1], 1e-30, None, ALU.max))
    step(nc.vector.reciprocal(m.cmx[:, 1], m.cmx[:, 1]))
    g0 = m.gsig[:].rearrange("p i (h r) -> p i h r", r=3)[:, :, :, 0]
    mx = m.cmx[:, 1].rearrange("p (i h) -> p i h", i=TT)
    step(nc.vector.tensor_tensor(mx, mx, g0, ALU.mult))
    mark.inc(nc.vector.tensor_tensor(flat, flat, over_keys(m.cmx[:, 1]), ALU.mult), "cp_ready")
    for u in range(8):
        i, kw = u // 4, (u // 4 + 1) * P
        acc = m.acc[:, i, 0:kw]
        need("relu_ready", u + 1)
        for e in range(2):
            h = (u % 4) * 2 + e
            relu, wh = m.sc[:, u % 2, e * kw:(e + 1) * kw], m.iws[:, i, h:h + 1]
            if h == 0:
                ins = nc.vector.tensor_scalar(acc, relu, wh, None, ALU.mult)
            else:
                after("acc_ready")
                ins = nc.vector.scalar_tensor_tensor(acc, relu, wh, acc, ALU.mult, ALU.add)
            mark.inc(ins, "acc_ready")

    def ordered():
        dve.sem_inc(s.order, 1)

    for i in range(TT):
        kw = (i + 1) * P
        acc, work, causal = m.acc[:, i, 0:kw], m.work[:, i, 0:kw], m.causal[:, i, 0:kw]
        after("acc_ready")
        step(nc.vector.tensor_tensor(acc, acc, causal, ALU.add))
        src = acc
        for _ in range(TOPK // 8):
            ordered()
            step(nc.vector.max(m.m8[:], src))
            ordered()
            step(nc.vector.match_replace(work, m.m8[:], src, REPLACED))
            src = work
        step(nc.vector.tensor_scalar(work, work, 0.5 * REPLACED, MASKED, ALU.is_gt, ALU.mult))
        mark.inc(nc.vector.tensor_tensor(m.dbias[:, i, 0:kw], work, causal, ALU.add), "dbias_ready")
    after("dbias_ready")
    for job in range(len(JOBS) + 3):
        if job < len(JOBS):
            p, i, br = JOBS[job]
            b, kw = job % 2, (i + 1) * P
            need("scores_done", job + 1)
            if job >= 2:
                need("probsT_done", job - 1)
            sc = m.sc[:, b, 0:2 * kw].rearrange("p (e t) -> p e t", e=2)
            bias = (m.dbias if br == 3 else m.causal)[:, i, 0:kw]
            mark.inc(nc.vector.scalar_tensor_tensor(
                sc, s.py[b][:, 0:2 * kw].rearrange("p (e t) -> p e t", e=2), SCALE,
                bias.rearrange("p (e t) -> p e t", e=1).to_broadcast([P, 2, kw]),
                ALU.mult, ALU.add), "biased")
            after("biased")
            mark.inc(nc.vector.tensor_reduce(m.nmax[:, b], sc, AX.X, ALU.max, negate=True),
                     "max_ready")
        if job >= 3 and LAST_JOB[job_group(job - 3)] == job - 3:
            g = job_group(job - 3)
            need("pv_done", job - 2)
            at = (slice(0, P), 2 + g // TT, slice((g % TT) * P, (g % TT + 1) * P))
            mark.inc(nc.vector.tensor_copy(m.oh[at], s.pa[g % 2][:, 0:P]), "o_hi")
            after("o_hi")
            mark.inc(nc.vector.tensor_tensor(m.ol[at], s.pa[g % 2][:, 0:P], m.oh[at].bitcast(F32),
                                             ALU.subtract), "o_ready")
        if job < len(JOBS):
            need("exp_ready", 2 * job + 2)
            mark.inc(nc.vector.reciprocal(m.inv[:, b], m.sum[:, b]), "inv_sum")
            after("inv_sum")
            if br != 3:
                gates = m.gsig[:, i].rearrange("p (h r) -> p h r", r=3)[:, 2 * p:2 * p + 2, br]
                mark.inc(nc.vector.tensor_tensor(m.inv[:, b], m.inv[:, b], gates, ALU.mult),
                         "inv_gated")
                after("inv_gated")
            for e in range(2):
                last = nc.vector.tensor_scalar(sc[:, e], sc[:, e], m.inv[:, b, e:e + 1], None,
                                               ALU.mult)
            mark.inc(last, "probs_ready")
    q = P2_Y
    for c in range(KD):
        q += 3 if c >= GATES_LATE_C else 0
        b, g = c % 2, 3 * (c if c < GATES_LATE_C else c - GATES_LATE_C)
        need("sigmoid_ready", 3 * c + 3)
        w.wait_taken(dve, base, slot0 + q // 3, q % 3)
        q += 1
        mark.inc(nc.vector.tensor_tensor(m.gy[:].rearrange("p j t -> p (j t)"), m.gate[g][:, 0:2 * T],
                                         s.pj[b][:], ALU.mult), "gated")
        mark.inc(nc.vector.tensor_tensor(m.gz[:, 0], m.gate[g + 2][:, 0:T], s.pa[b][:, 0:T],
                                         ALU.mult), "gated")
        after("gated")
        mark.inc(nc.vector.tensor_tensor(m.gz[:, 1], m.gy[:, 0], m.gy[:, 1], ALU.add), "summed")
        after("summed")
        mark.inc(nc.vector.tensor_tensor(m.m[:, b], m.gz[:, 1], m.gz[:, 0], ALU.add), "summed")
        need("m_hi", c + 1)
        mark.inc(nc.vector.tensor_tensor(m.ml[:, c], m.m[:, b], m.mh[:, c].bitcast(F32),
                                         ALU.subtract), "m_ready")
    finish(s, w, base, slot0 + (P2_O + 7) // 3, (P2_O + 7) % 3, n, 1.0, n + 1)


PAR1 = 3 * KD + 2 * KD
SLOTS1 = 2 * FC + MIX1_SLOTS
SLOTS2 = 2 * FC + MIX2_SLOTS


PAR = 3 * KD
SLOTS2_AT = LAYERS * SLOTS1
CONSTS1 = 3
CONSTS2 = 8
X2 = 3 * LAYERS + 1


def build(nc, a):
    with ExitStack() as ctx:
        def sb(name, shape, dt):
            return ctx.enter_context(nc.sbuf_tensor(name, shape, dt))

        def ps(name, shape, dt):
            return ctx.enter_context(nc.psum_tensor(name, shape, dt))

        def sem(name):
            return ctx.enter_context(nc.semaphore(name))

        w = Stream(nc, sb, sem, a["stream"])
        s = shared_state(nc, sb, ps, sem)
        s.par = sb("params", [P, PAR1], F32)
        s.par1_all = sb("params1_all", [P, LAYERS, PAR1], F32)
        s.par2_all = sb("params2_all", [P, LAYERS, PAR], F32)
        s.bias_loaded, s.gain_loaded = sem("bias_loaded"), sem("gain_loaded")
        s.par2_loaded = sem("par2_loaded")
        s.final_step, s.order = sem("final_step"), sem("order")
        s.consts2_loaded, s.zeroed = sem("consts2_loaded"), sem("zeroed")
        inputs_loaded, s.consts_loaded = sem("inputs_loaded"), sem("consts_loaded")
        par_ready, stored = sem("par_ready"), sem("stored")
        mark1, mark2 = Marks(sem, "m1_", MIX1_TOTALS), Marks(sem, "m2_", MIX2_TOTALS)
        with ExitStack() as own:
            m1 = mix1_state(lambda name, shape, dt: own.enter_context(nc.sbuf_tensor(name, shape, dt)))
        with ExitStack() as own:
            m2 = mix2_state(nc, lambda name, shape, dt: own.enter_context(nc.sbuf_tensor(name, shape, dt)), s)
        s.gfin = m1.u[:].rearrange("p i n -> p (i n)")
        loads = ((s.x[:], a["x"].rearrange("(i p) d -> p i d", p=P)), (s.ident[:], a["ident"]),
                 (s.par1_all[:], a["params1"]))
        later_loads = ((m1.dft_t[:], a["dft_t"]), (m1.dft_c[:], a["dft_c"]),
                       (s.par2_all[:], a["gains2"]))
        consts2 = ((m2.causal, "causal"), (m2.sbmask, "sbmask"), (m2.tri, "tri"),
                   (m2.cmask, "cmask"), (m2.hmask, "hmask"), (m2.rope, "rope"),
                   (m2.ropei, "ropei"), (m2.ropec, "ropec"))
        block = ctx.enter_context(nc.Block())

        @block.sync
        def _(sp):
            w.load(sp, 0, 0, 0)
            with sp.Fori(0, LAYERS) as layer:
                base = layer * SLOTS1
                w.load_slots(sp, base, FC)
                sp.wait_ge(s.x_ready, 12 * layer + 4)
                sp.dma_start(m1.bias[:], a["rel_bias"][layer]).then_inc(s.bias_loaded, 16)
                w.load_slots(sp, base + FC, MIX1_SLOTS + FC)
            sp.wait_ge(s.x_ready, 4 * 3 * LAYERS + 4)
            sp.dma_start(s.gfin, a["final_gain"]).then_inc(s.gain_loaded, 16)
            with sp.Fori(0, LAYERS) as layer:
                base = layer * SLOTS2 + SLOTS2_AT
                w.load_slots(sp, base, FC)
                sp.wait_ge(s.x_ready, 12 * layer + 4 * X2 + 4)
                sp.dma_start(m2.par[:], a["params2"][layer]).then_inc(s.par2_loaded, 16)
                w.load_slots(sp, base + FC, MIX2_SLOTS + FC)
            sp.wait_ge(s.x_ready, 4 * (X2 + 3 * LAYERS) + 4)
            sp.dma_start(a["out"].rearrange("(i p) d -> p i d", p=P), s.x[:]).then_inc(stored, 16)
            sp.wait_ge(stored, 16)

        @block.gpsimd
        def _(pool):
            pool.sem_inc(w.split[0], 2)
            pool.sem_inc(w.split[1], 2)
            w.rest(pool, 0, 0, 0)

            def split(first, end):
                with pool.Fori(first // 2, end // 2) as i:
                    for k in range(2):
                        w.rest(pool, 0, 2 * i + k + 1, 1 - k)
                        w.rest(pool, 1, 2 * i + k, k)

            split(0, SLOTS2_AT + FC)
            pool.wait_ge(s.x_ready, 4 * X2 + 4)
            for diagonals in (m2.kbd, m2.ikbd, m2.kcbd):
                last = nc.gpsimd.memset(diagonals[:], 0.0)
            last.then_inc(s.zeroed, 1)
            split(SLOTS2_AT + FC, LAYERS * (SLOTS1 + SLOTS2))

        @block.scalar
        def _(act):
            for dest, src in loads:
                act.dma_start(dest, src).then_inc(inputs_loaded, 16)
            for dest, src in later_loads:
                act.dma_start(dest, src).then_inc(s.consts_loaded, 16)
            act.wait_ge(inputs_loaded, 16 * len(loads))
            act.sem_inc(s.table_in, 1)
            w.round_hi(act, 0, 0, 0)
            with act.Fori(0, LAYERS) as layer:
                base, n = layer * SLOTS1, 3 * layer
                ffn_scalar(s, w, base, 0, n, 0, n)
                mix1_scalar(s, m1, mark1, w, base, FC, n + 1, n + 1, layer)
                ffn_scalar(s, w, base, FC + MIX1_SLOTS, n + 2, 2, n + 2)
            final_norm(s, "scalar", 3 * LAYERS)
            act.wait_ge(s.x_ready, 4 * X2 + 4)
            for dest, name in consts2:
                act.dma_start(dest[:], a[name]).then_inc(s.consts2_loaded, 16)
            with act.Fori(0, LAYERS) as layer:
                base, n = layer * SLOTS2 + SLOTS2_AT, 3 * layer + 3 * LAYERS
                ffn_scalar(s, w, base, 0, n, 0, n + 1)
                mix2_scalar(s, m2, mark2, w, base, FC, n + 1, n + 2, layer)
                ffn_scalar(s, w, base, FC + MIX2_SLOTS, n + 2, 2, n + 3)

        @block.vector
        def _(dve):
            nc.vector.memset(m1.kbd[:], 0.0)
            dve.wait_ge(inputs_loaded, 16 * len(loads))
            dve.sem_inc(s.x_ready, 4)
            with dve.Fori(0, LAYERS) as layer:
                base, n, c0 = layer * SLOTS1, 3 * layer, 2 * FC * layer
                nc.vector.tensor_copy(s.par[:], s.par1_all[:, layer]).then_inc(par_ready, 1)
                dve.wait_ge(par_ready, layer + 1)
                norm_start(s, n)
                ffn_vector(s, w, base, 0, n, c0, 0, False)
                mix1_vector(s, m1, mark1, w, base, FC, n + 1, layer)
                ffn_vector(s, w, base, FC + MIX1_SLOTS, n + 2, c0 + FC, 2, True)
            dve.wait_ge(s.gain_loaded, 16)
            final_norm(s, "vector", 3 * LAYERS)
            dve.wait_ge(s.x_ready, 4 * X2 + 4)
            dve.wait_ge(s.consts_loaded, 16 * CONSTS1)
            with dve.Fori(0, LAYERS) as layer:
                base, n = layer * SLOTS2 + SLOTS2_AT, 3 * layer + 3 * LAYERS
                c0 = 2 * FC * layer + 2 * FC * LAYERS
                nc.vector.tensor_copy(s.par[:, 0:PAR], s.par2_all[:, layer]).then_inc(par_ready, 1)
                dve.wait_ge(par_ready, layer + LAYERS + 1)
                norm_start(s, n)
                ffn_vector(s, w, base, 0, n, c0, 0, False)
                mix2_vector(s, m2, mark2, w, base, FC, n + 1, layer)
                ffn_vector(s, w, base, FC + MIX2_SLOTS, n + 2, c0 + FC, 2, True)

        @block.tensor
        def _(pe):
            pe.wait_ge(inputs_loaded, 16 * len(loads))
            pe.sem_inc(w.used[0], 4)
            pe.sem_inc(w.used[1], 2)
            with pe.Fori(0, LAYERS) as layer:
                base, n, c0 = layer * SLOTS1, 3 * layer, 2 * FC * layer
                ffn_tensor(s, w, base, 0, n, c0)
                mix1_tensor(s, m1, mark1, w, base, FC, n + 1, layer)
                ffn_tensor(s, w, base, FC + MIX1_SLOTS, n + 2, c0 + FC)
            with pe.Fori(0, LAYERS) as layer:
                base, n = layer * SLOTS2 + SLOTS2_AT, 3 * layer + 3 * LAYERS
                c0 = 2 * FC * layer + 2 * FC * LAYERS
                ffn_tensor(s, w, base, 0, n, c0)
                mix2_tensor(s, m2, mark2, w, base, FC, n + 1, layer)
                ffn_tensor(s, w, base, FC + MIX2_SLOTS, n + 2, c0 + FC)
        mark1.check()
        mark2.check()



def columns(mat):
    rows, cols = mat.shape
    return [mat[:, c * P:(c + 1) * P].reshape(rows // P, P, P).transpose(1, 0, 2).reshape(P, rows)
            for c in range(cols // P)]


def wide(mat):
    return [mat[2 * j * P:(2 * j + 2) * P].reshape(2, P, HALF).transpose(1, 0, 2).reshape(P, CH)
            for j in range(KD // 2)]


def row_chunks(mat):
    return [mat[k * P:(k + 1) * P] for k in range(mat.shape[0] // P)]


def ffn_chunks(w_in, w_out):
    gate, up, down = columns(w_in[:, :DFF]), columns(w_in[:, DFF:]), row_chunks(w_out)
    return [x for three in zip(gate, up, down) for x in three]


def side_by_side(a, b):
    return [np.concatenate(two, axis=1) for two in zip(a, b)]


def mix1_chunks(w_in, na_out, f_out, w_o):
    q, k, v, u, ga, gf = np.split(w_in, [512, 1024, 1536, 2048, 3072], axis=1)
    gates = [x for two in zip(columns(ga), columns(gf)) for x in two]
    return (wide(v) + wide(u) + columns(q) + columns(k) + gates
            + side_by_side(columns(na_out), columns(f_out)) + row_chunks(w_o))


def per_partition(vec):
    return vec.reshape(KD, P).T


def relative_bias(rpb):
    t = np.arange(T)
    r, c = t // GRID_W, t % GRID_W
    start = np.clip(c - NA_COLS // 2, 0, GRID_W - NA_COLS)
    inside = (c[None, :] >= start[:, None]) & (c[None, :] < start[:, None] + NA_COLS)
    dr = r[None, :] - r[:, None] + NA_ROWS - 1
    dc = np.clip(c[None, :] - c[:, None], 1 - NA_COLS, NA_COLS - 1) + NA_COLS - 1
    out = np.where(inside[None], rpb[:, dr, dc], np.float32(MASKED))
    return out.reshape(NA_HEADS, TT, P, T).transpose(2, 1, 0, 3)


def dft_constants():
    t = np.arange(T)
    ang_t = 2 * np.pi * ((t[:, None] * t[None, :]) % T) / T
    time = np.concatenate([np.cos(ang_t), np.sin(ang_t)], axis=1).reshape(TT, P, 2 * T)
    c = np.arange(F_DIM)
    ang_c = 2 * np.pi * ((c[:, None] * c[None, :]) % F_DIM) / F_DIM
    chan = np.stack([np.cos(ang_c), -np.sin(ang_c)], axis=1) / np.sqrt(T * F_DIM)
    return time.transpose(1, 0, 2).astype(np.float32), chan.astype(np.float32)


def mix2_chunks(w_in, w_gate, w1, br_a, br_b, br_c, w_out):
    widths = (256, 256, 256, 512, 128, 128, 128, 128, 128, 128, 24, 256, 64, 64, 256, 32, 8)
    (sb_q, sb_k, sb_v, nq, nkc, nvc, nks, nvs, nkw, nvw, ngate, dq, dk, dv, iq, ik, iw) = np.split(
        w_in, np.cumsum(widths)[:-1], axis=1)

    def cat(*parts):
        return np.concatenate(parts, axis=1)

    rest = cat(dk, nvw)
    width = rest.shape[1]
    rest = rest.reshape(2, 4, P, width).transpose(0, 2, 1, 3).reshape(2, P, 4 * width)
    comp = w1.reshape(2, 2, 8, P, P).transpose(0, 1, 3, 2, 4).reshape(4, P, CH)
    gates = [columns(part) for part in np.split(w_gate, 3, axis=1)]
    gates = [gates[g % 3][g // 3] for g in range(3 * KD)]
    out = [np.concatenate(three, axis=1) for three in zip(columns(br_a), columns(br_b), columns(br_c))]
    ys = []
    for c in range(KD):
        if c >= GATES_LATE_C:
            ys += gates[3 * c:3 * c + 3]
        ys.append(out[c])
    return (columns(sb_q) + columns(sb_k) + wide(cat(sb_v, nkc, nvc))
            + wide(cat(iq, ik, iw, ngate, nvs, dv)) + wide(nq) + wide(cat(dq, nks, nkw))
            + list(rest) + gates[:4] + list(comp) + gates[4:GATES_EARLY] + ys + row_chunks(w_out))


def mixer_params(q_norm, k_norm, dsa_q, dsa_k, w2, pe):
    gains = np.concatenate([q_norm] * NSA_HEADS + [dsa_q] * DSA_HEADS + [k_norm[1]] * NSA_GROUPS
                           + [k_norm[2]] * NSA_GROUPS + [dsa_k, k_norm[0]])
    pos = pe.reshape(2, CMP_LEN // 2, P).transpose(2, 0, 1).reshape(P, CMP_LEN)
    return np.concatenate([np.tile(gains, (P, 1)), w2[0], w2[1], pos], axis=1)


def rope_table(pos, rot):
    inv = np.float32(500000.0) ** (-np.arange(0, rot, 2, dtype=np.float32) / np.float32(rot))
    ang = pos.astype(np.float32)[:, None] * inv[None, :]
    return np.stack([np.cos(ang), np.sin(ang)], axis=1)


def block2_constants():
    t, p = np.arange(T), np.arange(P)
    off = np.float32(MASKED)

    def tiles(x):
        return x.reshape((TT, P) + x.shape[1:]).swapaxes(0, 1)

    def mask(ok):
        return np.where(ok, np.float32(0), off)

    ends = np.arange(CB) * CMP_STRIDE + CMP_LEN - 1
    sb = mask(t[:, None] < t[None, :])
    return dict(
        causal=tiles(mask(t[None, :] <= t[:, None])),
        sbmask=np.concatenate([sb[:P], sb[P:, P:]], axis=1),
        tri=np.stack([-(p[:, None] >= p[None, :]).astype(np.float32), -np.ones((P, P))], axis=1),
        cmask=tiles(mask((ends[None, :] <= t[:, None]) & (np.arange(CB) < NCMP)[None, :])),
        hmask=(p[:, None] // CB == np.arange(NSA_HEADS)[None, :]),
        rope=tiles(rope_table(t, DH // 4)), ropei=tiles(rope_table(t, IDX_DIM // 4)),
        ropec=np.tile(rope_table(ends, DH // 4), (NSA_GROUPS, 1, 1)))


def kernel(**inputs):
    import concourse.bacc as bacc
    from concourse.bass_utils import run_bass_kernel_spmd

    x = {name: np.asarray(value) for name, value in inputs.items()}
    stream = np.zeros((LAYERS * (SLOTS1 + SLOTS2) + 1, P, SLOT), np.float32)
    chunks = []
    for l in range(LAYERS):
        chunks += ffn_chunks(x["ffn1_w_in"][l], x["ffn1_w_out"][l])
        chunks += mix1_chunks(x["mix_w_in"][l], x["na_w_out"][l], x["f_w_out"][l], x["mix_w_o"][l])
        chunks += ffn_chunks(x["ffn2_w_in"][l], x["ffn2_w_out"][l])
    for l in range(LAYERS):
        chunks += ffn_chunks(x["ffn1_w_gu_2"][l], x["ffn1_w_down_2"][l])
        chunks += mix2_chunks(x["w_in_2"][l], x["w_gate_2"][l], x["nsa_cmp_w1_2"][l],
                              x["w_br_a_2"][l], x["w_br_b_2"][l], x["w_br_c_2"][l], x["w_out_2"][l])
        chunks += ffn_chunks(x["ffn2_w_gu_2"][l], x["ffn2_w_down_2"][l])
    assert len(chunks) == 3 * LAYERS * (SLOTS1 + SLOTS2)
    for n, chunk in enumerate(chunks):
        stream[n // 3, :, n % 3 * CH:n % 3 * CH + chunk.shape[1]] = chunk
    dft_t, dft_c = dft_constants()
    arrays = dict(
        stream=stream, x=x["x"][0], ident=np.eye(P), dft_t=dft_t, dft_c=dft_c,
        params1=np.stack([np.concatenate(
            [per_partition(x[k][l]) for k in ("ffn1_norm", "mix_norm", "ffn2_norm")]
            + [per_partition(x["mix_gate_bias"][l, j]) for j in range(2)], axis=1)
            for l in range(LAYERS)], axis=1),
        gains2=np.stack([np.concatenate(
            [per_partition(x[k][l]) for k in ("ffn1_norm_2", "mix_norm_2", "ffn2_norm_2")], axis=1)
            for l in range(LAYERS)], axis=1),
        rel_bias=np.stack([relative_bias(x["na_rpb"][l]) for l in range(LAYERS)]),
        final_gain=np.tile(x["final_norm"], (P, 1)),
        params2=np.stack([mixer_params(
            x["nsa_q_norm_2"][l], x["nsa_k_norm_2"][l], x["dsa_q_norm_2"][l], x["dsa_k_norm_2"][l],
            x["nsa_cmp_w2_2"][l], x["nsa_cmp_pe_2"][l]) for l in range(LAYERS)]),
        **block2_constants())
    arrays = {"in_" + k: np.ascontiguousarray(v, dtype=np.float32) for k, v in arrays.items()}

    nc = bacc.Bacc("TRN2", target_bir_lowering=False, num_devices=1)
    aps = {k[3:]: nc.dram_tensor(k, v.shape, F32, kind="ExternalInput").ap()
           for k, v in arrays.items()}
    aps["out"] = nc.dram_tensor("out", (T, D), F32, kind="ExternalOutput").ap()
    build(nc, aps)
    results = run_bass_kernel_spmd(nc, [arrays], core_ids=[0])
    return results.results[0]["out"].reshape(x["x"].shape)
```

```python
from contextlib import ExitStack

import numpy as np
from concourse import mybir

F32 = mybir.dt.float32
F32R = mybir.dt.float32r
ACT = mybir.ActivationFunctionType
ALU = mybir.AluOpType
AX = mybir.AxisListType

P = 128
D = 1024
KD = D // P
T = 256
TT = T // P
DFF = 2816
FC = DFF // P
LAYERS = 2
HALF = 512
CH = 1024
SLOT = 3 * CH
EPS = 1e-6
MASKED = -1.0e30

NA_HEADS, DH = 8, 64
NA_W = NA_HEADS * DH
F_GROUPS, F_DIM = 4, 128
GRID_W, NA_ROWS, NA_COLS = 64, 8, 16
SCALE = DH ** -0.5
PAIRS = NA_HEADS // 2
MIX1_SLOTS = 16
SB_HEADS, NSA_HEADS, NSA_GROUPS, DSA_HEADS = 4, 8, 2, 4
IDX_HEADS, IDX_DIM, TOPK = 8, 32, 64
CMP_LEN, CMP_STRIDE = 32, 16
NCMP = T // CMP_STRIDE - CMP_LEN // CMP_STRIDE + 1
CB = 16
MIX2_SLOTS = 22


class Stream:

    def __init__(self, nc, sb, sem, dram):
        self.nc, self.dram = nc, dram
        self.raw = [sb("w_raw_front", [P, 2, 2 * CH], F32), sb("w_raw_back", [P, 2, CH], F32)]
        self.hi = [sb("w_hi_front", [P, 2, 2 * CH], F32R), sb("w_hi_back", [P, 2, CH], F32R)]
        self.lo = [sb("w_lo_front", [P, 2, 2 * CH], F32R), sb("w_lo_back", [P, 2, CH], F32R)]
        self.loaded = [[sem(f"w_{part}_loaded{i}") for i in range(2)] for part in ("front", "back")]
        self.hi_done = [sem("w_front_hi"), sem("w_back_hi")]
        self.split = [sem("w_front_split"), sem("w_back_split")]
        self.used = [sem("w_front_used"), sem("w_back_used")]

    def load(self, sp, part, slot, parity):
        sp.wait_ge(self.split[part], slot + 1)
        at = slice(0, 2 * CH) if part == 0 else slice(2 * CH, SLOT)
        sp.dma_start(self.raw[part][:, parity], self.dram[slot][:, at]).then_inc(
            self.loaded[part][parity], 16)

    def load_slots(self, sp, first, count):
        with sp.Fori(0, count // 2) as i:
            for k in range(2):
                self.load(sp, 0, first + 2 * i + k + 1, 1 - k)
                self.load(sp, 1, first + 2 * i + k, k)

    def round_hi(self, act, part, base, slot):
        parity = slot % 2
        act.wait_ge(self.loaded[part][parity], 8 * (base + slot - parity) + 16)
        act.wait_ge(self.used[part], (base + slot) * (2 - part) + 2 - part)
        self.nc.scalar.copy(self.hi[part][:, parity], self.raw[part][:, parity]).then_inc(
            self.hi_done[part], 1)

    def feed(self, act, base, slot):
        self.round_hi(act, 0, base, slot + 1)
        self.round_hi(act, 1, base, slot)

    def rest(self, eng, part, slot, parity):
        eng.wait_ge(self.hi_done[part], slot + 1)
        if part == 1:
            eng.wait_ge(self.split[1], slot + 2)
        eng.tensor_tensor(
            self.lo[part][:, parity], self.raw[part][:, parity],
            self.hi[part][:, parity].bitcast(F32), ALU.subtract).then_inc(self.split[part], 1)

    def split_slots(self, pool, first, count, backs):
        with pool.Fori(0, count // 2) as i:
            for k in range(2):
                self.rest(pool, 0, first + 2 * i + k + 1, 1 - k)
                if backs:
                    self.rest(pool, 1, first + 2 * i + k, k)

    def chunk(self, pe, base, slot, c):
        part = c // 2
        if c != 1:
            pe.wait_ge(self.split[part], base + slot + 3)
        at = slice((c % 2) * CH, (c % 2) * CH + CH)
        return self.hi[part][:, slot % 2, at], self.lo[part][:, slot % 2, at]

    def taken(self, last, c):
        last.then_inc(self.used[c // 2], 1)

    def wait_taken(self, eng, base, slot, c):
        if c == 2:
            eng.wait_ge(self.used[1], base + slot + 3)
        else:
            eng.wait_ge(self.used[0], (base + slot) * 2 + 4 + c + 1)


class State:
    pass


class Marks:

    def __init__(self, sem, prefix, totals):
        self.sem = {name: sem(prefix + name) for name in totals}
        self.totals = totals
        self.made = {name: 0 for name in totals}

    def inc(self, instruction, name):
        self.made[name] += 1
        instruction.then_inc(self.sem[name], 1)

    def need(self, eng, layer, name, k):
        eng.wait_ge(self.sem[name], layer * self.totals[name] + k)

    def check(self):
        assert self.made == self.totals, {
            n: (self.made[n], self.totals[n]) for n in self.totals if self.made[n] != self.totals[n]}


def product(nc, out, a, b, start, stop):
    (ah, al), (bh, bl) = a, b
    nc.tensor.matmul(out, ah, bl, start=start, stop=False)
    nc.tensor.matmul(out, al, bh, start=False, stop=False)
    return nc.tensor.matmul(out, ah, bh, start=False, stop=stop)


def shared_state(nc, sb, ps, sem):
    s = State()
    s.nc = nc
    s.x = sb("x", [P, TT, D], F32)
    s.squares = sb("squares", [P, TT, D], F32)
    s.ss = sb("sum_sq", [P, TT, 2], F32)
    s.ms = sb("mean_sq", [P, TT], F32)
    s.rms = sb("rms", [P, TT], F32)
    s.inv = sb("inv_rms", [P, TT], F32)
    s.scrap = sb("scrap", [P, 2], F32)
    s.xlh = sb("xt_lo_hi", [P, KD, 2, T], F32R)
    s.xl, s.xh = s.xlh[:, :, 0], s.xlh[:, :, 1]
    s.act = sb("silu_gate", [P, 2, T], F32)
    s.hid = sb("hidden", [P, 2, T], F32)
    s.diag = s.hid[:, :, 0:P]
    s.hh = sb("hidden_hi", [P, 2, T], F32R)
    s.hl = sb("hidden_lo", [P, 2, T], F32R)
    s.ident = sb("identity", [P, P], F32)
    s.pj = [ps(f"ps_proj{i}", [P, HALF], F32) for i in range(2)]
    s.py = [ps(f"ps_y{i}", [P, HALF], F32) for i in range(4)]
    s.pa = [ps(f"ps_aux{i}", [P, HALF], F32) for i in range(2)]
    s.x_ready = sem("x_ready")
    s.sum_sq_ready = sem("sum_sq_ready")
    s.mean_sq_ready = sem("mean_sq_ready")
    s.rms_ready = sem("rms_ready")
    s.inv_ready = sem("inv_ready")
    s.diag_ready = sem("diag_ready")
    s.table_in = sem("table_in")
    s.y_tile = sem("y_tile")
    s.xt_banks = sem("xt_banks")
    s.xh_ready = sem("xh_ready")
    s.xl_ready = sem("xl_ready")
    s.gate_summed = sem("gate_summed")
    s.up_summed = sem("up_summed")
    s.silu_done = sem("silu_done")
    s.hid_done = sem("hid_done")
    s.hh_done = sem("hh_done")
    s.h_ready = sem("h_ready")
    return s



def norm_banks(s):
    return s.pj[0], s.pa[0], s.pa[1], s.pj[1]


def fetch_table(s, n, func, k):
    s.nc.scalar.wait_ge(s.table_in, 2 * n + k + 1)
    s.nc.scalar.activation(s.scrap[:, 0:1], s.scrap[:, 1:2], func).then_inc(s.table_in, 1)


def roots(s, n):
    nc, act = s.nc, s.nc.scalar
    for i in range(TT):
        for half in range(2):
            act.wait_ge(s.x_ready, 4 * n + 2 * i + half + 1)
            cols = slice(half * HALF, (half + 1) * HALF)
            nc.scalar.activation(s.squares[:, i, cols], s.x[:, i, cols], ACT.Square,
                                 accum_out=s.ss[:, i, half:half + 1]).then_inc(s.sum_sq_ready, 1)
        act.wait_ge(s.mean_sq_ready, 2 * n + i + 1)
        act.wait_ge(s.sum_sq_ready, 4 * n + 2 * i + 2)
        nc.scalar.activation(s.rms[:, i:i + 1], s.ss[:, i, 1:2], ACT.Sqrt, bias=s.ms[:, i:i + 1],
                             scale=1.0 / D).then_inc(s.rms_ready, 1)


def norm_scalar(s, w, base, slot0, n, g, then):
    nc, act = s.nc, s.nc.scalar
    fetch_table(s, n, ACT.Sqrt, 1)
    w.feed(act, base, slot0)
    roots(s, n)
    fetch_table(s, n, then, 2)
    for k in range(KD):
        if k % 2 == 0:
            act.wait_ge(s.xt_banks, 4 * n + k // 2 + 1)
        bank = norm_banks(s)[k // 2][:, (k % 2) * T:(k % 2 + 1) * T]
        nc.scalar.activation(s.xh[:, k], bank, ACT.Copy,
                             scale=s.par[:, g * KD + k:g * KD + k + 1]).then_inc(s.xh_ready, 1)


def first_mean(s, n, i):
    s.nc.vector.wait_ge(s.sum_sq_ready, 4 * n + 2 * i + 1)
    s.nc.vector.tensor_scalar(s.ms[:, i:i + 1], s.ss[:, i, 0:1], 1.0 / D, EPS, ALU.mult,
                              ALU.add).then_inc(s.mean_sq_ready, 1)


def inverse(s, n, i):
    s.nc.vector.wait_ge(s.rms_ready, 2 * n + i + 1)
    s.nc.vector.reciprocal(s.inv[:, i:i + 1], s.rms[:, i:i + 1]).then_inc(s.inv_ready, 1)
    s.nc.vector.wait_ge(s.inv_ready, 2 * n + i + 1)


def diagonal(s, n, i):
    inverse(s, n, i)
    s.nc.vector.tensor_scalar(s.diag[:, i], s.ident[:], s.inv[:, i:i + 1], None,
                              ALU.mult).then_inc(s.diag_ready, 1)


def norm_rest(s, n, g):
    nc, dve = s.nc, s.nc.vector
    for k in range(KD):
        if k % 2 == 0:
            dve.wait_ge(s.xh_ready, 8 * n + k + 2)
        bank = norm_banks(s)[k // 2][:, (k % 2) * T:(k % 2 + 1) * T]
        nc.vector.scalar_tensor_tensor(s.xl[:, k], bank, s.par[:, g * KD + k:g * KD + k + 1],
                                       s.xh[:, k].bitcast(F32), ALU.mult, ALU.subtract).then_inc(
            s.xl_ready, 1)


def norm_start(s, n):
    for i in range(TT):
        first_mean(s, n, i)
        diagonal(s, n, i)


def norm_tensor(s, n):
    nc, pe = s.nc, s.nc.tensor
    for i in range(TT):
        pe.wait_ge(s.diag_ready, 2 * n + i + 1)
        for k in range(KD):
            at = (k % 2) * T + i * P
            last = nc.tensor.matmul(norm_banks(s)[k // 2][:, at:at + P],
                                    s.x[:, i, k * P:(k + 1) * P], s.diag[:, i])
            if i == TT - 1 and k % 2 == 1:
                last.then_inc(s.xt_banks, 1)


def wait_normed(s, n, k):
    s.nc.tensor.wait_ge(s.xl_ready, 8 * n + max(k + 1, 2))



def ffn_up(s, w, base, slot, n, first=False):
    nc, pe = s.nc, s.nc.tensor
    for c in range(2):
        hi, lo = w.chunk(pe, base, slot, c)
        bank = (s.pj, s.pa)[c][slot % 2]
        for k in range(KD):
            if first and c == 0:
                wait_normed(s, n, k)
            cols = slice(k * P, (k + 1) * P)

            def by_hi():
                return nc.tensor.matmul(bank[:], hi[:, cols],
                                        s.xlh[:, k].rearrange("p j t -> p (j t)"),
                                        start=k == 0, stop=k == KD - 1)

            if k == 0:
                by_hi()
            last = nc.tensor.matmul(bank[:, 0:T], lo[:, cols], s.xh[:, k], start=False, stop=False)
            if k > 0:
                last = by_hi()
        w.taken(last, c)


def ffn_down(s, w, base, slot, h_count, start=False, stop=False):
    nc, pe = s.nc, s.nc.tensor
    hi, lo = w.chunk(pe, base, slot, 2)
    pe.wait_ge(s.h_ready, h_count)
    par = slot % 2
    for i in range(TT):
        toks = slice(i * P, (i + 1) * P)
        for half in range(2):
            cols = slice(half * HALF, (half + 1) * HALF)
            last = product(nc, s.py[2 * i + half][:], (s.hh[:, par, toks], s.hl[:, par, toks]),
                           (hi[:, cols], lo[:, cols]), start, stop)
        if stop and i == 0:
            last.then_inc(s.y_tile, 1)
    w.taken(last, 2)


def ffn_tensor(s, w, base, slot0, n, c0):
    norm_tensor(s, n)
    ffn_up(s, w, base, slot0, n, first=True)
    ffn_up(s, w, base, slot0 + 1, n)
    ffn_down(s, w, base, slot0, c0 + 1, start=True)
    with s.nc.tensor.Fori(1, FC // 2) as g:
        for k in range(2):
            ffn_up(s, w, base + 2 * g, slot0 + k, n)
            ffn_down(s, w, base + 2 * g, slot0 + k - 1, c0 + 2 * g + k)
    ffn_down(s, w, base, slot0 + FC - 1, c0 + FC, stop=True)


def ffn_scalar(s, w, base, slot0, n, c0, g):
    nc, act = s.nc, s.nc.scalar

    def silu(before, slot):
        s_done = c0 + before + slot - slot0 + 1
        act.wait_ge(s.gate_summed, s_done)
        at = s.act[:, slot % 2]
        nc.scalar.activation(at, at, ACT.Silu).then_inc(s.silu_done, 1)

    norm_scalar(s, w, base, slot0, n, g, ACT.Silu)
    silu(0, slot0)
    w.feed(act, base, slot0 + 1)
    with act.Fori(0, FC // 2 - 1) as i:
        for k in (1, 2):
            silu(2 * i, slot0 + k)
            w.feed(act, base + 2 * i, slot0 + k + 1)
    silu(0, slot0 + FC - 1)


def ffn_vector(s, w, base, slot0, n, c0, g, last):
    nc, dve = s.nc, s.nc.vector
    norm_rest(s, n, g)
    with dve.Fori(0, FC // 2) as i:
        for k in range(2):
            done = c0 + 2 * i + k + 1
            w.rest(nc.vector, 1, base + slot0 + 2 * i + k, k)
            gate, up = (x[k][:].rearrange("p (j t) -> p t j", j=2) for x in (s.pj, s.pa))
            w.wait_taken(dve, base + 2 * i, slot0 + k, 0)
            nc.vector.tensor_reduce(s.act[:, k], gate, AX.X, ALU.add).then_inc(s.gate_summed, 1)
            w.wait_taken(dve, base + 2 * i, slot0 + k, 1)
            nc.vector.tensor_reduce(s.hid[:, k], up, AX.X, ALU.add).then_inc(s.up_summed, 1)
            dve.wait_ge(s.up_summed, done)
            dve.wait_ge(s.silu_done, done)
            nc.vector.tensor_tensor(s.hid[:, k], s.act[:, k], s.hid[:, k],
                                    ALU.mult).then_inc(s.hid_done, 1)
            dve.wait_ge(s.hid_done, done)
            nc.vector.tensor_copy(s.hh[:, k], s.hid[:, k]).then_inc(s.hh_done, 1)
            dve.wait_ge(s.hh_done, done)
            nc.vector.tensor_tensor(s.hl[:, k], s.hid[:, k], s.hh[:, k].bitcast(F32),
                                    ALU.subtract).then_inc(s.h_ready, 1)
    finish(s, w, base, slot0 + FC - 1, 2, n, 0.5, None if last else n + 1)


def finish(s, w, base, slot, c, n, factor, n_next):
    nc, dve = s.nc, s.nc.vector

    def add(i, half):
        xs = s.x[:, i, half * HALF:(half + 1) * HALF]
        nc.vector.scalar_tensor_tensor(xs, s.py[2 * i + half][:], factor, xs, ALU.mult,
                                       ALU.add).then_inc(s.x_ready, 1)

    dve.wait_ge(s.y_tile, n + 1)
    add(0, 0)
    add(0, 1)
    w.wait_taken(dve, base, slot, c)
    add(1, 0)
    if n_next is not None:
        first_mean(s, n_next, 0)
        diagonal(s, n_next, 0)
    add(1, 1)
    if n_next is not None:
        first_mean(s, n_next, 1)
        diagonal(s, n_next, 1)


Q_V, Q_U, Q_Q, Q_K, Q_GATE, Q_Y, Q_O = 0, 4, 8, 12, 16, 32, 40
JOBS1 = PAIRS * TT

MIX1_TOTALS = dict(
    v_ready=2, u_ready=2, q_ready=4, k_ready=4, dft1_done=4, dft1_ready=4, dft2_done=4,
    dft_hi=4, dft_ready=4, gate_ready=16, scores_done=JOBS1, biased=JOBS1, max_ready=JOBS1,
    exp_ready=2 * JOBS1, inv_sum=JOBS1, probs_ready=JOBS1, probsT_done=JOBS1,
    probsT_ready=JOBS1, pv_done=JOBS1, o_hi=JOBS1, o_ready=JOBS1, sigmoid_ready=16, gated=8,
    summed=8, m_hi=8, m_ready=8)


def mix1_state(sb):
    u = sb("m1_u", [P, TT, NA_W], F32)
    v = sb("m1_v", [P, TT, NA_W], F32)
    m = State()
    m.qT = sb("m1_qT", [P, PAIRS, T], F32)
    m.kbd = sb("m1_k_block", [P, PAIRS, 2, T], F32)
    m.v = v
    m.u = u
    m.dft_t = sb("m1_dft_time", [P, TT, 2 * T], F32)
    m.dft_c = sb("m1_dft_chan", [P, 2, P], F32)
    m.a = sb("m1_dft_a", [P, F_GROUPS, 2 * T], F32)
    m.fh = sb("m1_fourier_hi", [P, F_GROUPS, T], F32R)
    m.fl = sb("m1_fourier_lo", [P, F_GROUPS, T], F32R)
    m.oh = sb("m1_attn_hi", [P, PAIRS, T], F32R)
    m.ol = sb("m1_attn_lo", [P, PAIRS, T], F32R)
    m.gate = sb("m1_gates", [P, KD, 2, T], F32)
    m.bias = sb("m1_rel_bias", [P, TT, NA_HEADS, T], F32)
    m.sc = sb("m1_scores", [P, 2, 2, T], F32)
    m.pT = sb("m1_probsT", [P, 2, 4, P], F32)
    m.nmax = sb("m1_neg_max", [P, 2, 2], F32)
    m.sum = sb("m1_exp_sum", [P, 2, 2], F32)
    m.inv = sb("m1_inv_exp_sum", [P, 2, 2], F32)
    m.gy = u[:, :].rearrange("p b (j t) -> p b j t", j=2)
    m.m = v[:, 0].rearrange("p (b t) -> p b t", b=2)
    return m


def project(s, w, base, slot0, q, out, n=None):
    hi, lo = w.chunk(s.nc.tensor, base, slot0 + q // 3, q % 3)
    for k in range(KD):
        if n is not None:
            wait_normed(s, n, k)
        cols = slice(k * P, (k + 1) * P)
        last = product(s.nc, out, (hi[:, cols], lo[:, cols]), (s.xh[:, k], s.xl[:, k]),
                       k == 0, k == KD - 1)
    w.taken(last, q % 3)


def project_wide(s, w, base, slot0, q0, banks, n=None):
    for j in range(KD // 2):
        q = q0 + j
        hi, lo = w.chunk(s.nc.tensor, base, slot0 + q // 3, q % 3)
        for kk in range(2):
            k, cols = 2 * j + kk, slice(kk * HALF, (kk + 1) * HALF)
            if n is not None:
                wait_normed(s, n, k)
            for i in range(TT):
                toks = slice(i * P, (i + 1) * P)
                last = product(s.nc, banks[i][:], (s.xh[:, k, toks], s.xl[:, k, toks]),
                               (hi[:, cols], lo[:, cols]), k == 0, k == KD - 1)
        w.taken(last, q % 3)


def project_out(s, merged_hi, merged_lo, w, base, slot0, q0, mark, layer):
    pe = s.nc.tensor
    for k in range(KD):
        q = q0 + k
        hi, lo = w.chunk(pe, base, slot0 + q // 3, q % 3)
        mark.need(pe, layer, "m_ready", k + 1)
        for i in range(TT):
            toks = slice(i * P, (i + 1) * P)
            for half in range(2):
                cols = slice(half * HALF, (half + 1) * HALF)
                last = product(s.nc, s.py[2 * i + half][:], (merged_hi[:, k, toks], merged_lo[:, k, toks]),
                               (hi[:, cols], lo[:, cols]), k == 0, k == KD - 1)
            if k == KD - 1 and i == 0:
                last.then_inc(s.y_tile, 1)
        w.taken(last, q % 3)


def mix1_tensor(s, m, mark, w, base, slot0, n, layer):
    nc, pe = s.nc, s.nc.tensor

    def need(name, k):
        mark.need(pe, layer, name, k)

    norm_tensor(s, n)
    project_wide(s, w, base, slot0, Q_V, s.py[0:2], n)
    project_wide(s, w, base, slot0, Q_U, s.py[2:4])
    for j in range(8):
        if j >= 6:
            need("k_ready", j - 5)
        elif j >= 2:
            need("q_ready", j - 1)
        project(s, w, base, slot0, Q_Q + j, s.pj[j % 2][:, 0:T])
    need("u_ready", 2)
    pe.wait_ge(s.consts_loaded, 16 * CONSTS1)
    for g in range(F_GROUPS):
        if g >= 2:
            need("dft1_ready", g - 1)
        for i in range(TT):
            last = nc.tensor.matmul(s.pa[g % 2][:], m.u[:, i, g * F_DIM:(g + 1) * F_DIM],
                                    m.dft_t[:, i], start=i == 0, stop=i == TT - 1)
        mark.inc(last, "dft1_done")
    for g in range(F_GROUPS):
        need("dft1_ready", min(g + 3, F_GROUPS))
        if g >= 2:
            need("dft_ready", g - 1)
        out = s.pa[g % 2][:, 0:T]
        nc.tensor.matmul(out, m.dft_c[:, 0], m.a[:, g, 0:T], start=True, stop=False)
        mark.inc(nc.tensor.matmul(out, m.dft_c[:, 1], m.a[:, g, T:2 * T], start=False, stop=True),
                 "dft2_done")
    need("q_ready", 4)
    for job in range(JOBS1 + 1):
        if job < JOBS1:
            pair, i = divmod(job, TT)
            if job == 0:
                need("v_ready", 2)
                need("k_ready", 4)
            if job >= 2:
                need("biased", job - 1)
            mark.inc(nc.tensor.matmul(s.py[job % 2][:], m.qT[:, pair, i * P:(i + 1) * P],
                                      m.kbd[:, pair].rearrange("p e t -> p (e t)")), "scores_done")
            if job >= 1:
                need("gate_ready", 2 * job - 1)
            project(s, w, base, slot0, Q_GATE + 2 * job, s.pj[0][:, 0:T])
        if job >= 1:
            b = (job - 1) % 2
            need("probs_ready", job)
            if job >= 3:
                need("probsT_ready", job - 2)
            for e in range(2):
                for kc in range(TT):
                    last = nc.tensor.transpose(s.py[2 + b][:, (e * 2 + kc) * P:(e * 2 + kc + 1) * P],
                                               m.sc[:, b, e, kc * P:(kc + 1) * P], s.ident[:])
            mark.inc(last, "probsT_done")
        if job < JOBS1:
            if job >= 1:
                need("gate_ready", 2 * job)
            project(s, w, base, slot0, Q_GATE + 2 * job + 1, s.pj[1][:, 0:T])
        if job >= 1:
            pair = (job - 1) // TT
            need("probsT_ready", job)
            if job >= 3:
                need("o_ready", job - 2)
            elif job == 1:
                need("dft_ready", 4)
            for e in range(2):
                head = 2 * pair + e
                for kc in range(TT):
                    last = nc.tensor.matmul(s.pa[b][e * DH:(e + 1) * DH, 0:P],
                                            m.v[:, kc, head * DH:(head + 1) * DH],
                                            m.pT[:, b, e * 2 + kc], start=kc == 0, stop=kc == TT - 1)
            mark.inc(last, "pv_done")
    for c in range(KD):
        q = Q_Y + c
        if c < 2:
            need("gate_ready", 15 + c)
        else:
            need("gated", c - 1)
        hi, lo = w.chunk(pe, base, slot0 + q // 3, q % 3)
        for j, h_, l_ in ((1, m.fh, m.fl), (0, m.oh, m.ol)):
            for k in range(PAIRS):
                if c == 0 and j == 0:
                    need("o_ready", TT * (k + 1))
                cols = slice((j * PAIRS + k) * P, (j * PAIRS + k + 1) * P)
                last = product(nc, s.pj[c % 2][:, j * T:(j + 1) * T], (hi[:, cols], lo[:, cols]),
                               (h_[:, k], l_[:, k]), k == 0, k == PAIRS - 1)
        w.taken(last, q % 3)
    project_out(s, s.xh, s.xl, w, base, slot0, Q_O, mark, layer)


def mix1_scalar(s, m, mark, w, base, slot0, n, layer):
    nc, act = s.nc, s.nc.scalar

    def need(name, k):
        mark.need(act, layer, name, k)

    def feed(q):
        if q % 3 == 2 and q // 3 + 1 < MIX1_SLOTS:
            w.feed(act, base, slot0 + q // 3 + 1)

    norm_scalar(s, w, base, slot0, n, 1, ACT.Exp)
    for q0, dest, banks, name in ((Q_V, m.v, s.py[0:2], "v_ready"), (Q_U, m.u, s.py[2:4], "u_ready")):
        for q in range(q0, q0 + 4):
            feed(q)
        w.wait_taken(act, base, slot0 + (q0 + 3) // 3, (q0 + 3) % 3)
        for i in range(TT):
            mark.inc(nc.scalar.copy(dest[:, i], banks[i][:]), name)
    for q in range(Q_Q, Q_K):
        feed(q)
    for j in range(PAIRS):
        q = Q_K + j
        feed(q)
        w.wait_taken(act, base, slot0 + q // 3, q % 3)
        for e in range(2):
            rows = slice(e * DH, (e + 1) * DH)
            last = nc.scalar.copy(m.kbd[rows, j, e], s.pj[j % 2][rows, 0:T])
        mark.inc(last, "k_ready")
    for g in range(F_GROUPS):
        need("dft1_done", g + 1)
        mark.inc(nc.scalar.copy(m.a[:, g], s.pa[g % 2][:]), "dft1_ready")

    def gate(idx):
        q = Q_GATE + idx
        feed(q)
        w.wait_taken(act, base, slot0 + q // 3, q % 3)
        mark.inc(nc.scalar.copy(m.gate[:, idx // 2, idx % 2], s.pj[idx % 2][:, 0:T]), "gate_ready")

    def sigmoid(c):
        for j in range(2):
            need("gate_ready", 2 * c + j + 1)
            col = 3 * KD + j * KD + c
            mark.inc(nc.scalar.activation(m.gate[:, c, j], m.gate[:, c, j], ACT.Sigmoid,
                                          bias=s.par[:, col:col + 1]), "sigmoid_ready")

    for job in range(JOBS1 + 1):
        if job < JOBS1:
            gate(2 * job)
        if job >= 1:
            need("probsT_done", job)
            b = (job - 1) % 2
            mark.inc(nc.scalar.copy(m.pT[:, b].rearrange("p j q -> p (j q)"), s.py[2 + b][:]),
                     "probsT_ready")
        if job < JOBS1:
            gate(2 * job + 1)
            need("max_ready", job + 1)
            b = job % 2
            for e in range(2):
                mark.inc(nc.scalar.activation(m.sc[:, b, e], m.sc[:, b, e], ACT.Exp,
                                              bias=m.nmax[:, b, e:e + 1],
                                              accum_out=m.sum[:, b, e:e + 1]), "exp_ready")
        if job == JOBS1 - 1:
            sigmoid(0)

    for c in range(KD):
        if c + 1 < KD:
            sigmoid(c + 1)
        feed(Q_Y + c)
        need("summed", c + 1)
        mark.inc(nc.scalar.copy(s.xh[:, c], m.m[:, c % 2]), "m_hi")
    for q in range(Q_O, Q_O + 8):
        feed(q)


def mix1_vector(s, m, mark, w, base, slot0, n, layer):
    nc, dve = s.nc, s.nc.vector

    def need(name, k):
        mark.need(dve, layer, name, k)

    norm_rest(s, n, 1)
    for j in range(PAIRS):
        q = Q_Q + j
        w.wait_taken(dve, base, slot0 + q // 3, q % 3)
        mark.inc(nc.vector.tensor_copy(m.qT[:, j], s.pj[j % 2][:, 0:T]), "q_ready")
    for g in range(F_GROUPS):
        need("dft2_done", g + 1)
        mark.inc(nc.vector.tensor_copy(m.fh[:, g], s.pa[g % 2][:, 0:T]), "dft_hi")
        need("dft_hi", g + 1)
        mark.inc(nc.vector.tensor_tensor(m.fl[:, g], s.pa[g % 2][:, 0:T],
                                         m.fh[:, g].bitcast(F32), ALU.subtract), "dft_ready")
    dve.wait_ge(s.bias_loaded, 16 * layer + 16)
    for job in range(JOBS1 + 2):
        b = job % 2
        if job < JOBS1:
            pair, i = divmod(job, TT)
            need("scores_done", job + 1)
            if job >= 2:
                need("probsT_done", job - 1)
            scores = m.sc[:, b].rearrange("p e t -> p (e t)")
            mark.inc(nc.vector.scalar_tensor_tensor(
                scores, s.py[b][:], SCALE,
                m.bias[:, i, 2 * pair:2 * pair + 2].rearrange("p e t -> p (e t)"),
                ALU.mult, ALU.add), "biased")
            need("biased", job + 1)
            mark.inc(nc.vector.tensor_reduce(m.nmax[:, b], m.sc[:, b], AX.X, ALU.max, negate=True),
                     "max_ready")
        if job >= 2:
            done, i = job - 1, (job - 2) % TT
            need("pv_done", done)
            toks = slice(i * P, (i + 1) * P)
            oh, ol = m.oh[:, (job - 2) // TT, toks], m.ol[:, (job - 2) // TT, toks]
            mark.inc(nc.vector.tensor_copy(oh, s.pa[b][:, 0:P]), "o_hi")
            need("o_hi", done)
            mark.inc(nc.vector.tensor_tensor(ol, s.pa[b][:, 0:P], oh.bitcast(F32), ALU.subtract),
                     "o_ready")
        if job < JOBS1:
            need("exp_ready", 2 * job + 2)
            mark.inc(nc.vector.reciprocal(m.inv[:, b], m.sum[:, b]), "inv_sum")
            need("inv_sum", job + 1)
            for e in range(2):
                last = nc.vector.tensor_scalar(m.sc[:, b, e], m.sc[:, b, e], m.inv[:, b, e:e + 1],
                                               None, ALU.mult)
            mark.inc(last, "probs_ready")
    merge_vector(s, m, mark, w, base, slot0, Q_Y, layer)
    finish(s, w, base, slot0 + (Q_O + 7) // 3, (Q_O + 7) % 3, n, 1.0, n + 1)


def merge_vector(s, m, mark, w, base, slot0, q0, layer):
    nc, dve = s.nc, s.nc.vector
    for c in range(KD):
        q, b = q0 + c, c % 2
        mark.need(dve, layer, "sigmoid_ready", 2 * c + 2)
        w.wait_taken(dve, base, slot0 + q // 3, q % 3)
        mark.inc(nc.vector.tensor_tensor(m.gy[:, b].rearrange("p j t -> p (j t)"),
                                         m.gate[:, c].rearrange("p j t -> p (j t)"),
                                         s.pj[b][:], ALU.mult), "gated")
        mark.need(dve, layer, "gated", c + 1)
        mark.inc(nc.vector.tensor_tensor(m.m[:, b], m.gy[:, b, 0], m.gy[:, b, 1], ALU.add), "summed")
        mark.need(dve, layer, "m_hi", c + 1)
        mark.inc(nc.vector.tensor_tensor(s.xl[:, c], m.m[:, b], s.xh[:, c].bitcast(F32),
                                         ALU.subtract), "m_ready")


def move_on(eng, sem, count, by):
    eng.wait_ge(sem, count)
    eng.sem_inc(sem, by)


def final_norm_scalar(s, n):
    fetch_table(s, n, ACT.Sqrt, 1)
    roots(s, n)
    move_on(s.nc.scalar, s.table_in, 2 * n + 3, 1)
    move_on(s.nc.scalar, s.xh_ready, KD * n, KD)


def final_norm_vector(s, n):
    nc, dve = s.nc, s.nc.vector
    for i in range(TT):
        first_mean(s, n, i)
    dve.wait_ge(s.gain_loaded, 16)
    for i in range(TT):
        inverse(s, n, i)
        for half in range(2):
            cols = slice(half * HALF, (half + 1) * HALF)
            nc.vector.scalar_tensor_tensor(s.x[:, i, cols], s.x[:, i, cols], s.inv[:, i:i + 1],
                                           s.gfin[:, cols], ALU.mult, ALU.mult).then_inc(
                s.x_ready, 1)
    move_on(dve, s.diag_ready, TT * n, TT)
    move_on(dve, s.xl_ready, KD * n, KD)


def final_norm_tensor(s, n):
    move_on(s.nc.tensor, s.xt_banks, KD // 2 * n, KD // 2)
    move_on(s.nc.tensor, s.y_tile, n, 1)


GATES = 3 * KD
P2_SBQ, P2_WIDE, P2_G0, P2_Y = 0, 4, 22, 50
P2_CMP = (26, 27, 29, 30)
P2_GATE = [q for q in range(P2_G0, P2_Y) if q not in P2_CMP]
P2_O = P2_Y + KD
NG = NSA_HEADS + DSA_HEADS + 2 * NSA_GROUPS + 1
NORM_W = NG * DH
ZN_W = NORM_W + NSA_GROUPS * DH
ZI_IK, ZI_IW, ZI_GATE, ZI_NVS, ZI_DV = 256, 288, 296, 320, 448
KD_AT = (NSA_HEADS + DSA_HEADS) * DH
NKV = 2 * NSA_GROUPS + 1
SBW = T + P
REPLACED = -3.0e38
NSA_JOBS = [(p, i, br) for p in range(NSA_HEADS // 2) for i in range(TT) for br in (1, 2)]
DSA_JOBS = [(p, i, 3) for p in range(DSA_HEADS // 2) for i in range(TT)]
JOBS = NSA_JOBS + DSA_JOBS
GROUPS = [(p, i) for p in range((NSA_HEADS + DSA_HEADS) // 2) for i in range(TT)]


def job_group(job):
    p, i, br = JOBS[job]
    return (p + (NSA_HEADS // 2 if br == 3 else 0)) * TT + i


LAST_JOB = {g: max(j for j in range(len(JOBS)) if job_group(j) == g) for g in range(len(GROUPS))}
GATE_AT = dict(zip((1, 2, 3, 5, 6, 7, 9, 10, 11, 13, 14, 15, 16, 17, 18, 19), range(8, GATES)))
GATES_IN_SORT = 20

MIX2_TOTALS = dict(
    sq_ready=2, sk_ready=2, wide_ready=10, z_done=4, zm_ready=4, abs_ready=4, e_ready=4,
    l_ready=4, sp_ready=4, d_done=4, dm_ready=4, w_ready=4, osb_done=2, osb_hi=2, osb_ready=2,
    xg_done=1, xb_ready=1, xbh_ready=1, xbl_ready=1, gate_ready=24, hid_ready=2,
    silu_ready=1, hidT_done=1, cmp2_done=1, kc_raw=1, square_ready=2, ms_ready=2, root_ready=2, vec_step=57,
    iq_turned=1, iqd_ready=1, qk_turned=1, kdup_ready=1, kc_dup=1, iqT_done=1, ikT_done=1,
    iqT_ready=1, ikT_ready=1, qT_done=3, qT_ready=3, kT_done=3, kT_ready=3, kcT_done=1,
    kcT_ready=1, vbd_ready=1, gate_exp=1, gate_sig=1, idx_done=8, relu_ready=8, acc_ready=16,
    dbias_ready=2, cs_done=1, cs_ready=1, cexp_ready=1, cp_ready=1, pcT_done=1, pcT_ready=1,
    scores_done=20, biased=20, max_ready=20, exp_ready=40, inv_sum=20, inv_gated=16,
    probs_ready=20, probsT_done=20, probsT_ready=20, pv_done=20, o_hi=12, o_ready=12,
    sigmoid_ready=24, gated=16, summed=16, m_hi=8, m_ready=8)

PAR2 = NORM_W + DH + 2 * DH + 2 * (CMP_LEN // 2)


def mix2_state(sb, s):
    zn = sb("m2_z_heads", [P, TT, ZN_W], F32)
    tmp = sb("m2_tmp", [P, TT * NORM_W], F32)
    zv = sb("m2_z_sbv_cmp", [P, TT, HALF], F32)
    sq = sb("m2_sb_qT", [P, 2, T], F32)
    sk = sb("m2_sb_kT", [P, 2, T], F32)
    sw = sb("m2_weights", [P, 2, HALF], F32)
    sc = sb("m2_scores", [P, 2, HALF], F32)
    oh = sb("m2_attn_hi", [P, 8, T], F32R)
    ol = sb("m2_attn_lo", [P, 8, T], F32R)
    gates = sb("m2_gates", [P, 7, T], F32)
    m = State()
    m.par = sb("m2_params", [P, PAR2], F32)
    m.sq = sq
    m.sk = sk
    m.zv = zv
    m.sc = sc
    m.sw = sw
    m.oh = oh
    m.ol = ol
    m.zi = sb("m2_z_index_v", [P, TT, HALF], F32)
    m.zn = zn
    m.xb = tmp[:, 0:CH].rearrange("p (a o g c) -> p a o g c", a=2, o=16, g=2)
    m.squares = tmp[:, :].rearrange("p (i n) -> p i n", i=TT)
    m.kdup = tmp[:, 0:TT * NKV * P].rearrange("p (i j e d) -> p i j e d", i=TT, j=NKV, e=2)
    m.ikdup = tmp[:, 1280:1536].rearrange("p (i e d) -> p i e d", i=TT, e=4)
    m.vbd = tmp[:, 1536:2048].rearrange("p (h d) -> p h d", h=NSA_HEADS)
    m.pT = tmp[:, 0:CH].rearrange("p (b j q) -> p b j q", b=2, j=4)
    m.xbh = oh[:, 4:8].rearrange("p a (o g c) -> p (a o) g c", g=2, c=CB)
    m.xbl = ol[:, 4:8].rearrange("p a (o g c) -> p (a o) g c", g=2, c=CB)
    m.qT = sb("m2_qT", [P, 6, T], F32)
    m.kbd = sb("m2_k_block", [P, NKV, 2, T], F32)
    m.iqT = sq
    m.pcT = sk[:, 0]
    m.ikbd = sb("m2_ik_block", [P, 4, T], F32)
    m.kcbd = sb("m2_kc_block", [P, NSA_GROUPS, 2, CB], F32)
    m.gate = ([s.squares[:].rearrange("p i d -> p (i d)")[:, g * T:] for g in range(8)]
             + [gates[:, g:].rearrange("p g t -> p (g t)") for g in range(7)]
             + [s.hid[:, g:].rearrange("p g t -> p (g t)") for g in range(2)] + [sk[:, 1]]
             + [sq[:, g:].rearrange("p g t -> p (g t)") for g in range(2)]
             + [sw[:, 0, 0:T], sw[:, 1], sw[:, 1, T:], sw[:, 0, T:]])
    m.hidt = s.act[0:2 * CB, 0]
    m.hidk = sb("m2_hidden_k", [P, NSA_GROUPS * CB], F32)
    m.hidv = sb("m2_hidden_v", [P, NSA_GROUPS, 4, CB], F32)
    m.kc = sb("m2_kc", [2 * CB, DH], F32)
    m.kcs = sb("m2_kc_square", [2 * CB, DH], F32)
    m.kc2 = sb("m2_kc_twice", [2 * CB, 2, DH], F32)
    m.stat = sb("m2_stats", [P, 4, TT * NG], F32)
    m.kstat = sb("m2_kc_stats", [2 * CB, 4], F32)
    m.turn = [t[:, j, 0:TT * NG * 8] for t in (sc, sw) for j in range(2)]
    m.acc = sw[:, 0].rearrange("p (i t) -> p i t", i=TT)
    m.work = sw[:, 1].rearrange("p (i t) -> p i t", i=TT)
    m.dbias = s.act
    m.m8 = sb("m2_top8", [P, 8], F32)
    m.iws = sb("m2_index_w", [P, TT, IDX_HEADS], F32)
    m.gsig = sb("m2_branch_gates", [P, TT, 3 * NSA_HEADS], F32)
    m.cs = sk[:, 1].rearrange("p (i h c) -> p i h c", i=TT, c=CB)
    m.cmx = sb("m2_cmp_max", [P, 2, TT * NSA_HEADS], F32)
    m.nmax = sb("m2_neg_max", [P, 2, 2], F32)
    m.sum = sb("m2_exp_sum", [P, 2, 2], F32)
    m.inv = sb("m2_inv_exp_sum", [P, 2, 2], F32)
    m.gy = zv[:, 0:1].rearrange("p a (b t) -> p (a b) t", b=2)
    m.gz = zv[:, 1:2].rearrange("p a (b t) -> p (a b) t", b=2)
    m.m = tmp[:, 0:2 * T].rearrange("p (b t) -> p b t", b=2)
    m.causal = sb("m2_causal", [P, TT, T], F32)
    m.sbmask = sb("m2_sb_mask", [P, SBW], F32)
    m.tri = sb("m2_tri_ones", [P, 2, P], F32)
    m.cmask = sb("m2_cmp_mask", [P, TT, CB], F32)
    m.hmask = sb("m2_head_mask", [P, NSA_HEADS], F32)
    m.rope = sb("m2_rope", [P, TT, 2, 8], F32)
    m.ropei = sb("m2_rope_index", [P, TT, 2, 4], F32)
    m.ropec = sb("m2_rope_cmp", [2 * CB, 2, 8], F32)
    return m


def mix2_tensor(s, m, mark, w, base, slot0, n, layer):
    nc, pe = s.nc, s.nc.tensor

    def need(name, k):
        mark.need(pe, layer, name, k)

    def gate(g):
        if g < 2:
            need("dm_ready", 3 + g)
        else:
            need("gate_ready", g - 1)
        project(s, w, base, slot0, P2_GATE[g], s.pj[g % 2][:, 0:T])

    def sb_z(h, last):
        rows, bank = slice((h % 2) * DH, (h % 2 + 1) * DH), s.pj[h % 2]
        nc.tensor.matmul(bank[:, 0:T], m.sk[rows, h // 2, 0:P], m.sq[rows, h // 2], start=True,
                         stop=False)
        return nc.tensor.matmul(bank[:, T:SBW], m.sk[rows, h // 2, P:T], m.sq[rows, h // 2, P:T],
                                start=False, stop=last)

    def sb_scores(h):
        if h < 2:
            need("sk_ready", h + 1)
        else:
            need("dm_ready", h - 1)
        mark.inc(sb_z(h, True), "z_done")

    def sb_tails(h):
        sp, bank = m.sc[:, h % 2], s.pj[h % 2]
        need("sp_ready", h + 1)
        sb_z(h, False)
        nc.tensor.matmul(bank[:, 0:T], m.tri[:, 0], sp[:, 0:T], start=False, stop=False)
        nc.tensor.matmul(bank[:, P:T], m.tri[:, 1], sp[:, T:SBW], start=False, stop=False)
        mark.inc(nc.tensor.matmul(bank[:, T:SBW], m.tri[:, 0], sp[:, T:SBW], start=False,
                                  stop=True), "d_done")

    def sb_out(pair):
        for h in (2 * pair, 2 * pair + 1):
            need("w_ready", h + 1)
            rows, cols = slice((h % 2) * DH, (h % 2 + 1) * DH), slice(h * DH, (h + 1) * DH)
            nc.tensor.matmul(s.pa[pair][rows, 0:T], m.zv[:, 0, cols], m.sw[:, h % 2, 0:T],
                             start=True, stop=False)
            last = nc.tensor.matmul(s.pa[pair][rows, P:T], m.zv[:, 1, cols], m.sw[:, h % 2, T:SBW],
                                    start=False, stop=True)
        mark.inc(last, "osb_done")

    norm_tensor(s, n)
    pe.wait_ge(s.zeroed, 1)
    for j in range(4):
        if j >= 2:
            need("sq_ready", j - 1)
        project(s, w, base, slot0, P2_SBQ + j, s.pj[j % 2][:, 0:T], n if j == 0 else None)
    project_wide(s, w, base, slot0, P2_WIDE, s.py[0:2])
    for h in (0, 1):
        sb_scores(h)
    project_wide(s, w, base, slot0, P2_WIDE + 4, s.py[2:4])
    for h in (0, 1):
        sb_tails(h)
    need("wide_ready", 2)
    project_wide(s, w, base, slot0, P2_WIDE + 8, s.py[0:2])
    sb_out(0)
    for h in (2, 3):
        sb_scores(h)
    need("wide_ready", 4)
    project_wide(s, w, base, slot0, P2_WIDE + 12, s.py[2:4])
    for h in (2, 3):
        sb_tails(h)
    need("wide_ready", 6)
    width = ZN_W - 2 * HALF
    for j in range(2):
        q = P2_WIDE + 16 + j
        hi, lo = w.chunk(pe, base, slot0 + q // 3, q % 3)
        for kk in range(4):
            k, cols = 4 * j + kk, slice(kk * width, (kk + 1) * width)
            for i in range(TT):
                toks = slice(i * P, (i + 1) * P)
                last = product(nc, s.py[i][:, 0:width], (s.xh[:, k, toks], s.xl[:, k, toks]),
                               (hi[:, cols], lo[:, cols]), k == 0, k == KD - 1)
        w.taken(last, q % 3)
    sb_out(1)
    need("wide_ready", 8)
    for a in range(2):
        for g in range(NSA_GROUPS):
            at = T + (a * NSA_GROUPS + g) * DH
            for i in range(TT):
                for e in range(2):
                    col = (a * NSA_GROUPS + g) * P + i * DH
                    last = nc.tensor.matmul(s.py[2][e * DH:(e + 1) * DH, col:col + DH],
                                            m.zv[:, i, at:at + DH], s.ident[:, e::2])
    mark.inc(last, "xg_done")
    for g in range(4):
        gate(g)
    need("osb_ready", 2)
    need("xbl_ready", 1)
    for j in range(4):
        q, a = P2_CMP[j], j // 2
        if j == 2:
            gate(4)
        hi, lo = w.chunk(pe, base, slot0 + q // 3, q % 3)
        for k in range(8):
            o, cols = (j % 2) * 8 + k, slice(k * P, (k + 1) * P)
            xh = m.xbh[:, a * 16 + o].rearrange("p g c -> p (g c)")
            xl = m.xbl[:, a * 16 + o].rearrange("p g c -> p (g c)")
            last = product(nc, s.pa[1][0:2 * CB, a * P:(a + 1) * P], (xh, xl),
                           (hi[:, cols], lo[:, cols]), o == 0, o == 15)
        w.taken(last, q % 3)
    gate(5)
    need("silu_ready", 1)
    pe.sem_inc(s.order, 1)
    for a in range(2):
        last = nc.tensor.transpose(s.pa[0][:, a * 2 * CB:(a + 1) * 2 * CB],
                                   m.hidt[:, a * P:(a + 1) * P], s.ident[0:2 * CB, 0:2 * CB])
    mark.inc(last, "hidT_done")
    gate(6)
    need("hid_ready", 2)
    w2 = m.par[:, NORM_W + DH:NORM_W + 3 * DH]
    nc.tensor.matmul(s.pa[0][0:2 * CB, 0:DH], m.hidk[:], w2[:, 0:DH])
    mark.inc(nc.tensor.matmul(s.pa[0][:, DH:2 * DH], m.hidv[:].rearrange("p g r c -> p (g r c)"),
                              w2[:, DH:2 * DH]), "cmp2_done")
    need("wide_ready", 10)
    need("iq_turned", 1)
    for cq in range(2):
        for i in range(TT):
            last = nc.tensor.transpose(s.py[0][:, cq * T + i * P:cq * T + (i + 1) * P],
                                       m.zi[:, i, cq * P:(cq + 1) * P], s.ident[:])
    mark.inc(last, "iqT_done")
    need("iqd_ready", 1)
    for i in range(TT):
        last = nc.tensor.transpose(s.py[1][:, i * P:(i + 1) * P],
                                   m.ikdup[:, i].rearrange("p e d -> p (e d)"), s.ident[:])
    mark.inc(last, "ikT_done")
    gate(7)
    need("qk_turned", 1)
    for c3, bank in enumerate((2, 3, 0)):
        if bank == 0:
            need("iqT_ready", 1)
        for cc in range(2):
            c = 2 * c3 + cc
            for i in range(TT):
                last = nc.tensor.transpose(s.py[bank][:, cc * T + i * P:cc * T + (i + 1) * P],
                                           m.zn[:, i, c * P:(c + 1) * P], s.ident[:])
        mark.inc(last, "qT_done")
    need("kdup_ready", 1)
    for j3, bank in enumerate((1, 2, 3)):
        if bank == 1:
            need("ikT_ready", 1)
        else:
            need("qT_ready", bank - 1)
        for j in range(2 * j3, min(2 * j3 + 2, NKV)):
            for i in range(TT):
                at = (j - 2 * j3) * T + i * P
                last = nc.tensor.transpose(s.py[bank][:, at:at + P],
                                           m.kdup[:, i, j].rearrange("p e d -> p (e d)"), s.ident[:])
        mark.inc(last, "kT_done")
    need("kc_dup", 1)
    pe.sem_inc(s.order, 1)
    mark.inc(nc.tensor.transpose(s.pa[1][:, 0:2 * CB], m.kc2[:].rearrange("c e d -> c (e d)"),
                                 s.ident[0:2 * CB, 0:2 * CB]), "kcT_done")
    need("kcT_ready", 1)
    need("vbd_ready", 1)
    need("qT_ready", 2)
    for i in range(TT):
        for p in range(NSA_HEADS // 2):
            last = nc.tensor.matmul(s.pa[0][:, i * P + p * 2 * CB:i * P + (p + 1) * 2 * CB],
                                    m.qT[:, p, i * P:(i + 1) * P],
                                    m.kcbd[:, p // 2].rearrange("p e c -> p (e c)"))
    mark.inc(last, "cs_done")
    need("kT_ready", 3)
    need("qT_ready", 3)
    for u in range(8):
        i, cq, hh = u // 4, u // 2 % 2, u % 2
        kw = (i + 1) * P
        if u >= 4:
            need("relu_ready", u - 3)
        mark.inc(nc.tensor.matmul(s.py[u % 4][:, 0:2 * kw], m.iqT[:, cq, i * P:(i + 1) * P],
                                  m.ikbd[:, 2 * hh:2 * hh + 2, 0:kw]), "idx_done")
    need("cp_ready", 1)
    for i in range(TT):
        last = nc.tensor.transpose(s.pa[1][:, i * P:(i + 1) * P],
                                   m.cs[:, i].rearrange("p h c -> p (h c)"), s.ident[:])
    mark.inc(last, "pcT_done")
    need("pcT_ready", 1)
    for step in range(len(JOBS) + 2):
        if step < len(JOBS):
            p, i, br = JOBS[step]
            if step < 2:
                need("relu_ready", 8)
            else:
                need("biased", step - 1)
            kv = {1: p // 2, 2: NSA_GROUPS + p // 2, 3: NKV - 1}[br]
            qc, kw = p + (NSA_HEADS // 2 if br == 3 else 0), (i + 1) * P
            mark.inc(nc.tensor.matmul(s.py[step % 2][:, 0:2 * kw], m.qT[:, qc, i * P:(i + 1) * P],
                                      m.kbd[:, kv, :, 0:kw]), "scores_done")
        if 1 <= step <= len(JOBS):
            job = step - 1
            i, b = JOBS[job][1], job % 2
            need("probs_ready", job + 1)
            if job >= 2:
                need("probsT_ready", job - 1)
            for e in range(2):
                for kc in range(i + 1):
                    j = e * (i + 1) + kc
                    last = nc.tensor.transpose(s.py[2 + b][:, j * P:(j + 1) * P],
                                               m.sc[:, b, j * P:(j + 1) * P], s.ident[:])
            mark.inc(last, "probsT_done")
        if step in GATE_AT:
            gate(GATE_AT[step])
        if step >= 2:
            job = step - 2
            p, i, br = JOBS[job]
            g, toks = job_group(job), slice(i * P, (i + 1) * P)
            out, first = s.pa[g % 2], job == 0 or job_group(job - 1) != g
            need("probsT_ready", job + 1)
            if first and g >= 2:
                need("o_ready", g - 1)
            if first and br != 3:
                nc.tensor.matmul(out[:, 0:P], m.vbd[:, 2 * p:2 * p + 2].rearrange("p h d -> p (h d)"),
                                 m.pcT[:, toks], start=True, stop=False)
            for e in range(2):
                for kc in range(i + 1):
                    v = {1: m.zi[:, kc, ZI_NVS + p // 2 * DH:][:, 0:DH],
                         2: m.zn[:, kc, NORM_W + p // 2 * DH:][:, 0:DH],
                         3: m.zi[:, kc, ZI_DV:ZI_DV + DH]}[br]
                    last = nc.tensor.matmul(out[e * DH:(e + 1) * DH, 0:P], v,
                                            m.pT[:, job % 2, e * (i + 1) + kc],
                                            start=br == 3 and kc == 0, stop=kc == i and br >= 2)
            mark.inc(last, "pv_done")
    for c in range(KD):
        q = P2_Y + c
        if c < 2:
            need("gate_ready", GATES - 1 + c)
        else:
            need("gated", 2 * (c - 1))
        hi, lo = w.chunk(pe, base, slot0 + q // 3, q % 3)
        for k in range(8):
            if c == 0 and k >= 2:
                need("o_ready", {6: 11, 7: 12}.get(k, 2 * (k - 1)))
            out = (s.pj[c % 2][:, 0:T] if k < 2 else s.pj[c % 2][:, T:2 * T] if k < 6
                   else s.pa[c % 2][:, 0:T])
            cols = slice(k * P, (k + 1) * P)
            last = product(nc, out, (hi[:, cols], lo[:, cols]), (m.oh[:, k], m.ol[:, k]),
                           k in (0, 2, 6), k in (1, 5, 7))
        w.taken(last, q % 3)
    project_out(s, s.xh, s.xl, w, base, slot0, P2_O, mark, layer)


def mix2_scalar(s, m, mark, w, base, slot0, n, layer):
    nc, act = s.nc, s.nc.scalar
    fed = [0]

    def need(name, k):
        mark.need(act, layer, name, k)

    def chunk(q, wait=True):
        while fed[0] <= q:
            if fed[0] % 3 == 2 and fed[0] // 3 + 1 < MIX2_SLOTS:
                w.feed(act, base, slot0 + fed[0] // 3 + 1)
            fed[0] += 1
        if wait:
            w.wait_taken(act, base, slot0 + q // 3, q % 3)

    def gate(g):
        chunk(P2_GATE[g])
        mark.inc(nc.scalar.copy(m.gate[g][:, 0:T], s.pj[g % 2][:, 0:T]), "gate_ready")

    def wide(b, dests):
        chunk(P2_WIDE + (4 * b + 3 if b < 4 else 17))
        for i in range(TT):
            bank = s.py[2 * (b % 2) + i]
            mark.inc(nc.scalar.copy(dests[i], bank[:, 0:dests[i].shape[-1]]), "wide_ready")
        chunk(P2_WIDE + 4 * b + 4 if b < 4 else P2_G0, False)

    def sb_softplus(h):
        for k in (h, h + 1):
            need("abs_ready", k + 1)
            a = m.sw[:, k % 2, 0:SBW]
            mark.inc(nc.scalar.activation(a, a, ACT.Exp, scale=-1.0), "e_ready")
        for k in (h, h + 1):
            need("e_ready", k + 1)
            a = m.sw[:, k % 2, 0:SBW]
            mark.inc(nc.scalar.activation(a, a, ACT.Ln, bias=1.0), "l_ready")

    def sb_weights(h):
        for k in (h, h + 1):
            need("dm_ready", k + 1)
            a = m.sw[:, k % 2, 0:SBW]
            mark.inc(nc.scalar.activation(a, a, ACT.Exp), "w_ready")

    norm_scalar(s, w, base, slot0, n, 1, ACT.Exp)
    chunk(P2_SBQ + 1, False)
    for j in range(2):
        chunk(P2_SBQ + 2 + j)
        mark.inc(nc.scalar.copy(m.sk[:, j], s.pj[j][:, 0:T]), "sk_ready")
    wide(0, [m.zv[:, i] for i in range(TT)])
    sb_softplus(0)
    wide(1, [m.zi[:, i] for i in range(TT)])
    sb_weights(0)
    wide(2, [m.zn[:, i, 0:HALF] for i in range(TT)])
    sb_softplus(2)
    wide(3, [m.zn[:, i, HALF:2 * HALF] for i in range(TT)])
    sb_weights(2)
    wide(4, [m.zn[:, i, 2 * HALF:ZN_W] for i in range(TT)])
    need("xb_ready", 1)
    mark.inc(nc.scalar.copy(m.xbh[:], m.xb[:].rearrange("p a o g c -> p (a o) g c")), "xbh_ready")
    gate(0)
    gate(1)
    need("xbl_ready", 1)
    for i in range(TT):
        mark.inc(nc.scalar.activation(m.squares[:, i], m.zn[:, i, 0:NORM_W], ACT.Square),
                 "square_ready")
    gate(2)
    gate(3)
    need("ms_ready", 1)
    mark.inc(nc.scalar.activation(m.stat[:, 2], m.stat[:, 1], ACT.Sqrt), "root_ready")
    gate(4)
    chunk(P2_CMP[3])
    mark.inc(nc.scalar.activation(m.hidt, s.pa[1][0:2 * CB, 0:2 * P], ACT.Silu), "silu_ready")
    gate(5)
    need("hidT_done", 1)
    mark.inc(nc.scalar.copy(m.hidk[:], s.pa[0][:, 0:2 * CB]), "hid_ready")
    hv = s.pa[0][:, 2 * CB:4 * CB].rearrange("p (g a c) -> p g a c", g=NSA_GROUPS, a=1)
    mark.inc(nc.scalar.copy(m.hidv[:], hv.to_broadcast([P, NSA_GROUPS, 4, CB])), "hid_ready")
    gate(6)
    need("iqT_done", 1)
    mark.inc(nc.scalar.copy(m.iqT[:].rearrange("p a t -> p (a t)"), s.py[0][:]), "iqT_ready")
    need("ikT_done", 1)
    for e in range(4):
        rows = slice(e * IDX_DIM, (e + 1) * IDX_DIM)
        last = nc.scalar.copy(m.ikbd[rows, e], s.py[1][rows, 0:T])
    mark.inc(last, "ikT_ready")
    need("ms_ready", 2)
    mark.inc(nc.scalar.activation(m.kstat[:, 2:3], m.kstat[:, 1:2], ACT.Sqrt), "root_ready")
    gate(7)
    for c3, bank in enumerate((2, 3, 0)):
        need("qT_done", c3 + 1)
        mark.inc(nc.scalar.copy(m.qT[:, 2 * c3:2 * c3 + 2].rearrange("p a t -> p (a t)"),
                                s.py[bank][:]), "qT_ready")
    for j3, bank in enumerate((1, 2, 3)):
        need("kT_done", j3 + 1)
        k = min(2, NKV - 2 * j3)
        for e in range(2):
            rows = slice(e * DH, (e + 1) * DH)
            last = nc.scalar.copy(m.kbd[rows, 2 * j3:2 * j3 + k, e],
                                  s.py[bank][rows, 0:k * T].rearrange("p (a t) -> p a t", a=k))
        mark.inc(last, "kT_ready")
    mark.inc(nc.scalar.activation(m.gsig[:], m.zi[:, :, ZI_GATE:ZI_NVS], ACT.Exp, scale=-1.0),
             "gate_exp")
    need("cs_ready", 1)
    mark.inc(nc.scalar.activation(m.cs[:], m.cs[:], ACT.Exp), "cexp_ready")
    for u in range(8):
        kw = (u // 4 + 1) * P
        need("idx_done", u + 1)
        if u >= 2:
            need("acc_ready", 2 * (u - 1))
        mark.inc(nc.scalar.activation(m.sc[:, u % 2, 0:2 * kw], s.py[u % 4][:, 0:2 * kw], ACT.Relu),
                 "relu_ready")
    need("pcT_done", 1)
    mark.inc(nc.scalar.copy(m.pcT[:], s.pa[1][:, 0:T]), "pcT_ready")
    def sigmoids(c):
        for g in range(3 * c, 3 * c + 3):
            at = m.gate[g][:, 0:T]
            need("gate_ready", g + 1)
            mark.inc(nc.scalar.activation(at, at, ACT.Sigmoid), "sigmoid_ready")

    for step in range(len(JOBS) + 1):
        if step >= 1:
            job = step - 1
            b, width = job % 2, 2 * (JOBS[job][1] + 1)
            need("probsT_done", job + 1)
            mark.inc(nc.scalar.copy(m.pT[:, b, 0:width].rearrange("p j q -> p (j q)"),
                                    s.py[2 + b][:, 0:width * P]), "probsT_ready")
        if step < len(JOBS):
            b, kw = step % 2, (JOBS[step][1] + 1) * P
            need("max_ready", step + 1)
            for e in range(2):
                at = m.sc[:, b, e * kw:(e + 1) * kw]
                mark.inc(nc.scalar.activation(at, at, ACT.Exp, bias=m.nmax[:, b, e:e + 1],
                                              accum_out=m.sum[:, b, e:e + 1]), "exp_ready")
        if step == len(JOBS) - 1:
            sigmoids(0)
        if step in GATE_AT:
            if GATE_AT[step] == GATES_IN_SORT:
                need("dbias_ready", 2)
            gate(GATE_AT[step])

    for c in range(KD):
        chunk(P2_Y + c, False)
        if c + 1 < KD:
            sigmoids(c + 1)
        need("summed", 2 * c + 2)
        mark.inc(nc.scalar.copy(s.xh[:, c], m.m[:, c % 2]), "m_hi")
    chunk(P2_O + KD - 1, False)


def mix2_vector(s, m, mark, w, base, slot0, n, layer):
    nc, dve = s.nc, s.nc.vector

    def need(name, k):
        mark.need(dve, layer, name, k)

    def step(ins):
        mark.inc(ins, "vec_step")
        need("vec_step", mark.made["vec_step"])

    def after(name):
        need(name, mark.made[name])

    norm_rest(s, n, 1)
    dve.wait_ge(s.consts2_loaded, 16 * CONSTS2)
    for j in range(2):
        q = P2_SBQ + j
        w.wait_taken(dve, base, slot0 + q // 3, q % 3)
        mark.inc(nc.vector.tensor_scalar(m.sq[:, j], s.pj[j][:, 0:T], SCALE, None, ALU.mult),
                 "sq_ready")
    for pair in range(2):
        for h in (2 * pair, 2 * pair + 1):
            z, a = m.sc[:, h % 2, 0:SBW], m.sw[:, h % 2, 0:SBW]
            need("z_done", h + 1)
            if h >= 2:
                need("d_done", h - 1)
                need("osb_done", 1)
            mark.inc(nc.vector.tensor_tensor(z, s.pj[h % 2][:, 0:SBW], m.sbmask[:], ALU.add),
                     "zm_ready")
            after("zm_ready")
            mark.inc(nc.vector.scalar_tensor_tensor(a, z, -1.0, z, ALU.mult, ALU.max), "abs_ready")
        for h in (2 * pair, 2 * pair + 1):
            z, a = m.sc[:, h % 2, 0:SBW], m.sw[:, h % 2, 0:SBW]
            need("l_ready", h + 1)
            mark.inc(nc.vector.scalar_tensor_tensor(z, z, 0.0, a, ALU.max, ALU.add), "sp_ready")
        for h in (2 * pair, 2 * pair + 1):
            need("d_done", h + 1)
            mark.inc(nc.vector.tensor_tensor(m.sw[:, h % 2, 0:SBW], s.pj[h % 2][:, 0:SBW],
                                             m.sbmask[:], ALU.add), "dm_ready")
        need("osb_done", pair + 1)
        mark.inc(nc.vector.tensor_copy(m.oh[:, pair], s.pa[pair][:, 0:T]), "osb_hi")
        after("osb_hi")
        mark.inc(nc.vector.tensor_tensor(m.ol[:, pair], s.pa[pair][:, 0:T],
                                         m.oh[:, pair].bitcast(F32), ALU.subtract), "osb_ready")
    need("xg_done", 1)
    dve.wait_ge(s.par2_loaded, 16 * layer + 16)
    nc.vector.memset(m.xb[:].rearrange("p a o g c -> p (a o g) c")[:, :, NCMP:CB], 0.0)
    xg = s.py[2][:].rearrange("p (a g c o) -> p a g c o", a=2, g=NSA_GROUPS, c=CB)
    pe_col = NORM_W + 3 * DH
    for a in range(2):
        for half in range(2):
            pos = m.par[:, pe_col + a * 16 + half * 8:pe_col + a * 16 + half * 8 + 8]
            last = nc.vector.tensor_tensor(
                m.xb[:, a, half * 8:half * 8 + 8, :, 0:NCMP].rearrange("p o g c -> p g c o"),
                xg[:, a, :, half:half + NCMP, :],
                pos.rearrange("p (x y o) -> p x y o", x=1, y=1).to_broadcast([P, 2, NCMP, 8]),
                ALU.add)
    mark.inc(last, "xb_ready")
    need("xbh_ready", 1)
    mark.inc(nc.vector.tensor_tensor(m.xbl[:], m.xb[:].rearrange("p a o g c -> p (a o) g c"),
                                     m.xbh[:].bitcast(F32), ALU.subtract), "xbl_ready")

    def turn(x, half, cos, sin, name):
        shape = list(x.shape[:-1]) + [half]
        x1, x2 = x[..., 0:half], x[..., half:2 * half]
        size = 1
        for dim in shape[1:]:
            size *= dim
        t = []
        for buf in m.turn:
            flat = buf[0:shape[0], 0:size]
            t.append(flat.rearrange("p (i g f) -> p i g f", i=shape[1], f=half) if len(shape) == 4
                     else flat)
        for out, a, table in ((t[0], x1, cos), (t[1], x2, sin), (t[2], x2, cos), (t[3], x1, sin)):
            last = nc.vector.tensor_tensor(out, a, table.to_broadcast(shape), ALU.mult)
        step(last)
        nc.vector.tensor_tensor(x1, t[0], t[1], ALU.subtract)
        mark.inc(nc.vector.tensor_tensor(x2, t[2], t[3], ALU.add), name)

    def table(r, k, half):
        return r[:, :, k].rearrange("p i (g f) -> p i g f", g=1)

    need("wide_ready", 4)
    turn(m.zi[:, :, 0:ZI_IW].rearrange("p i (g f) -> p i g f", f=IDX_DIM), 4,
         table(m.ropei, 0, 4), table(m.ropei, 1, 4), "iq_turned")
    heads = m.zn[:, :, 0:NORM_W].rearrange("p i (g f) -> p i g f", f=DH)
    need("square_ready", 2)
    step(nc.vector.tensor_reduce(m.stat[:, 0], m.squares[:].rearrange("p i (g f) -> p (i g) f", f=DH),
                                 AX.X, ALU.add))
    mark.inc(nc.vector.tensor_scalar(m.stat[:, 1], m.stat[:, 0], 1.0 / DH, EPS, ALU.mult, ALU.add),
             "ms_ready")
    ik = m.zi[:, :, ZI_IK:ZI_IW].rearrange("p i (e d) -> p i e d", e=1)
    after("iq_turned")
    mark.inc(nc.vector.tensor_copy(m.ikdup[:], ik.to_broadcast([P, TT, 4, IDX_DIM])), "iqd_ready")
    need("root_ready", 1)
    step(nc.vector.reciprocal(m.stat[:, 3], m.stat[:, 2]))
    step(nc.vector.tensor_tensor(
        heads, heads, m.stat[:, 3].rearrange("p (i g f) -> p i g f", i=TT, f=1).to_broadcast(
            [P, TT, NG, DH]), ALU.mult))
    for i in range(TT):
        last = nc.vector.tensor_tensor(m.zn[:, i, 0:NORM_W], m.zn[:, i, 0:NORM_W],
                                       m.par[:, 0:NORM_W], ALU.mult)
    step(last)
    turn(m.zn[:, :, 0:NORM_W].rearrange("p i (g f) -> p i g f", f=DH), 8,
         table(m.rope, 0, 8), table(m.rope, 1, 8), "qk_turned")
    after("qk_turned")
    for i in range(TT):
        keys = m.zn[:, i, KD_AT:KD_AT + NKV * DH].rearrange("p (j e d) -> p j e d", j=NKV, e=1)
        last = nc.vector.tensor_copy(m.kdup[:, i], keys.to_broadcast([P, NKV, 2, DH]))
    mark.inc(last, "kdup_ready")
    need("cmp2_done", 1)
    mark.inc(nc.vector.tensor_tensor(
        m.vbd[:], s.pa[0][:, DH:2 * DH].rearrange("p (h d) -> p h d", h=1).to_broadcast(
            [P, NSA_HEADS, DH]),
        m.hmask[:].rearrange("p (h d) -> p h d", d=1).to_broadcast([P, NSA_HEADS, DH]), ALU.mult),
        "vbd_ready")
    step(nc.vector.tensor_copy(m.kc[:], s.pa[0][0:2 * CB, 0:DH]))
    step(nc.vector.tensor_tensor(m.kcs[:], m.kc[:], m.kc[:], ALU.mult))
    step(nc.vector.tensor_reduce(m.kstat[:, 0:1], m.kcs[:], AX.X, ALU.add))
    mark.inc(nc.vector.tensor_scalar(m.kstat[:, 1:2], m.kstat[:, 0:1], 1.0 / DH, EPS, ALU.mult,
                                     ALU.add), "ms_ready")
    need("root_ready", 2)
    step(nc.vector.reciprocal(m.kstat[:, 3:4], m.kstat[:, 2:3]))
    step(nc.vector.scalar_tensor_tensor(m.kc[:], m.kc[:], m.kstat[:, 3:4],
                                        m.par[0:2 * CB, NORM_W:NORM_W + DH], ALU.mult, ALU.mult))
    turn(m.kc[:], 8, m.ropec[:, 0], m.ropec[:, 1], "kc_raw")
    after("kc_raw")
    mark.inc(nc.vector.tensor_copy(m.kc2[:], m.kc[:].rearrange("c (e d) -> c e d", e=1)
                                   .to_broadcast([2 * CB, 2, DH])), "kc_dup")
    step(nc.vector.tensor_scalar(m.iws[:], m.zi[:, :, ZI_IW:ZI_GATE],
                                 (IDX_HEADS * IDX_DIM) ** -0.5, None, ALU.mult))
    need("kcT_done", 1)
    for e in range(2):
        rows = slice(e * DH, (e + 1) * DH)
        last = nc.vector.tensor_copy(m.kcbd[rows, :, e],
                                     s.pa[1][rows, 0:2 * CB].rearrange("p (g c) -> p g c", c=CB))
    mark.inc(last, "kcT_ready")
    need("cs_done", 1)
    for i in range(TT):
        last = nc.vector.scalar_tensor_tensor(
            m.cs[:, i], s.pa[0][:, i * P:(i + 1) * P].rearrange("p (h c) -> p h c", c=CB), SCALE,
            m.cmask[:, i].rearrange("p (h c) -> p h c", h=1).to_broadcast([P, NSA_HEADS, CB]),
            ALU.mult, ALU.add)
    step(last)
    flat = m.cs[:].rearrange("p i h c -> p (i h) c")

    def over_keys(x):
        return x.rearrange("p (n c) -> p n c", c=1).to_broadcast([P, TT * NSA_HEADS, CB])

    step(nc.vector.tensor_reduce(m.cmx[:, 0], flat, AX.X, ALU.max))
    step(nc.vector.tensor_scalar(m.cmx[:, 0], m.cmx[:, 0], 0.1 * MASKED, None, ALU.max))
    mark.inc(nc.vector.tensor_tensor(flat, flat, over_keys(m.cmx[:, 0]), ALU.subtract), "cs_ready")
    need("gate_exp", 1)
    step(nc.vector.tensor_scalar(m.gsig[:], m.gsig[:], 1.0, None, ALU.add))
    mark.inc(nc.vector.reciprocal(m.gsig[:], m.gsig[:]), "gate_sig")
    need("cexp_ready", 1)
    step(nc.vector.tensor_reduce(m.cmx[:, 1], flat, AX.X, ALU.add))
    step(nc.vector.tensor_scalar(m.cmx[:, 1], m.cmx[:, 1], 1e-30, None, ALU.max))
    step(nc.vector.reciprocal(m.cmx[:, 1], m.cmx[:, 1]))
    after("gate_sig")
    g0 = m.gsig[:].rearrange("p i (h r) -> p i h r", r=3)[:, :, :, 0]
    mx = m.cmx[:, 1].rearrange("p (i h) -> p i h", i=TT)
    step(nc.vector.tensor_tensor(mx, mx, g0, ALU.mult))
    mark.inc(nc.vector.tensor_tensor(flat, flat, over_keys(m.cmx[:, 1]), ALU.mult), "cp_ready")
    for u in range(8):
        i, kw = u // 4, (u // 4 + 1) * P
        acc = m.acc[:, i, 0:kw]
        need("relu_ready", u + 1)
        for e in range(2):
            h = (u % 4) * 2 + e
            relu, wh = m.sc[:, u % 2, e * kw:(e + 1) * kw], m.iws[:, i, h:h + 1]
            if h == 0:
                ins = nc.vector.tensor_scalar(acc, relu, wh, None, ALU.mult)
            else:
                after("acc_ready")
                ins = nc.vector.scalar_tensor_tensor(acc, relu, wh, acc, ALU.mult, ALU.add)
            mark.inc(ins, "acc_ready")

    def ordered():
        dve.sem_inc(s.order, 1)

    def sort_round(i, r):
        kw = (i + 1) * P
        acc, work, causal = m.acc[:, i, 0:kw], m.work[:, i, 0:kw], m.causal[:, i, 0:kw]
        if r == 0:
            after("acc_ready")
            step(nc.vector.tensor_tensor(acc, acc, causal, ALU.add))
        src = work if r else acc
        ordered()
        step(nc.vector.max(m.m8[:], src))
        ordered()
        step(nc.vector.match_replace(work, m.m8[:], src, REPLACED))
        if r == TOPK // 8 - 1:
            step(nc.vector.tensor_scalar(work, work, 0.5 * REPLACED, MASKED, ALU.is_gt, ALU.mult))
            mark.inc(nc.vector.tensor_tensor(m.dbias[:, i, 0:kw], work, causal, ALU.add),
                     "dbias_ready")

    assert len(NSA_JOBS) == TT * (TOPK // 8)
    for job in range(len(JOBS) + 3):
        if job < len(JOBS):
            p, i, br = JOBS[job]
            b, kw = job % 2, (i + 1) * P
            if job == len(NSA_JOBS):
                after("dbias_ready")
            need("scores_done", job + 1)
            if job >= 2:
                need("probsT_done", job - 1)
            sc = m.sc[:, b, 0:2 * kw].rearrange("p (e t) -> p e t", e=2)
            bias = (m.dbias if br == 3 else m.causal)[:, i, 0:kw]
            mark.inc(nc.vector.scalar_tensor_tensor(
                sc, s.py[b][:, 0:2 * kw].rearrange("p (e t) -> p e t", e=2), SCALE,
                bias.rearrange("p (e t) -> p e t", e=1).to_broadcast([P, 2, kw]),
                ALU.mult, ALU.add), "biased")
            after("biased")
            mark.inc(nc.vector.tensor_reduce(m.nmax[:, b], sc, AX.X, ALU.max, negate=True),
                     "max_ready")
        if job >= 3 and LAST_JOB[job_group(job - 3)] == job - 3:
            g = job_group(job - 3)
            need("pv_done", job - 2)
            at = (slice(0, P), 2 + g // TT, slice((g % TT) * P, (g % TT + 1) * P))
            mark.inc(nc.vector.tensor_copy(m.oh[at], s.pa[g % 2][:, 0:P]), "o_hi")
            after("o_hi")
            mark.inc(nc.vector.tensor_tensor(m.ol[at], s.pa[g % 2][:, 0:P], m.oh[at].bitcast(F32),
                                             ALU.subtract), "o_ready")
        if job < len(NSA_JOBS):
            sort_round(*divmod(job, TOPK // 8))
        if job < len(JOBS):
            need("exp_ready", 2 * job + 2)
            mark.inc(nc.vector.reciprocal(m.inv[:, b], m.sum[:, b]), "inv_sum")
            after("inv_sum")
            if br != 3:
                gates = m.gsig[:, i].rearrange("p (h r) -> p h r", r=3)[:, 2 * p:2 * p + 2, br]
                mark.inc(nc.vector.tensor_tensor(m.inv[:, b], m.inv[:, b], gates, ALU.mult),
                         "inv_gated")
                after("inv_gated")
            for e in range(2):
                last = nc.vector.tensor_scalar(sc[:, e], sc[:, e], m.inv[:, b, e:e + 1], None,
                                               ALU.mult)
            mark.inc(last, "probs_ready")
    for c in range(KD):
        q, b, g = P2_Y + c, c % 2, 3 * c
        need("sigmoid_ready", 3 * c + 3)
        w.wait_taken(dve, base, slot0 + q // 3, q % 3)
        mark.inc(nc.vector.tensor_tensor(m.gy[:].rearrange("p j t -> p (j t)"), m.gate[g][:, 0:2 * T],
                                         s.pj[b][:], ALU.mult), "gated")
        mark.inc(nc.vector.tensor_tensor(m.gz[:, 0], m.gate[g + 2][:, 0:T], s.pa[b][:, 0:T],
                                         ALU.mult), "gated")
        after("gated")
        mark.inc(nc.vector.tensor_tensor(m.gz[:, 1], m.gy[:, 0], m.gy[:, 1], ALU.add), "summed")
        after("summed")
        mark.inc(nc.vector.tensor_tensor(m.m[:, b], m.gz[:, 1], m.gz[:, 0], ALU.add), "summed")
        need("m_hi", c + 1)
        mark.inc(nc.vector.tensor_tensor(s.xl[:, c], m.m[:, b], s.xh[:, c].bitcast(F32),
                                         ALU.subtract), "m_ready")
    finish(s, w, base, slot0 + (P2_O + 7) // 3, (P2_O + 7) % 3, n, 1.0, n + 1)


PAR1 = 3 * KD + 2 * KD
SLOTS1 = 2 * FC + MIX1_SLOTS
SLOTS2 = 2 * FC + MIX2_SLOTS
PAR = 3 * KD
SLOTS2_AT = LAYERS * SLOTS1
CONSTS1 = 3
CONSTS2 = 8
X2 = 3 * LAYERS + 1


def build(nc, a):
    with ExitStack() as ctx:
        def sb(name, shape, dt):
            return ctx.enter_context(nc.sbuf_tensor(name, shape, dt))

        def ps(name, shape, dt):
            return ctx.enter_context(nc.psum_tensor(name, shape, dt))

        def sem(name):
            return ctx.enter_context(nc.semaphore(name))

        w = Stream(nc, sb, sem, a["stream"])
        s = shared_state(nc, sb, ps, sem)
        s.par = sb("params", [P, PAR1], F32)
        s.par1_all = sb("params1_all", [P, LAYERS, PAR1], F32)
        s.par2_all = sb("params2_all", [P, LAYERS, PAR], F32)
        s.bias_loaded, s.gain_loaded = sem("bias_loaded"), sem("gain_loaded")
        s.par2_loaded = sem("par2_loaded")
        s.order = sem("order")
        s.consts2_loaded, s.zeroed = sem("consts2_loaded"), sem("zeroed")
        inputs_loaded, s.consts_loaded = sem("inputs_loaded"), sem("consts_loaded")
        par_ready, stored = sem("par_ready"), sem("stored")
        mark1, mark2 = Marks(sem, "m1_", MIX1_TOTALS), Marks(sem, "m2_", MIX2_TOTALS)
        with ExitStack() as own:
            m1 = mix1_state(lambda name, shape, dt: own.enter_context(nc.sbuf_tensor(name, shape, dt)))
        with ExitStack() as own:
            m2 = mix2_state(lambda name, shape, dt: own.enter_context(nc.sbuf_tensor(name, shape, dt)), s)
        s.gfin = m1.u[:].rearrange("p i n -> p (i n)")
        loads = ((s.ident[:], a["ident"]), (s.par1_all[:], a["params1"]),
                 (s.x[:], a["x"].rearrange("(i p) d -> p i d", p=P)))
        later_loads = ((m1.dft_t[:], a["dft_t"]), (m1.dft_c[:], a["dft_c"]),
                       (s.par2_all[:], a["gains2"]))
        consts2 = ((m2.causal, "causal"), (m2.sbmask, "sbmask"), (m2.tri, "tri"),
                   (m2.cmask, "cmask"), (m2.hmask, "hmask"), (m2.rope, "rope"),
                   (m2.ropei, "ropei"), (m2.ropec, "ropec"))
        block = ctx.enter_context(nc.Block())

        @block.sync
        def _(sp):
            w.load(sp, 0, 0, 0)
            with sp.Fori(0, LAYERS) as layer:
                base = layer * SLOTS1
                w.load_slots(sp, base, FC)
                sp.wait_ge(s.x_ready, 12 * layer + 4)
                sp.dma_start(m1.bias[:], a["rel_bias"][layer]).then_inc(s.bias_loaded, 16)
                w.load_slots(sp, base + FC, MIX1_SLOTS + FC)
            sp.wait_ge(s.x_ready, 4 * 3 * LAYERS)
            sp.dma_start(s.gfin, a["final_gain"]).then_inc(s.gain_loaded, 16)
            w.load_slots(sp, SLOTS2_AT, FC)
            sp.wait_ge(s.x_ready, 4 * X2 + 4)
            for dest, name in consts2:
                sp.dma_start(dest[:], a[name]).then_inc(s.consts2_loaded, 16)
            sp.dma_start(m2.par[:], a["params2"][0]).then_inc(s.par2_loaded, 16)
            with sp.Fori(0, LAYERS - 1) as layer:
                w.load_slots(sp, layer * SLOTS2 + SLOTS2_AT + FC, SLOTS2)
                sp.wait_ge(s.x_ready, 12 * layer + 4 * X2 + 16)
                sp.dma_start(m2.par[:], a["params2"][layer + 1]).then_inc(s.par2_loaded, 16)
            w.load_slots(sp, LAYERS * SLOTS2 + SLOTS2_AT - MIX2_SLOTS - FC, MIX2_SLOTS + FC)
            sp.wait_ge(s.x_ready, 4 * (X2 + 3 * LAYERS) + 4)
            sp.dma_start(a["out"].rearrange("(i p) d -> p i d", p=P), s.x[:]).then_inc(stored, 16)
            sp.wait_ge(stored, 16)

        @block.gpsimd
        def _(pool):
            pool.sem_inc(w.split[0], 2)
            pool.sem_inc(w.split[1], 2)
            w.rest(nc.gpsimd, 0, 0, 0)
            for dest, src in later_loads:
                pool.dma_start(dest, src).then_inc(s.consts_loaded, 16)
            with pool.Fori(0, LAYERS) as layer:
                base = layer * SLOTS1
                w.split_slots(pool, base, FC, False)
                w.split_slots(pool, base + FC, MIX1_SLOTS, True)
                w.split_slots(pool, base + FC + MIX1_SLOTS, FC, False)
            w.split_slots(pool, SLOTS2_AT, FC, False)
            pool.wait_ge(s.x_ready, 4 * X2 + 4)
            for diagonals in (m2.kbd, m2.ikbd, m2.kcbd):
                last = nc.gpsimd.memset(diagonals[:], 0.0)
            last.then_inc(s.zeroed, 1)
            with pool.Fori(0, LAYERS - 1) as layer:
                base = layer * SLOTS2 + SLOTS2_AT
                w.split_slots(pool, base + FC, MIX2_SLOTS, True)
                w.split_slots(pool, base + FC + MIX2_SLOTS, 2 * FC, False)
            base = (LAYERS - 1) * SLOTS2 + SLOTS2_AT
            w.split_slots(pool, base + FC, MIX2_SLOTS, True)
            w.split_slots(pool, base + FC + MIX2_SLOTS, FC, False)

        @block.scalar
        def _(act):
            act.wait_ge(s.table_in, 1)
            nc.scalar.activation(s.scrap[:, 0:1], s.scrap[:, 1:2], ACT.Sqrt).then_inc(s.table_in, 1)
            for dest, src in loads:
                act.dma_start(dest, src).then_inc(inputs_loaded, 16)
            w.round_hi(act, 0, 0, 0)
            with act.Fori(0, LAYERS) as layer:
                base, n, c0 = layer * SLOTS1, 3 * layer, 2 * FC * layer
                ffn_scalar(s, w, base, 0, n, c0, 0)
                mix1_scalar(s, m1, mark1, w, base, FC, n + 1, layer)
                ffn_scalar(s, w, base, FC + MIX1_SLOTS, n + 2, c0 + FC, 2)
            final_norm_scalar(s, 3 * LAYERS)
            with act.Fori(0, LAYERS) as layer:
                base, n = layer * SLOTS2 + SLOTS2_AT, 3 * layer + X2
                c0 = 2 * FC * layer + 2 * FC * LAYERS
                ffn_scalar(s, w, base, 0, n, c0, 0)
                mix2_scalar(s, m2, mark2, w, base, FC, n + 1, layer)
                ffn_scalar(s, w, base, FC + MIX2_SLOTS, n + 2, c0 + FC, 2)

        @block.vector
        def _(dve):
            nc.vector.memset(s.scrap[:], 0.0).then_inc(s.table_in, 1)
            nc.vector.memset(m1.kbd[:], 0.0)
            dve.wait_ge(inputs_loaded, 16 * len(loads))
            dve.sem_inc(s.x_ready, 4)
            with dve.Fori(0, LAYERS) as layer:
                base, n, c0 = layer * SLOTS1, 3 * layer, 2 * FC * layer
                nc.vector.tensor_copy(s.par[:], s.par1_all[:, layer]).then_inc(par_ready, 1)
                dve.wait_ge(par_ready, layer + 1)
                norm_start(s, n)
                ffn_vector(s, w, base, 0, n, c0, 0, False)
                mix1_vector(s, m1, mark1, w, base, FC, n + 1, layer)
                ffn_vector(s, w, base, FC + MIX1_SLOTS, n + 2, c0 + FC, 2, True)
            final_norm_vector(s, 3 * LAYERS)
            dve.wait_ge(s.consts_loaded, 16 * CONSTS1)
            with dve.Fori(0, LAYERS) as layer:
                base, n = layer * SLOTS2 + SLOTS2_AT, 3 * layer + X2
                c0 = 2 * FC * layer + 2 * FC * LAYERS
                nc.vector.tensor_copy(s.par[:, 0:PAR], s.par2_all[:, layer]).then_inc(par_ready, 1)
                dve.wait_ge(par_ready, layer + LAYERS + 1)
                norm_start(s, n)
                ffn_vector(s, w, base, 0, n, c0, 0, False)
                mix2_vector(s, m2, mark2, w, base, FC, n + 1, layer)
                ffn_vector(s, w, base, FC + MIX2_SLOTS, n + 2, c0 + FC, 2, True)

        @block.tensor
        def _(pe):
            pe.sem_inc(w.used[0], 4)
            pe.sem_inc(w.used[1], 2)
            pe.wait_ge(inputs_loaded, 16 * len(loads))
            with pe.Fori(0, LAYERS) as layer:
                base, n, c0 = layer * SLOTS1, 3 * layer, 2 * FC * layer
                ffn_tensor(s, w, base, 0, n, c0)
                mix1_tensor(s, m1, mark1, w, base, FC, n + 1, layer)
                ffn_tensor(s, w, base, FC + MIX1_SLOTS, n + 2, c0 + FC)
            final_norm_tensor(s, 3 * LAYERS)
            with pe.Fori(0, LAYERS) as layer:
                base, n = layer * SLOTS2 + SLOTS2_AT, 3 * layer + X2
                c0 = 2 * FC * layer + 2 * FC * LAYERS
                ffn_tensor(s, w, base, 0, n, c0)
                mix2_tensor(s, m2, mark2, w, base, FC, n + 1, layer)
                ffn_tensor(s, w, base, FC + MIX2_SLOTS, n + 2, c0 + FC)
        mark1.check()
        mark2.check()



def columns(mat):
    rows, cols = mat.shape
    return [mat[:, c * P:(c + 1) * P].reshape(rows // P, P, P).transpose(1, 0, 2).reshape(P, rows)
            for c in range(cols // P)]


def wide(mat):
    return [mat[2 * j * P:(2 * j + 2) * P].reshape(2, P, HALF).transpose(1, 0, 2).reshape(P, CH)
            for j in range(KD // 2)]


def row_chunks(mat):
    return [mat[k * P:(k + 1) * P] for k in range(mat.shape[0] // P)]


def ffn_chunks(w_in, w_out):
    gate, up, down = columns(w_in[:, :DFF]), columns(w_in[:, DFF:]), row_chunks(w_out)
    return [x for three in zip(gate, up, down) for x in three]


def side_by_side(a, b):
    return [np.concatenate(two, axis=1) for two in zip(a, b)]


def mix1_chunks(w_in, na_out, f_out, w_o):
    q, k, v, u, ga, gf = np.split(w_in, [512, 1024, 1536, 2048, 3072], axis=1)
    gates = [x for two in zip(columns(ga), columns(gf)) for x in two]
    return (wide(v) + wide(u) + columns(q) + columns(k) + gates
            + side_by_side(columns(na_out), columns(f_out)) + row_chunks(w_o))


def per_partition(vec):
    return vec.reshape(KD, P).T


def relative_bias(rpb):
    t = np.arange(T)
    r, c = t // GRID_W, t % GRID_W
    start = np.clip(c - NA_COLS // 2, 0, GRID_W - NA_COLS)
    inside = (c[None, :] >= start[:, None]) & (c[None, :] < start[:, None] + NA_COLS)
    dr = r[None, :] - r[:, None] + NA_ROWS - 1
    dc = np.clip(c[None, :] - c[:, None], 1 - NA_COLS, NA_COLS - 1) + NA_COLS - 1
    out = np.where(inside[None], rpb[:, dr, dc], np.float32(MASKED))
    return out.reshape(NA_HEADS, TT, P, T).transpose(2, 1, 0, 3)


def dft_constants():
    t = np.arange(T)
    ang_t = 2 * np.pi * ((t[:, None] * t[None, :]) % T) / T
    time = np.concatenate([np.cos(ang_t), np.sin(ang_t)], axis=1).reshape(TT, P, 2 * T)
    c = np.arange(F_DIM)
    ang_c = 2 * np.pi * ((c[:, None] * c[None, :]) % F_DIM) / F_DIM
    chan = np.stack([np.cos(ang_c), -np.sin(ang_c)], axis=1) / np.sqrt(T * F_DIM)
    return time.transpose(1, 0, 2).astype(np.float32), chan.astype(np.float32)


def mix2_chunks(w_in, w_gate, w1, br_a, br_b, br_c, w_out):
    widths = (256, 256, 256, 512, 128, 128, 128, 128, 128, 128, 24, 256, 64, 64, 256, 32, 8)
    (sb_q, sb_k, sb_v, nq, nkc, nvc, nks, nvs, nkw, nvw, ngate, dq, dk, dv, iq, ik, iw) = np.split(
        w_in, np.cumsum(widths)[:-1], axis=1)

    def cat(*parts):
        return np.concatenate(parts, axis=1)

    rest = cat(dk, nvw)
    width = rest.shape[1]
    rest = rest.reshape(2, 4, P, width).transpose(0, 2, 1, 3).reshape(2, P, 4 * width)
    comp = w1.reshape(2, 2, 8, P, P).transpose(0, 1, 3, 2, 4).reshape(4, P, CH)
    gates = [columns(part) for part in np.split(w_gate, 3, axis=1)]
    gates = [gates[g % 3][g // 3] for g in range(3 * KD)]
    out = [np.concatenate(three, axis=1) for three in zip(columns(br_a), columns(br_b), columns(br_c))]
    return (columns(sb_q) + columns(sb_k) + wide(cat(sb_v, nkc, nvc))
            + wide(cat(iq, ik, iw, ngate, nvs, dv)) + wide(nq) + wide(cat(dq, nks, nkw))
            + list(rest) + gates[:4] + list(comp[:2]) + gates[4:5] + list(comp[2:])
            + gates[5:] + out + row_chunks(w_out))


def mixer_params(q_norm, k_norm, dsa_q, dsa_k, w2, pe):
    gains = np.concatenate([q_norm] * NSA_HEADS + [dsa_q] * DSA_HEADS + [k_norm[1]] * NSA_GROUPS
                           + [k_norm[2]] * NSA_GROUPS + [dsa_k, k_norm[0]])
    pos = pe.reshape(2, CMP_LEN // 2, P).transpose(2, 0, 1).reshape(P, CMP_LEN)
    return np.concatenate([np.tile(gains, (P, 1)), w2[0], w2[1], pos], axis=1)


def rope_table(pos, rot):
    inv = np.float32(500000.0) ** (-np.arange(0, rot, 2, dtype=np.float32) / np.float32(rot))
    ang = pos.astype(np.float32)[:, None] * inv[None, :]
    return np.stack([np.cos(ang), np.sin(ang)], axis=1)


def block2_constants():
    t, p = np.arange(T), np.arange(P)
    off = np.float32(MASKED)

    def tiles(x):
        return x.reshape((TT, P) + x.shape[1:]).swapaxes(0, 1)

    def mask(ok):
        return np.where(ok, np.float32(0), off)

    ends = np.arange(CB) * CMP_STRIDE + CMP_LEN - 1
    sb = mask(t[:, None] < t[None, :])
    return dict(
        causal=tiles(mask(t[None, :] <= t[:, None])),
        sbmask=np.concatenate([sb[:P], sb[P:, P:]], axis=1),
        tri=np.stack([-(p[:, None] >= p[None, :]).astype(np.float32), -np.ones((P, P))], axis=1),
        cmask=tiles(mask((ends[None, :] <= t[:, None]) & (np.arange(CB) < NCMP)[None, :])),
        hmask=(p[:, None] // CB == np.arange(NSA_HEADS)[None, :]),
        rope=tiles(rope_table(t, DH // 4)), ropei=tiles(rope_table(t, IDX_DIM // 4)),
        ropec=np.tile(rope_table(ends, DH // 4), (NSA_GROUPS, 1, 1)))


def kernel(**inputs):
    import concourse.bacc as bacc
    from concourse.bass_utils import run_bass_kernel_spmd

    x = {name: np.asarray(value) for name, value in inputs.items()}
    stream = np.zeros((LAYERS * (SLOTS1 + SLOTS2) + 1, P, SLOT), np.float32)
    chunks = []
    for l in range(LAYERS):
        chunks += ffn_chunks(x["ffn1_w_in"][l], x["ffn1_w_out"][l])
        chunks += mix1_chunks(x["mix_w_in"][l], x["na_w_out"][l], x["f_w_out"][l], x["mix_w_o"][l])
        chunks += ffn_chunks(x["ffn2_w_in"][l], x["ffn2_w_out"][l])
    for l in range(LAYERS):
        chunks += ffn_chunks(x["ffn1_w_gu_2"][l], x["ffn1_w_down_2"][l])
        chunks += mix2_chunks(x["w_in_2"][l], x["w_gate_2"][l], x["nsa_cmp_w1_2"][l],
                              x["w_br_a_2"][l], x["w_br_b_2"][l], x["w_br_c_2"][l], x["w_out_2"][l])
        chunks += ffn_chunks(x["ffn2_w_gu_2"][l], x["ffn2_w_down_2"][l])
    assert len(chunks) == 3 * LAYERS * (SLOTS1 + SLOTS2)
    for n, chunk in enumerate(chunks):
        stream[n // 3, :, n % 3 * CH:n % 3 * CH + chunk.shape[1]] = chunk
    dft_t, dft_c = dft_constants()
    arrays = dict(
        stream=stream, x=x["x"][0], ident=np.eye(P), dft_t=dft_t, dft_c=dft_c,
        params1=np.stack([np.concatenate(
            [per_partition(x[k][l]) for k in ("ffn1_norm", "mix_norm", "ffn2_norm")]
            + [per_partition(x["mix_gate_bias"][l, j]) for j in range(2)], axis=1)
            for l in range(LAYERS)], axis=1),
        gains2=np.stack([np.concatenate(
            [per_partition(x[k][l]) for k in ("ffn1_norm_2", "mix_norm_2", "ffn2_norm_2")], axis=1)
            for l in range(LAYERS)], axis=1),
        rel_bias=np.stack([relative_bias(x["na_rpb"][l]) for l in range(LAYERS)]),
        final_gain=np.tile(x["final_norm"], (P, 1)),
        params2=np.stack([mixer_params(
            x["nsa_q_norm_2"][l], x["nsa_k_norm_2"][l], x["dsa_q_norm_2"][l], x["dsa_k_norm_2"][l],
            x["nsa_cmp_w2_2"][l], x["nsa_cmp_pe_2"][l]) for l in range(LAYERS)]),
        **block2_constants())
    arrays = {"in_" + k: np.ascontiguousarray(v, dtype=np.float32) for k, v in arrays.items()}

    nc = bacc.Bacc("TRN2", target_bir_lowering=False, num_devices=1)
    aps = {k[3:]: nc.dram_tensor(k, v.shape, F32, kind="ExternalInput").ap()
           for k, v in arrays.items()}
    aps["out"] = nc.dram_tensor("out", (T, D), F32, kind="ExternalOutput").ap()
    build(nc, aps)
    results = run_bass_kernel_spmd(nc, [arrays], core_ids=[0])
    return results.results[0]["out"].reshape(x["x"].shape)
```
